# Optimizing a Trainium2 kernel written in Bass

```python
import math
import jax, jax.numpy as jnp
from jax import lax
import numpy as np

D_MODEL = 2048
BATCH = 1
SEQ = 256
DEPTH = 2

GRID_W = 64
CTX_LEN = 256
Q_BLOCK = 128
RET_CHUNK = 128
ROPE_THETA = 10000.0
EPS = 1e-6

A_WIDTH = D_MODEL // 2
A_HEADS = 8
A_HEAD_DIM = A_WIDTH // A_HEADS // 2
A_V_DIM = 2 * A_HEAD_DIM
A_QK_WIDTH = 2 * A_HEADS * A_HEAD_DIM
B_WIDTH = D_MODEL - A_WIDTH
B_HEADS = 4
B_V_DIM = B_WIDTH // B_HEADS
B_K_DIM = B_V_DIM // 2
B_QK_WIDTH = B_HEADS * B_K_DIM
EV_SIZES = (A_QK_WIDTH, A_QK_WIDTH, A_WIDTH, A_WIDTH, B_QK_WIDTH, B_QK_WIDTH, B_WIDTH, B_WIDTH)
EV_IN = sum(EV_SIZES)
EV_MIX = A_WIDTH + B_WIDTH

C_HEADS = 16
C_KV_HEADS = 4
C_GROUP = C_HEADS // C_KV_HEADS
C_HEAD_DIM = D_MODEL // C_HEADS
C_WIDTH = C_HEADS * C_HEAD_DIM
C_KV_WIDTH = C_KV_HEADS * C_HEAD_DIM
OD_SIZES = (C_WIDTH, C_KV_WIDTH, C_KV_WIDTH, C_WIDTH)
OD_IN = sum(OD_SIZES)

N_EVEN = (DEPTH + 1) // 2
N_ODD = DEPTH // 2

kernel_name = 'hybrid_diffattn_retention_gqa_dit'

def rms_norm(x, g):
    x32 = x.astype(jnp.float32)
    y = x32 * lax.rsqrt(jnp.mean(x32 * x32, axis=-1, keepdims=True) + EPS)
    return y.astype(x.dtype) * g

def group_norm(x, g):
    x32 = x.astype(jnp.float32)
    mu = jnp.mean(x32, axis=-1, keepdims=True)
    xc = x32 - mu
    y = xc * lax.rsqrt(jnp.mean(xc * xc, axis=-1, keepdims=True) + EPS)
    return y.astype(x.dtype) * g

def split_sizes(t, sizes):
    idx, acc = [], 0
    for s in sizes[:-1]:
        acc += s
        idx.append(acc)
    return jnp.split(t, idx, axis=-1)

def to_heads(t, n_heads):
    b, l, _ = t.shape
    return t.reshape(b, l, n_heads, -1).transpose(0, 2, 1, 3)

def merge_heads(t):
    b, h, l, d = t.shape
    return t.transpose(0, 2, 1, 3).reshape(b, l, h * d)

def grid_positions(n_lat):
    n_rows = n_lat // GRID_W
    rows = jnp.broadcast_to(jnp.arange(n_rows, dtype=jnp.int32)[:, None], (n_rows, GRID_W)).reshape(-1)
    cols = jnp.broadcast_to(jnp.arange(GRID_W, dtype=jnp.int32)[None, :], (n_rows, GRID_W)).reshape(-1)
    return rows, cols

def rope_tables(rows, cols, head_dim):
    axis_dim = head_dim // 2
    inv = ROPE_THETA ** (-jnp.arange(0, axis_dim, 2, dtype=jnp.float32) / axis_dim)
    ang_r = rows.astype(jnp.float32)[:, None] * inv
    ang_c = cols.astype(jnp.float32)[:, None] * inv
    return (jnp.cos(ang_r), jnp.sin(ang_r), jnp.cos(ang_c), jnp.sin(ang_c))

def _rotate(x, cos, sin):
    x1, x2 = jnp.split(x, 2, axis=-1)
    return jnp.concatenate([x1 * cos - x2 * sin, x1 * sin + x2 * cos], axis=-1)

def apply_rope_2d(x, tables):
    cr, sr, cc, sc = tables
    xr, xc = jnp.split(x, 2, axis=-1)
    return jnp.concatenate([_rotate(xr, cr, sr), _rotate(xc, cc, sc)], axis=-1).astype(x.dtype)

def _to_blocks(q):
    *lead, n, d = q.shape
    return jnp.moveaxis(q.reshape(*lead, n // Q_BLOCK, Q_BLOCK, d), -3, 0)

def _from_blocks(o):
    o = jnp.moveaxis(o, 0, -3)
    *lead, nb, qb, d = o.shape
    return o.reshape(*lead, nb * qb, d)

def diff_attn_core(q1, q2, k1, k2, v, lam):
    scale = A_HEAD_DIM ** -0.5
    s1 = jnp.einsum('bhqd,bhkd->bhqk', q1, k1) * scale
    s2 = jnp.einsum('bhqd,bhkd->bhqk', q2, k2) * scale
    p = jax.nn.softmax(s1.astype(jnp.float32), axis=-1) - lam * jax.nn.softmax(s2.astype(jnp.float32), axis=-1)
    return jnp.einsum('bhqk,bhke->bhqe', p.astype(v.dtype), v)

def gqa_core(q, k, v):
    s = jnp.einsum('bhgqd,bhkd->bhgqk', q, k) * (C_HEAD_DIM ** -0.5)
    p = jax.nn.softmax(s.astype(jnp.float32), axis=-1).astype(v.dtype)
    return jnp.einsum('bhgqk,bhkd->bhgqd', p, v)

def retention_chunkwise(q, k, v, log_g, s0):
    b, h, l, dk = q.shape
    dv = v.shape[-1]
    nc = l // RET_CHUNK
    dt = q.dtype
    qc = q.reshape(b, h, nc, RET_CHUNK, dk)
    kc = k.reshape(b, h, nc, RET_CHUNK, dk)
    vc = v.reshape(b, h, nc, RET_CHUNK, dv)
    pos = jnp.arange(RET_CHUNK, dtype=jnp.float32)
    lg = log_g.astype(jnp.float32)[:, None]
    rel = pos[:, None] - pos[None, :]
    decay = jnp.where(rel >= 0, jnp.exp(lg[:, :, None] * jnp.maximum(rel, 0.0)), 0.0)
    q_decay = jnp.exp(lg * (pos + 1.0))
    k_decay = jnp.exp(lg * (RET_CHUNK - 1.0 - pos))
    chunk_decay = jnp.exp(lg[:, 0] * RET_CHUNK).astype(dt)
    scores = jnp.einsum('bhnid,bhnjd->bhnij', qc, kc) * decay[None, :, None].astype(dt)
    intra = jnp.einsum('bhnij,bhnje->bhnie', scores, vc)
    upd = jnp.einsum('bhnjd,bhnje->nbhde', kc * k_decay[None, :, None, :, None].astype(dt), vc)

    def step(s, u):
        return s * chunk_decay[None, :, None, None] + u, s

    s_final, s_prev = lax.scan(step, s0, upd)
    cross = jnp.einsum('bhnid,nbhde->bhnie', qc * q_decay[None, :, None, :, None].astype(dt), s_prev)
    return (intra + cross).reshape(b, h, l, dv), s_final

def bi_retention(q_c, k_c, v_c, q_l, k_l, v_l, log_g_fwd, log_g_bwd):
    flip = lambda t: jnp.flip(t, axis=2)
    b, h, _, dk = q_c.shape
    s0 = jnp.zeros((b, h, dk, v_c.shape[-1]), q_c.dtype)
    o_cf, s_cf = retention_chunkwise(q_c, k_c, v_c, log_g_fwd, s0)
    o_cb, s_cb = retention_chunkwise(flip(q_c), flip(k_c), flip(v_c), log_g_bwd, s0)
    o_lf, _ = retention_chunkwise(q_l, k_l, v_l, log_g_fwd, s_cf)
    o_lb, _ = retention_chunkwise(flip(q_l), flip(k_l), flip(v_l), log_g_bwd, s_cb)
    return o_lf + flip(o_lb), o_cf + flip(o_cb)

def even_mixer(h_lat, h_ctx, w_in, w_out, lam_p, subln_g, ret_log_a, ret_g, rope_a, layer_idx, need_ctx):
    lambda_init = 0.8 - 0.6 * math.exp(-0.3 * layer_idx)
    lp = lam_p.astype(jnp.float32)
    lam = jnp.exp(jnp.sum(lp[0] * lp[1])) - jnp.exp(jnp.sum(lp[2] * lp[3])) + lambda_init
    log_g = -jnp.exp(ret_log_a.astype(jnp.float32))

    def project(h, rope):
        aq, ak, av, ag, bq, bk, bv, bg = split_sizes(h @ w_in, EV_SIZES)
        aq = to_heads(aq, 2 * A_HEADS)
        ak = to_heads(ak, 2 * A_HEADS)
        if rope is not None:
            aq = apply_rope_2d(aq, rope)
            ak = apply_rope_2d(ak, rope)
        b, _, l, _ = aq.shape
        aq = aq.reshape(b, A_HEADS, 2, l, A_HEAD_DIM)
        ak = ak.reshape(b, A_HEADS, 2, l, A_HEAD_DIM)
        return (aq[:, :, 0], aq[:, :, 1], ak[:, :, 0], ak[:, :, 1], to_heads(av, A_HEADS), ag,
                to_heads(bq, B_HEADS), to_heads(bk, B_HEADS) * (B_K_DIM ** -0.5), to_heads(bv, B_HEADS), bg)

    def finish(o_a, a_gate, o_b, b_gate):
        ya = merge_heads(rms_norm(o_a, subln_g) * (1.0 - lambda_init)) * jax.nn.silu(a_gate)
        yb = merge_heads(group_norm(o_b, ret_g[None, :, None, :])) * jax.nn.silu(b_gate)
        return jnp.concatenate([ya, yb], axis=-1) @ w_out

    lat = project(h_lat, rope_a)
    cx = project(h_ctx, None)
    k1_all = jnp.concatenate([cx[2], lat[2]], axis=2)
    k2_all = jnp.concatenate([cx[3], lat[3]], axis=2)
    v_all = jnp.concatenate([cx[4], lat[4]], axis=2)
    o_a_lat = _from_blocks(lax.map(lambda qs: diff_attn_core(qs[0], qs[1], k1_all, k2_all, v_all, lam),
                                   (_to_blocks(lat[0]), _to_blocks(lat[1]))))
    o_b_lat, o_b_ctx = bi_retention(cx[6], cx[7], cx[8], lat[6], lat[7], lat[8], log_g[0], log_g[1])
    y_lat = finish(o_a_lat, lat[5], o_b_lat, lat[9])
    y_ctx = None
    if need_ctx:
        o_a_ctx = diff_attn_core(cx[0], cx[1], cx[2], cx[3], cx[4], lam)
        y_ctx = finish(o_a_ctx, cx[5], o_b_ctx, cx[9])
    return y_lat, y_ctx

def odd_mixer(h_lat, h_ctx, w_in, w_out, qk_g, rope_c, need_ctx):
    def project(h, rope):
        q, k, v, g = split_sizes(h @ w_in, OD_SIZES)
        q = rms_norm(to_heads(q, C_HEADS), qk_g[0])
        k = rms_norm(to_heads(k, C_KV_HEADS), qk_g[1])
        if rope is not None:
            q = apply_rope_2d(q, rope)
            k = apply_rope_2d(k, rope)
        b, _, l, _ = q.shape
        return q.reshape(b, C_KV_HEADS, C_GROUP, l, C_HEAD_DIM), k, to_heads(v, C_KV_HEADS), g

    def finish(o, g):
        b, hk, gr, l, d = o.shape
        return (merge_heads(o.reshape(b, hk * gr, l, d)) * jax.nn.silu(g)) @ w_out

    ql, kl, vl, gl = project(h_lat, rope_c)
    qc, kc, vc, gc = project(h_ctx, None)
    k_all = jnp.concatenate([kc, kl], axis=2)
    v_all = jnp.concatenate([vc, vl], axis=2)
    o_lat = _from_blocks(lax.map(lambda qb: gqa_core(qb, k_all, v_all), _to_blocks(ql)))
    y_lat = finish(o_lat, gl)
    y_ctx = finish(gqa_core(qc, kc, vc), gc) if need_ctx else None
    return y_lat, y_ctx

def setup_inputs(seed: int = 0) -> dict:
    key = jax.random.key(seed)
    ks = jax.random.split(key, 20)
    f32 = jnp.float32
    nrm = lambda k, shape, s: jax.random.normal(k, shape, f32) * s
    heads = jnp.arange(B_HEADS, dtype=f32)
    base_decay = jnp.log(-jnp.log1p(-(2.0 ** (-5.0 - heads))))
    return {
        'x': nrm(ks[0], (BATCH, SEQ, D_MODEL), 1.0),
        'c': nrm(ks[1], (BATCH, D_MODEL), 1.0),
        'ctx': nrm(ks[2], (BATCH, CTX_LEN, D_MODEL), 1.0),
        'c_ctx': nrm(ks[3], (D_MODEL,), 1.0),
        'norm_g': 1.0 + nrm(ks[4], (DEPTH, D_MODEL), 0.02),
        'w_mod': nrm(ks[5], (DEPTH, D_MODEL, 3 * D_MODEL), D_MODEL ** -0.5),
        'b_mod': nrm(ks[6], (DEPTH, 3 * D_MODEL), 0.02),
        'ev_w_in': nrm(ks[7], (N_EVEN, D_MODEL, EV_IN), D_MODEL ** -0.5),
        'ev_w_out': nrm(ks[8], (N_EVEN, EV_MIX, D_MODEL), EV_MIX ** -0.5),
        'diff_lambda': nrm(ks[9], (N_EVEN, 4, A_HEAD_DIM), 0.1),
        'diff_subln': 1.0 + nrm(ks[10], (N_EVEN, A_V_DIM), 0.02),
        'ret_decay': base_decay + nrm(ks[11], (N_EVEN, 2, B_HEADS), 0.05),
        'ret_gn': 1.0 + nrm(ks[12], (N_EVEN, B_HEADS, B_V_DIM), 0.02),
        'od_w_in': nrm(ks[13], (N_ODD, D_MODEL, OD_IN), D_MODEL ** -0.5),
        'od_w_out': nrm(ks[14], (N_ODD, C_WIDTH, D_MODEL), C_WIDTH ** -0.5),
        'qk_norm': 1.0 + nrm(ks[15], (N_ODD, 2, C_HEAD_DIM), 0.02),
        'final_norm': 1.0 + nrm(ks[16], (D_MODEL,), 0.02),
    }

def reference(x, c, ctx, c_ctx, norm_g, w_mod, b_mod, ev_w_in, ev_w_out, diff_lambda, diff_subln,
              ret_decay, ret_gn, od_w_in, od_w_out, qk_norm, final_norm):
    n_lat = x.shape[1]
    rows, cols = grid_positions(n_lat)
    rope_a = rope_tables(rows, cols, A_HEAD_DIM)
    rope_c = rope_tables(rows, cols, C_HEAD_DIM)
    s_lat = jax.nn.silu(c)
    s_ctx = jax.nn.silu(c_ctx)
    for i in range(DEPTH):
        shift, scale, gate = jnp.split(s_lat @ w_mod[i] + b_mod[i], 3, axis=-1)
        shift_c, scale_c, gate_c = jnp.split(s_ctx @ w_mod[i] + b_mod[i], 3, axis=-1)
        h_lat = rms_norm(x, norm_g[i]) * (1 + scale[:, None]) + shift[:, None]
        h_ctx = rms_norm(ctx, norm_g[i]) * (1 + scale_c) + shift_c
        need_ctx = i < DEPTH - 1
        if i % 2 == 0:
            e = i // 2
            y_lat, y_ctx = even_mixer(h_lat, h_ctx, ev_w_in[e], ev_w_out[e], diff_lambda[e], diff_subln[e],
                                      ret_decay[e], ret_gn[e], rope_a, i, need_ctx)
        else:
            o = i // 2
            y_lat, y_ctx = odd_mixer(h_lat, h_ctx, od_w_in[o], od_w_out[o], qk_norm[o], rope_c, need_ctx)
        x = x + gate[:, None] * y_lat
        if need_ctx:
            ctx = ctx + gate_c * y_ctx
    return rms_norm(x, final_norm)


_drawn_inputs = setup_inputs


def setup_inputs(seed=0):
    import zlib

    import numpy as np

    out = dict(_drawn_inputs(seed))
    spreads = {}
    factors = {'norm_g': 3.996,
     'diff_lambda': 8.0,
     'diff_subln': 8.0,
     'ret_gn': 8.0,
     'qk_norm': 8.0,
     'final_norm': 2.895}
    for name, (base, spread) in spreads.items():
        noise = np.random.default_rng([zlib.crc32(name.encode()), seed]).standard_normal(out[name].shape)
        drawn = base * np.exp(spread * noise) if base else spread * noise
        out[name] = __import__('jax').numpy.asarray(drawn.astype(out[name].dtype))
    for name, factor in factors.items():
        out[name] = (out[name] * factor).astype(out[name].dtype)
    return out
```

```python
import math
from contextlib import ExitStack

import numpy as np

import concourse.bass as bass
from concourse import mybir

F32 = mybir.dt.float32
F32R = mybir.dt.float32r
ALU = mybir.AluOpType
ACT = mybir.ActivationFunctionType
AX_X = mybir.AxisListType.X

P = 128
D_MODEL = 2048
SEQ = 256
CTX = 256
T = SEQ + CTX
GRID_W = 64
ROPE_THETA = 10000.0
EPS = 1e-6
KT = D_MODEL // P
NCH = KT // 2
CH = 2 * 512
A_HEADS, A_DIM = 8, 64
B_HEADS, B_DIM = 4, 128
C_HEADS, C_KV, C_DIM = 16, 4, 128
C_GROUP = C_HEADS // C_KV
LAMBDA_INIT = 0.8 - 0.6 * math.exp(-0.3 * 0)
WSLOTS, MSLOTS = 4, 2
AHEAD = 3

MOD0_GROUPS = 8
PAIRS = 4
N_A = NCH * MOD0_GROUPS
N_B = N_A + NCH * A_HEADS
N_O0 = N_B + 2 * NCH * B_HEADS
N_C = N_O0 + NCH * 4
N_O1 = N_C + 3 * NCH * C_KV
N_END = N_O1 + NCH * 4
EARLY = 12

S_C, S_G, S_B, S_SUBLN, S_DECAY, S_GN, S_QK, S_FN, S_DL = 0, 32, 64, 160, 161, 169, 177, 179, 195
S_SEL = 199
S_END = 201
(R_S, R_LG, R_LAM, R_EXP2, R_PROD, R_NEG, R_SUM, R_REC, R_C2, R_SUB, R_EPS, R_ZERO) = (
    0, 32, 40, 41, 43, 45, 47, 49, 51, 52, 53, 54)
R_END = 55
M_SCALE0, M_SHIFT0, M_GATE0, M_SCALE1, M_SHIFT1, M_GATE1 = (16 * i for i in range(6))


def prologue():
    n = 0
    for pair in range(PAIRS):
        for g in (2 * pair, 2 * pair + 1):
            yield "mod", g, n
            n += NCH
        if pair > 0:
            yield "head", 4 * (pair - 1), n
            n += 2
    yield "head", 4 * (PAIRS - 1), n


def out_blocks():
    for i in range(8):
        first = i < 4
        yield (i, i % 4, range(EARLY) if first else range(EARLY, KT),
               EARLY // 2 * i if first else 4 * (EARLY // 2) + (KT - EARLY) // 2 * (i - 4))


def bass_hybrid_backbone(nc, x_t, w_mod, w_all, small_in, mats_in, trig_in,
                         dist_in, out):
    ctx = ExitStack()
    with ctx:
        def sb(name, shape, dt=F32):
            return ctx.enter_context(nc.sbuf_tensor(name, shape, dt))

        def sem(name):
            return ctx.enter_context(nc.semaphore(name))

        w_raw = sb("w_raw", [P, WSLOTS, CH])
        w_hi = sb("w_hi", [P, WSLOTS, CH], F32R)
        w_lo = sb("w_lo", [P, WSLOTS, CH], F32R)
        m_raw = sb("m_raw", [P, MSLOTS, CH])
        m_acc = sb("m_acc", [P, 2, 512])
        act_hi = sb("act_hi", [P, KT, T], F32R)
        act_lo = sb("act_lo", [P, KT, T], F32R)
        stream = sb("stream", [P, KT, T])
        mats = sb("mats", [P, 4, P])
        trig = sb("trig", [P, 2, SEQ])
        aux = sb("aux", [P, 5, 512])
        qk = sb("qk", [P, 2, T])
        kv = sb("kv", [P, 2, T])
        v_tok = sb("v_tok", [P, 4, 256])
        pt = sb("pt", [P, 2, 4, 256])
        prob = sb("prob", [P, 3, 512])
        tmp_o = sb("tmp_o", [P, 2, 512])
        tmp_r = sb("tmp_r", [P, 2, 512])
        small = sb("small", [P, S_END])
        stat = sb("stat", [P, R_END])
        modv = sb("modv", [P, 2, 96])
        s_parts = sb("s_parts", [P, 4 * KT + P], F32R)

        pj = ctx.enter_context(nc.psum_tensor("pj", [P, 4, 512], F32))
        sa = ctx.enter_context(nc.psum_tensor("sa", [P, 512], F32))
        sc = ctx.enter_context(nc.psum_tensor("sc", [P, 512], F32))
        tr = ctx.enter_context(nc.psum_tensor("tr", [P, 512], F32))
        ov = ctx.enter_context(nc.psum_tensor("ov", [P, 512], F32))

        rot_a, rot_c, ones, ident = (mats[:, i, :] for i in range(4))

        def st(c, n=1):
            return stat[:, c:c + n]

        def sm(c, n=1):
            return small[:, c:c + n]

        consts_loaded, dist_loaded = sem("consts_loaded"), sem("dist_loaded")
        x_loaded = [sem(f"x_loaded{i}") for i in range(4)]
        w_loaded = [sem(f"w_loaded{i}") for i in range(WSLOTS)]
        m_loaded = [sem(f"m_loaded{i}") for i in range(MSLOTS)]
        xr_loaded = sem("xr_loaded")
        trig_loaded = sem("trig_loaded")
        out_stored = sem("out_stored")
        w_hi_done, w_lo_done, w_used = sem("w_hi_done"), sem("w_lo_done"), sem("w_used")
        row_copied, row_spread, mod0_read = sem("row_copied"), sem("row_spread"), sem("mod0_read")
        m_lat, m_ctx, m_sum, m_out = sem("m_lat"), sem("m_ctx"), sem("m_sum"), sem("m_out")
        setup_v, setup_a, setup_p = sem("setup_v"), sem("setup_a"), sem("setup_p")
        s_whole, s_ready, zeroed = sem("s_whole"), sem("s_ready"), sem("zeroed")
        ss_sq, ss_add, ss_sum, ss_root, ss_inv = (sem("ss_sq"), sem("ss_add"), sem("ss_sum"), sem("ss_root"),
                                                  sem("ss_inv"))
        h_norm, h_lat, h_ctx = sem("h_norm"), sem("h_lat"), sem("h_ctx")
        act_hi_done, act_lo_done = sem("act_hi_done"), sem("act_lo_done")
        scale_ready = sem("scale_ready")
        proj_done = [sem(f"proj_done{i}") for i in range(4)]
        bank_free = [sem(f"bank_free{i}") for i in range(4)]
        x1_lat = sem("x1_lat")
        out_ready = sem("out_ready")
        a_rot, a_vt, a_vtok, a_tmp, a_cos, a_rope = (sem("a_rot"), sem("a_vt"), sem("a_vtok"), sem("a_tmp"),
                                                     sem("a_cos"), sem("a_rope"))
        a_s, a_max, a_exp, a_rec, a_c2, a_p2, a_p = (sem("a_s"), sem("a_max"), sem("a_exp"), sem("a_rec"),
                                                     sem("a_c2"), sem("a_p2"), sem("a_p"))
        a_t, a_pt, a_o, a_sq, a_ss, a_root, a_inv, a_y, a_out = (
            sem("a_t"), sem("a_pt"), sem("a_o"), sem("a_sq"), sem("a_ss"), sem("a_root"), sem("a_inv"), sem("a_y"),
            sem("a_out"))
        b_vt, b_vtok, b_argb, b_arg, b_expi, b_expc, b_di, b_dc = (
            sem("b_vt"), sem("b_vtok"), sem("b_argb"), sem("b_arg"), sem("b_expi"), sem("b_expc"), sem("b_di"),
            sem("b_dc"))
        b_s, b_pt, b_o, b_ocopy, b_mean, b_xc, b_sq, b_var, b_root, b_inv, b_y, b_out = (
            sem("b_s"), sem("b_pt"), sem("b_o"), sem("b_ocopy"), sem("b_mean"), sem("b_xc"), sem("b_sq"),
            sem("b_var"), sem("b_root"), sem("b_inv"), sem("b_y"), sem("b_out"))
        cq_sq, cq_ss, cq_root, cq_inv, cq_n, cq_rot, cq_sin, cq_cos, cq_rope = (
            sem("cq_sq"), sem("cq_ss"), sem("cq_root"), sem("cq_inv"), sem("cq_n"), sem("cq_rot"), sem("cq_sin"),
            sem("cq_cos"), sem("cq_rope"))
        ck_sq, ck_ss, ck_root, ck_inv, ck_n, ck_rot, ck_sin, ck_cos, ck_rope = (
            sem("ck_sq"), sem("ck_ss"), sem("ck_root"), sem("ck_inv"), sem("ck_n"), sem("ck_rot"), sem("ck_sin"),
            sem("ck_cos"), sem("ck_rope"))
        c_vt, c_vtok, c_s, c_max, c_exp, c_rec, c_p, c_t, c_pt, c_o, c_out = (
            sem("c_vt"), sem("c_vtok"), sem("c_s"), sem("c_max"), sem("c_exp"), sem("c_rec"), sem("c_p"),
            sem("c_t"), sem("c_pt"), sem("c_o"), sem("c_out"))

        block = ctx.enter_context(nc.Block())

        def past(eng, s, value):
            if not isinstance(value, int) or value > 0:
                eng.wait_ge(s, value)

        def evacs_a(h, t):
            return h

        def evacs_b(b, blk, t):
            return 8 + 2 * b + blk if t < 3 else 8

        def evacs_o0(i, t):
            return 16 + i if t < 3 else 8 + i

        def evacs_c(j, blk, t):
            return 24 + 3 * j + blk if t < 2 else (24 if t == 2 else 16) + 2 * j + blk

        def evacs_o1(i, t):
            return 36 + i if t < 2 else (32 if t == 2 else 24) + i

        def done_c(j, blk, t):
            return {0: 24 + 3 * j + blk, 1: 24 + 2 * j + blk, 2: 16 + 2 * j + blk}[t]

        def done_out(layer, i, t):
            return ((16, 16, 8), (36, 32, 24))[layer][t] + i

        @block.sync
        def _(sp):
            sp.dma_start(small[:, :], small_in).then_inc(consts_loaded, 16)
            sp.dma_start(mats[:, :, :], mats_in).then_inc(consts_loaded, 16)

            def load_w(n, c, width=CH):
                if isinstance(n, int) and n >= N_END:
                    return
                past(sp, w_lo_done, n - WSLOTS + 1)
                sp.dma_start(w_raw[:, c % WSLOTS, 0:width], w_all[n, :, 0:width]).then_inc(w_loaded[c % WSLOTS], 16)

            def load_m(it, c):
                ops = 2 * NCH * it + 2 * (c - 1)
                past(sp, m_lat, ops)
                past(sp, m_ctx, ops)
                sp.dma_start(m_raw[:, c % MSLOTS, :], w_mod[NCH * it + c]) \
                    .then_inc(m_loaded[c % MSLOTS], 16)

            def load_m_lat(it, c):
                sp.wait_ge(m_lat, 2 * NCH * it + 2 * (c - 1))
                if isinstance(it, int) and c < MSLOTS:
                    sp.wait_ge(m_ctx, 2 * NCH * it + 2 * (c - 1))
                sp.dma_start(m_raw[:, c % MSLOTS, :], w_mod[NCH * it + c]) \
                    .then_inc(m_loaded[c % MSLOTS], 16)

            for n in range(WSLOTS):
                load_w(n, n)
            sp.dma_start(trig[:, :, :], trig_in[0]).then_inc(trig_loaded, 16)
            sp.dma_start(aux[:, :, :], dist_in).then_inc(dist_loaded, 16)
            with sp.Fori(1, (N_A + NCH) // WSLOTS) as i:
                for c in range(WSLOTS):
                    load_w(WSLOTS * i + c, c)
            for c in range(AHEAD):
                load_w(N_A + NCH + c, c)

            def body_a(h):
                for c in range(NCH):
                    load_w(N_A + NCH * h + c + AHEAD, c + AHEAD)
                    load_m(h - 1, c)

            def body_b(b):
                for c in range(2 * NCH):
                    load_w(N_B + 2 * NCH * b + c + AHEAD, c + AHEAD, 768 if c + AHEAD < 2 * NCH else CH)
                    if c % 2 == 0:
                        load_m(7 + b, c // 2)

            body_a(1)
            with sp.Fori(2, A_HEADS) as h:
                body_a(h)
            body_b(0)
            with sp.Fori(1, B_HEADS) as b:
                body_b(b)
            for i, fb, kts, n0 in out_blocks():
                for c in range(len(kts) // 2):
                    load_w(N_O0 + n0 + c + AHEAD, n0 + c + AHEAD)
                    if i < 4 and n0 + c < 2 * NCH and (n0 + c) % 2 == 0:
                        load_m(11, (n0 + c) // 2)
                if i < 4:
                    if i == 0:
                        sp.wait_ge(b_dc, B_HEADS)
                        sp.wait_ge(b_di, B_HEADS)
                    else:
                        sp.wait_ge(bank_free[3], evacs_o0(i, 3))
                    sp.dma_start(aux[:, 0:4, :], x_t[4 * fb:4 * fb + 4].rearrange("k p t -> p k t")) \
                        .then_inc(xr_loaded, 16)
            sp.wait_ge(a_rope, A_HEADS)
            sp.dma_start(trig[:, :, :], trig_in[1]).then_inc(trig_loaded, 16)

            def body_c(j):
                for c in range(3 * NCH):
                    load_w(N_C + 3 * NCH * j + c + AHEAD, c + AHEAD,
                           CH // 2 if 2 * NCH <= c + AHEAD < 3 * NCH else CH)
                    if c % 3 == 0:
                        load_m_lat(12 + j, c // 3)

            body_c(0)
            with sp.Fori(1, C_KV) as j:
                body_c(j)
            with sp.Fori(0, 7) as i:
                for c in range(AHEAD, WSLOTS + AHEAD):
                    load_w(N_O1 + WSLOTS * i + c, c)
            load_w(N_END - 1, 3)
            for q in range(4):
                sp.wait_ge(out_ready, 4 * (q + 1))
                sp.dma_start(out[4 * q:4 * q + 4].rearrange("k p t -> p k t"), stream[:, 4 * q:4 * q + 4, 0:SEQ]) \
                    .then_inc(out_stored, 16)
            sp.wait_ge(out_stored, 64)

        @block.tensor
        def _(pe):
            mm, tp = pe.matmul, pe.transpose

            pe.wait_ge(setup_v, 1)
            pe.wait_ge(consts_loaded, 32)
            mm(sc[:, 0:2], ones[0:64, :], stat[0:64, R_PROD:R_PROD + 2], start=True, stop=True).then_inc(setup_p, 1)
            def mod_rows(g, c, n0):
                if c == 0:
                    if g == 0:
                        pe.wait_ge(s_ready, 2 * KT)
                    past(pe, row_copied, g - 1)
                pe.wait_ge(w_lo_done, n0 + c + 1)
                slot = (n0 + c) % WSLOTS
                for k2 in range(2):
                    k = 2 * c + k2
                    for part in (w_hi, w_lo):
                        last = mm((tr, sa)[g % 2][:, :], s_parts[:, 4 * k:4 * k + P],
                                  part[:, slot, 512 * k2:512 * k2 + 512], start=(k == 0 and part is w_hi),
                                  stop=(k == KT - 1 and part is w_lo))
                last.then_inc(w_used, 1)

            def spread_rows(g):
                pe.wait_ge(row_copied, g + 1)
                past(pe, mod0_read, g)
                for f in range(4):
                    last = mm(ov[:, 2 * f:2 * f + 2], m_acc[0:4, g % 2, P * f:P * f + P], small[0:4, S_SEL:S_SEL + 2],
                              start=True, stop=True)
                last.then_inc(row_spread, 1)

            def project(n0, kt, ntiles, ncols, free_count, act_base=None, kts=range(KT), slot0=0):
                c, k2 = (kt - kts[0]) // 2, kt % 2
                slot, width = (slot0 + c) % WSLOTS, P * ntiles
                if k2 == 0:
                    pe.wait_ge(w_lo_done, n0 + c + 1)
                if act_base is not None:
                    pe.wait_ge(act_lo_done, act_base + kt + 1)
                for t in range(ntiles):
                    if kt == kts[0]:
                        past(pe, bank_free[t], free_count(t))
                    cols = slice(k2 * width + P * t, k2 * width + P * t + P)
                    acc = pj[:, t, 0:ncols]
                    wh, wl = w_hi[:, slot, cols], w_lo[:, slot, cols]
                    mm(acc, wh, act_hi[:, kt, 0:ncols], start=(kt == kts[0]), stop=False)
                    mm(acc, wh, act_lo[:, kt, 0:ncols], start=False, stop=False)
                    last = mm(acc, wl, act_hi[:, kt, 0:ncols], start=False, stop=(kt == kts[-1]))
                    if kt == kts[-1] and t < ntiles - 1:
                        last.then_inc(proj_done[t], 1)
                if k2 == 1:
                    last.then_inc(w_used, 1)

            def sum_mod(it):
                pe.wait_ge(m_lat, 2 * NCH * (it + 1))
                pe.wait_ge(m_ctx, 2 * NCH * (it + 1))
                for v in range(2):
                    for f in range(4):
                        last = mm(sa[:, 4 * v + f:4 * v + f + 1], m_acc[:, v, P * f:P * f + P], ones[:, 0:1],
                                  start=True, stop=True)
                last.then_inc(m_sum, 1)

            def sum_mod_lat(it):
                pe.wait_ge(m_lat, 2 * NCH * (it + 1))
                for f in range(4):
                    last = mm(sa[:, f:f + 1], m_acc[:, 0, P * f:P * f + P], ones[:, 0:1], start=True, stop=True)
                last.then_inc(m_sum, 1)

            def attend_a(a, s):
                if s == 0:
                    if isinstance(a, int) and a == 0:
                        pe.wait_ge(row_copied, MOD0_GROUPS)
                        pe.wait_ge(mod0_read, MOD0_GROUPS)
                        pe.wait_ge(ss_root, 1)
                    else:
                        pe.wait_ge(a_exp, 8 * a)
                        sum_mod(a - 1)
                    pe.wait_ge(bank_free[0], a + 1)
                    pe.wait_ge(bank_free[1], a + 1)
                    pe.wait_ge(bank_free[2], a + 1)
                    past(pe, a_root, a)
                    past(pe, a_y, a)
                    for i in range(2):
                        last = mm(tr[:, 256 * i:256 * i + 256], rot_a, qk[:, i, 0:SEQ], start=True, stop=True)
                    last.then_inc(a_rot, 1)
                    for i in range(4):
                        last = tp(ov[:, P * i:P * i + P], kv[:, 0, P * i:P * i + P], ident)
                    last.then_inc(a_vt, 1)
                if s in (2, 4, 6, 8) and s >= 6:
                    transposes_a(a, (s - 6) // 2)
                if s in (2, 4, 6, 8):
                    q = (s - 2) // 2
                    if q == 0:
                        pe.wait_ge(a_rope, a + 1)
                        past(pe, m_out, a)
                    else:
                        pe.wait_ge(a_exp, 8 * a + 2 * q)
                    keys = slice(0, T) if q < 2 else slice(SEQ, T)
                    nk = T if q < 2 else CTX
                    for m, bank in enumerate((sa, sc)):
                        rows = slice(64 * m, 64 * m + 64)
                        mm(bank[:, 0:nk], qk[rows, 0, P * q:P * q + P], qk[rows, 1, keys], start=True, stop=True) \
                            .then_inc(a_s, 1)
                if s == 10:
                    transposes_a(a, 2)
                    pe.wait_ge(a_vtok, a + 1)
                    pe.wait_ge(a_pt, 4 * a + 2)
                    for i in range(4):
                        last = mm(ov[:, 0:SEQ], v_tok[:, i, 0:P], pt[:, 0, i, :], start=(i == 0), stop=(i == 3))
                    last.then_inc(a_o, 1)
                if s == 12:
                    transposes_a(a, 3)
                if s == 13:
                    pe.wait_ge(a_pt, 4 * a + 4)
                    for i in range(2):
                        last = mm(ov[:, SEQ:T], v_tok[:, 2 + i, 0:P], pt[:, 1, i, :], start=(i == 0), stop=(i == 1))
                    last.then_inc(a_o, 1)
                if s == 14:
                    pe.wait_ge(a_sq, a + 1)
                    mm(tr[:, :], ones, tmp_r[:, 0, :], start=True, stop=True).then_inc(a_ss, 1)

            def transposes_a(a, q):
                pe.wait_ge(a_p, 4 * a + q + 1)
                past(pe, a_pt, 4 * a + q)
                for i in range(4 if q < 2 else 2):
                    last = tp(tr[:, P * i:P * i + P], prob[:, 2, P * i:P * i + P], ident)
                last.then_inc(a_t, 1)

            def retain_b(b, s):
                if s == 0:
                    if isinstance(b, int) and b == 0:
                        pe.wait_ge(a_exp, 8 * A_HEADS)
                    past(pe, b_xc, 2 * b)
                    sum_mod(7 + b)
                    pe.wait_ge(bank_free[0], 8 + 2 * b + 2)
                    pe.wait_ge(bank_free[1], 8 + 2 * b + 1)
                    pe.wait_ge(bank_free[2], 8 + 2 * b + 1)
                    if isinstance(b, int) and b == 0:
                        pe.wait_ge(a_root, A_HEADS)
                        pe.wait_ge(a_y, A_HEADS)
                    past(pe, b_ocopy, 2 * b)
                    for e, bank in enumerate((tr, ov)):
                        for i in range(4):
                            last = tp(bank[:, P * i:P * i + P], kv[:, e, P * i:P * i + P], ident)
                        last.then_inc(b_vt, 1)
                if s == 1:
                    pe.wait_ge(m_out, 8 + b)
                    for i in range(2):
                        last = mm(sa[:, 256 * i:256 * i + 256], qk[:, 1, P * i:P * i + P], qk[:, 0, 0:SEQ],
                                  start=True, stop=True)
                    last.then_inc(b_s, 1)
                if s == 2:
                    past(pe, b_root, b)
                    if isinstance(b, int) and b == 0:
                        pe.wait_ge(a_exp, 8 * A_HEADS)
                    for i in range(2):
                        last = mm(sc[:, 256 * i:256 * i + 256], qk[:, 1, SEQ + P * i:SEQ + P * i + P],
                                  qk[:, 0, 0:SEQ], start=True, stop=True)
                    last.then_inc(b_s, 1)
                if s == 6:
                    pe.wait_ge(b_pt, 3 * b + 1)
                    for i in range(2):
                        last = mm(sa[:, 256 * i:256 * i + 256], qk[:, 1, SEQ + P * i:SEQ + P * i + P],
                                  qk[:, 0, SEQ:T], start=True, stop=True)
                    last.then_inc(b_s, 1)
                if s == 9:
                    pe.wait_ge(b_pt, 3 * b + 3)
                    pe.wait_ge(b_vtok, 2 * b + 2)
                    for e, bank in enumerate((tr, ov)):
                        ecols = slice(P * e, P * e + P)
                        for i in range(4):
                            mm(bank[:, 0:SEQ], v_tok[:, i, ecols], pt[:, i // 4, i % 4, :], start=(i == 0),
                               stop=(i == 3))
                        for i in range(2):
                            last = mm(bank[:, SEQ:T], v_tok[:, 2 + i, ecols], pt[:, 1, i, :], start=(i == 0),
                                      stop=(i == 1))
                        last.then_inc(b_o, 1)
                if s == 12:
                    pe.wait_ge(b_ocopy, 2 * b + 2)
                    pe.wait_ge(b_pt, 3 * b + 3)
                    for e in range(2):
                        last = mm(sa[:, :], ones, tmp_o[:, e, :], start=(e == 0), stop=(e == 1))
                    last.then_inc(b_mean, 1)
                if s == 16:
                    pe.wait_ge(b_sq, 2 * b + 2)
                    for e in range(2):
                        last = mm(sc[:, :], ones, tmp_r[:, e, :], start=(e == 0), stop=(e == 1))
                    last.then_inc(b_var, 1)

            def norm_q_c(j, s):
                if s == 35:
                    pe.wait_ge(cq_sq, 2 * j + 2)
                    past(pe, c_exp, 8 * j)
                    for i, bank in enumerate((sa, sc)):
                        mm(bank[:, :], ones, tmp_o[:, i, :], start=True, stop=True).then_inc(cq_ss, 1)
                if s == 41:
                    pe.wait_ge(cq_n, j + 1)
                    for i, bank in enumerate((sa, sc)):
                        mm(bank[:, :], rot_c, qk[:, i, :], start=True, stop=True).then_inc(cq_rot, 1)

            def attend_c(j, s):
                if s == 0:
                    pe.wait_ge(cq_sin, 2 * j + 2)
                    sum_mod_lat(12 + j)
                if s == 1:
                    pe.wait_ge(ck_sq, j + 1)
                    pe.wait_ge(m_out, 13 + j)
                    mm(sa[:, :], ones, tmp_o[:, 0, :], start=True, stop=True).then_inc(ck_ss, 1)
                    past(pe, c_out, 4 * j)
                    for i in range(4):
                        last = tp(ov[:, P * i:P * i + P], kv[:, 1, P * i:P * i + P], ident)
                    last.then_inc(c_vt, 1)
                if s == 5:
                    pe.wait_ge(ck_n, j + 1)
                    mm(sc[:, 0:SEQ], rot_c, kv[:, 0, 0:SEQ], start=True, stop=True).then_inc(ck_rot, 1)
                if s >= 11 and (s - 11) % 2 == 0 and (s - 11) // 2 < 8:
                    u = (s - 11) // 2
                    pe.wait_ge(c_p, 8 * j + u + 1)
                    past(pe, c_pt, 8 * j + u)
                    for i in range(4):
                        last = tp(tr[:, P * i:P * i + P], prob[:, u % 2, P * i:P * i + P], ident)
                    last.then_inc(c_t, 1)
                if s >= 8 and s % 2 == 0 and (s - 8) // 2 < 8:
                    u = (s - 8) // 2
                    g, q = u // 2, u % 2
                    if u == 0:
                        pe.wait_ge(ck_rope, j + 1)
                        pe.wait_ge(cq_rope, j + 1)
                        pe.wait_ge(ck_root, j + 1)
                    if u >= 2:
                        pe.wait_ge(c_exp, 8 * j + u - 1)
                    bank = (sa, sc)[u % 2]
                    qcol = 256 * (g % 2) + P * q
                    mm(bank[:, :], qk[:, g // 2, qcol:qcol + P], kv[:, 0, :], start=True, stop=True) \
                        .then_inc(c_s, 1)
                if s >= 14 and (s - 14) % 4 == 0 and (s - 14) // 4 < 4:
                    g = (s - 14) // 4
                    pe.wait_ge(c_pt, 8 * j + 2 * g + 2)
                    if g == 0:
                        pe.wait_ge(c_vtok, j + 1)
                    past(pe, c_out, 4 * j + g)
                    for i in range(4):
                        last = mm(ov[:, 0:SEQ], v_tok[:, i, 0:P], pt[:, g % 2, i, :], start=(i == 0), stop=(i == 3))
                    last.then_inc(c_o, 1)

            ready = 0
            spread = 0
            for kind, what, n0 in prologue():
                for c in range(NCH if kind == "mod" else 2):
                    if kind == "mod":
                        mod_rows(what, c, n0)
                    else:
                        for kt in (what + 2 * c, what + 2 * c + 1):
                            project(n0 - what // 2, kt, 4, T, lambda t: 0, 0, slot0=n0 - what // 2)
                    if c == 0 and spread < ready:
                        spread_rows(spread)
                        spread += 1
                    if kind == "mod" and what == 2 and c == 0:
                        pe.wait_ge(setup_a, 2)
                        pe.wait_ge(ss_add, KT)
                        mm(sc[:, :], ones, prob[:, 1, :], start=True, stop=True).then_inc(ss_sum, 1)
                if kind == "mod":
                    ready = what + 1

            def body_a(h, a):
                for kt in range(KT):
                    project(N_A + NCH * h, kt, 4, T, lambda t: evacs_a(h, t))
                    attend_a(a, kt)

            body_a(1, 0)
            with pe.Fori(2, A_HEADS) as h:
                body_a(h, h - 1)

            def body_b(b, first=False):
                for s in range(2 * KT):
                    blk, kt = s // KT, s % KT
                    project(N_B + 2 * NCH * b + NCH * blk, kt, 3, T, lambda t: evacs_b(b, blk, t))
                    if not first:
                        retain_b(b - 1, s)
                    elif s < KT:
                        attend_a(A_HEADS - 1, s)

            body_b(0, True)
            body_b(1)
            with pe.Fori(2, B_HEADS) as b:
                body_b(b)

            for i, fb, kts, n0 in out_blocks():
                for kt in kts:
                    project(N_O0 + n0, kt, 4, T, lambda t: evacs_o0(i, t), KT if i in (0, 4) else None, kts, n0)
                    if i < 4:
                        retain_b(B_HEADS - 1, EARLY * i + kt)
                if i == 3:
                    pe.wait_ge(b_xc, 2 * B_HEADS)
                    sum_mod(11)
            pe.wait_ge(m_out, 12)
            pe.wait_ge(ss_add, 2 * KT)
            pe.wait_ge(b_root, B_HEADS)
            mm(sc[:, :], ones, prob[:, 1, :], start=True, stop=True).then_inc(ss_sum, 1)

            def body_c(j, first=False):
                for s in range(3 * KT):
                    blk, kt = s // KT, s % KT
                    n0 = N_C + 3 * NCH * j + NCH * blk
                    project(n0, kt, 4 if blk < 2 else 2, SEQ if blk < 2 else T, lambda t: evacs_c(j, blk, t),
                            2 * KT if first and blk == 0 else None)
                    if not first:
                        attend_c(j - 1, s)
                    norm_q_c(j, s)

            body_c(0, True)
            body_c(1)
            with pe.Fori(2, C_KV) as j:
                body_c(j)
            for i, fb, kts, n0 in out_blocks():
                for kt in kts:
                    project(N_O1 + n0, kt, 4, SEQ, lambda t: evacs_o1(i, t), 3 * KT if i in (0, 4) else None, kts,
                            n0)
                    if i < 4:
                        attend_c(C_KV - 1, EARLY * i + kt)
            pe.wait_ge(ss_add, 3 * KT)
            mm(sc[:, 0:SEQ], ones, prob[:, 1, 0:SEQ], start=True, stop=True).then_inc(ss_sum, 1)

        @block.scalar
        def _(act):
            f = act.activation
            for q in range(4):
                act.dma_start(stream[:, 4 * q:4 * q + 4, :], x_t[4 * q:4 * q + 4].rearrange("k p t -> p k t")) \
                    .then_inc(x_loaded[q], 16)
            act.wait_ge(consts_loaded, 32)
            f(st(R_S, 32), sm(S_C, 32), ACT.Silu).then_inc(s_whole, 1)
            act.wait_ge(s_whole, 1)
            act.wait_ge(zeroed, 2)
            for k in range(KT):
                f(s_parts[:, 4 * k:4 * k + 2], st(R_S + 2 * k, 2), ACT.Copy).then_inc(s_ready, 1)
            act.wait_ge(setup_p, 1)
            f(st(R_EXP2, 2), sc[:, 0:2], ACT.Exp).then_inc(setup_a, 1)
            f(st(R_LG, 8), sm(S_DECAY, 8), ACT.Exp).then_inc(setup_a, 1)

            def root_of_mean(i, n):
                act.wait_ge(ss_sum, i + 1)
                act.wait_ge(setup_v, 2)
                f(prob[:, 2, 0:n], sc[:, 0:n], ACT.Sqrt, bias=st(R_EPS), scale=1.0 / D_MODEL).then_inc(ss_root, 1)

            def split_hi(n, c, width=CH):
                past(act, w_used, n - WSLOTS + 1)
                act.wait_ge(w_loaded[c % WSLOTS], loads(n, c))
                f(w_hi[:, c % WSLOTS, 0:width], w_raw[:, c % WSLOTS, 0:width], ACT.Copy).then_inc(w_hi_done, 1)

            def loads(n, c):
                return (n - c % WSLOTS) * (16 // WSLOTS) + 16

            def act_split(i, k, full):
                f(act_hi[:, k, 0:full.shape[-1]], full, ACT.Copy).then_inc(act_hi_done, 1)

            def h_hi(layer, k):
                i = KT * layer + k
                c_scale, c_shift = ((M_SCALE0, M_SHIFT0), (M_SCALE1, M_SHIFT1))[layer]
                act.wait_ge(h_norm, i + 1)
                act.wait_ge(scale_ready, 2 * (k // 4 + 1) if layer == 0 else 2 * PAIRS + 2)
                past(act, act_lo_done, 2 * KT * layer + k - 2 + 1)
                f(tmp_o[:, k % 2, SEQ:T], tmp_r[:, k % 2, SEQ:T], ACT.Identity,
                  bias=modv[:, 1, c_shift + k:c_shift + k + 1], scale=modv[:, 1, c_scale + k:c_scale + k + 1]) \
                    .then_inc(h_ctx, 1)
                act.wait_ge(h_ctx, i + 1)
                act.wait_ge(h_lat, i + 1)
                act_split(layer, k, tmp_o[:, k % 2, :])

            def copy_out(t, dst, count, ready, func=ACT.Copy, ncols=T, scale=1.0):
                act.wait_ge(ready[0], ready[1])
                f(dst, pj[:, t, 0:ncols], func, scale=scale).then_inc(bank_free[t], 1)

            def attend_a(a, s):
                if s == 0:
                    act.wait_ge(a_vt, a + 1)
                    f(v_tok[:, :, 0:P], ov[:, :].rearrange("p (i d) -> p i d", i=4), ACT.Copy).then_inc(a_vtok, 1)
                if s in (6, 8, 10, 12):
                    q = (s - 6) // 2
                    act.wait_ge(a_t, 4 * a + q + 1)
                    n = 4 if q < 2 else 2
                    f(pt[:, q // 2, 0:n, P * (q % 2):P * (q % 2) + P],
                      tr[:, 0:P * n].rearrange("p (i d) -> p i d", i=n), ACT.Copy).then_inc(a_pt, 1)
                if s in (2, 4, 6, 8):
                    q = (s - 2) // 2
                    nk = T if q < 2 else CTX
                    past(act, a_p, 4 * a + q)
                    for m, bank in enumerate((sa, sc)):
                        act.wait_ge(a_max, 8 * a + 2 * q + m + 1)
                        f(prob[:, m, 0:nk], bank[:, 0:nk], ACT.Exp, bias=st(R_NEG + m), accum_out=st(R_SUM + m)) \
                            .then_inc(a_exp, 1)
                if s == 13:
                    act.wait_ge(a_o, 2 * a + 2)
                    past(act, a_y, a)
                    f(tmp_r[:, 0, :], ov[:, :], ACT.Square).then_inc(a_sq, 1)
                if s == 14:
                    act.wait_ge(a_ss, a + 1)
                    f(tmp_r[:, 1, :], tr[:, :], ACT.Sqrt, bias=st(R_EPS), scale=1.0 / (2 * A_DIM)) \
                        .then_inc(a_root, 1)

            def retain_b(b, s):
                if s == 0:
                    past(act, b_pt, 3 * b)
                    past(act, b_y, 2 * b)
                    if isinstance(b, int) and b == 0:
                        act.wait_ge(a_t, 4 * A_HEADS)
                        act.wait_ge(a_out, A_HEADS)
                    f(prob[:, 1, :], aux[:, 3, :], ACT.Exp, scale=stat[:, lg_col(b, 0)]).then_inc(b_expc, 1)
                    f(tmp_r[:, 1, :], aux[:, 4, :], ACT.Exp, scale=stat[:, lg_col(b, 1)]).then_inc(b_expc, 1)
                    act.wait_ge(b_arg, b + 1)
                    f(prob[:, 0, :], tmp_r[:, 0, :], ACT.Exp).then_inc(b_expi, 1)
                    for e, bank in enumerate((tr, ov)):
                        act.wait_ge(b_vt, 2 * b + e + 1)
                        f(v_tok[:, :, P * e:P * e + P], bank[:, :].rearrange("p (i d) -> p i d", i=4), ACT.Copy) \
                            .then_inc(b_vtok, 1)
                if s == 9:
                    for e, bank in enumerate((tr, ov)):
                        act.wait_ge(b_o, 2 * b + e + 1)
                        f(tmp_o[:, e, :], bank[:, :], ACT.Copy).then_inc(b_ocopy, 1)
                if s == 13:
                    for e in range(2):
                        act.wait_ge(b_xc, 2 * b + e + 1)
                        f(tmp_r[:, e, :], tmp_o[:, e, :], ACT.Square).then_inc(b_sq, 1)
                if s == 16:
                    act.wait_ge(b_var, b + 1)
                    f(prob[:, 2, :], sc[:, :], ACT.Sqrt, bias=st(R_EPS), scale=1.0 / (2 * B_DIM)).then_inc(b_root, 1)

            def lg_col(b, direction):
                return bass.ds(R_LG + 4 * direction + b, 1)

            def norm_q_c(j, s):
                if s == 32:
                    for i in range(2):
                        act.wait_ge(bank_free[1 + 2 * i], evacs_c(j, 1, 1 + 2 * i) + 1)
                        act.wait_ge(bank_free[2 * i], evacs_c(j, 1, 2 * i) + 1)
                        if i == 0:
                            past(act, ck_sin, j)
                        f(tmp_o[:, i, :], qk[:, i, :], ACT.Square).then_inc(cq_sq, 1)
                if s == 35:
                    for i, bank in enumerate((sa, sc)):
                        act.wait_ge(cq_ss, 2 * j + i + 1)
                        f(tmp_r[:, i, :], bank[:, :], ACT.Sqrt, bias=st(R_EPS), scale=1.0 / C_DIM) \
                            .then_inc(cq_root, 1)

            def attend_c(j, s):
                if s == 0:
                    act.wait_ge(bank_free[0], evacs_c(j, 2, 0) + 1)
                    act.wait_ge(cq_rope, j + 1)
                    f(tmp_o[:, 0, :], kv[:, 0, :], ACT.Square).then_inc(ck_sq, 1)
                if s == 1:
                    act.wait_ge(ck_ss, j + 1)
                    f(tmp_r[:, 0, :], sa[:, :], ACT.Sqrt, bias=st(R_EPS), scale=1.0 / C_DIM).then_inc(ck_root, 1)
                    act.wait_ge(c_vt, j + 1)
                    f(v_tok[:, :, 0:P], ov[:, :].rearrange("p (i d) -> p i d", i=4), ACT.Copy).then_inc(c_vtok, 1)
                if s >= 11 and (s - 11) % 2 == 0 and (s - 11) // 2 < 8:
                    u = (s - 11) // 2
                    g, q = u // 2, u % 2
                    act.wait_ge(c_t, 8 * j + u + 1)
                    past(act, c_o, 4 * j + max(g - 1, 0))
                    f(pt[:, g % 2, :, P * q:P * q + P], tr[:, :].rearrange("p (i d) -> p i d", i=4), ACT.Copy) \
                        .then_inc(c_pt, 1)
                if s >= 8 and s % 2 == 0 and (s - 8) // 2 < 8:
                    u = (s - 8) // 2
                    act.wait_ge(c_max, 8 * j + u + 1)
                    past(act, c_t, 8 * j + max(u - 1, 0))
                    f(prob[:, u % 2, :], (sa, sc)[u % 2][:, :], ACT.Exp, bias=st(R_NEG + u % 2),
                      accum_out=st(R_SUM + u % 2)).then_inc(c_exp, 1)

            def evac_a(h):
                act.wait_ge(proj_done[1], h + 1)
                past(act, a_s, 8 * h)
                f(qk[:, 1, :], pj[:, 1, :], ACT.Copy).then_inc(bank_free[1], 1)
                act.wait_ge(w_used, N_A + NCH * (h + 1))
                f(stream[:, bass.ds(h, 1), :], pj[:, 3:4, :], ACT.Silu).then_inc(bank_free[3], 1)

            for n in range(AHEAD):
                split_hi(n, n)
            for kind, what, n0 in prologue():
                for c in range(NCH if kind == "mod" else 2):
                    split_hi(n0 + c + AHEAD, n0 + c + AHEAD)
                    if kind == "mod" and what < 2:
                        k = NCH * what + c
                        act.wait_ge(x_loaded[k // 4], 16)
                        past(act, ss_add, k - 1)
                        f(tmp_r[:, k % 2, :], stream[:, k, :], ACT.Square).then_inc(ss_sq, 1)
                    if kind == "mod" and what == 2 and c == 2:
                        root_of_mean(0, T)
                    if kind == "mod" and what >= 2 and what % 2 == 0 and c >= 4:
                        h_hi(0, 2 * (what - 2) + c - 4)
                if kind == "head" and what == 4 * (PAIRS - 2):
                    for k in range(KT - 4, KT):
                        h_hi(0, k)
            evac_a(0)

            def body_a(h, a):
                n0 = N_A + NCH * h
                for kt in range(KT):
                    if kt % 2 == 0:
                        split_hi(n0 + kt // 2 + AHEAD, kt // 2 + AHEAD)
                    if kt == KT - 1:
                        evac_a(h)
                    attend_a(a, kt)

            body_a(1, 0)
            with act.Fori(2, A_HEADS) as h:
                body_a(h, h - 1)

            def body_b(b, first=False):
                n0 = N_B + 2 * NCH * b
                for s in range(2 * KT):
                    if s % 2 == 0:
                        c = s // 2 + AHEAD
                        split_hi(n0 + c, c, 768 if c < 2 * NCH else CH)
                    if s == KT - 1:
                        act.wait_ge(proj_done[1], 8 + 2 * b + 1)
                        if first:
                            act.wait_ge(a_s, 8 * A_HEADS)
                        else:
                            act.wait_ge(b_s, 3 * b)
                        f(qk[:, 1, :], pj[:, 1, :], ACT.Copy, scale=B_DIM ** -0.5).then_inc(bank_free[1], 1)
                    if s == 2 * KT - 1:
                        act.wait_ge(proj_done[1], 8 + 2 * b + 2)
                        f(stream[:, bass.ds(2 * b + 8, 1), :], pj[:, 1:2, :], ACT.Silu).then_inc(bank_free[1], 1)
                        act.wait_ge(w_used, n0 + 2 * NCH)
                        f(stream[:, bass.ds(2 * b + 9, 1), :], pj[:, 2:3, :], ACT.Silu).then_inc(bank_free[2], 1)
                    if not first:
                        retain_b(b - 1, s)
                    elif s < KT:
                        attend_a(A_HEADS - 1, s)

            body_b(0, True)
            body_b(1)
            with act.Fori(2, B_HEADS) as b:
                body_b(b)

            def squares(i, fb, tiles, n):
                for t in range(4):
                    if i == 1:
                        act.wait_ge(x1_lat, 4 * (4 + fb) + t + 1)
                    act.wait_ge(bank_free[t], (evacs_o0, evacs_o1)[i - 1](4 + fb, t) + 1)
                    act.wait_ge(ss_add, tiles + t - 1)
                    f(tmp_r[:, t % 2:t % 2 + 1, 0:n], tiles_of(tiles - KT * i, t, n), ACT.Square).then_inc(ss_sq, 1)

            def tiles_of(first, t, n):
                return stream[:, bass.ds(first + t, 1), 0:n]

            def o_hi(i, k, n_last):
                act.wait_ge(w_used, n_last + k // 2 + 1)
                if i == 1:
                    act.wait_ge(*((a_out, k + 1) if k < A_HEADS else (b_out, k - A_HEADS + 1)))
                    act_split(i, k, stream[:, k, :])
                else:
                    act.wait_ge(c_out, k + 1)
                    act_split(i, k, stream[:, k, SEQ:T])

            for i, fb, kts, n0 in out_blocks():
                for kt in kts:
                    if kt % 2 == 0:
                        c = n0 + (kt - kts[0]) // 2 + AHEAD
                        split_hi(N_O0 + c, c)
                    if i == 0:
                        o_hi(1, kt, N_O0 - NCH)
                    if i == 3 and kt >= EARLY - 4:
                        o_hi(1, kt + 4, N_O0 - NCH)
                    if i < 4:
                        retain_b(B_HEADS - 1, EARLY * i + kt)
                if i >= 4:
                    squares(1, fb, KT + 4 * fb, T)
            root_of_mean(1, T)

            def body_c(j, first=False):
                n0 = N_C + 3 * NCH * j
                for s in range(3 * KT):
                    if s % 2 == 0:
                        c = s // 2 + AHEAD
                        split_hi(n0 + c, c, CH // 2 if 2 * NCH <= c < 3 * NCH else CH)
                    if first and s < KT:
                        h_hi(1, s)
                    if s == KT - 1:
                        for t in range(4):
                            if t < 3:
                                act.wait_ge(proj_done[t], done_c(j, 0, t) + 1)
                            else:
                                act.wait_ge(w_used, n0 + NCH)
                            f(stream[:, bass.ds(4 * j + t, 1), SEQ:T], pj[:, t:t + 1, 0:SEQ], ACT.Silu) \
                                .then_inc(bank_free[t], 1)
                    if s == 2 * KT - 1:
                        for t in (1, 3):
                            if t < 3:
                                act.wait_ge(proj_done[t], done_c(j, 1, t) + 1)
                            else:
                                act.wait_ge(w_used, n0 + 2 * NCH)
                            past(act, c_s, 8 * j)
                            f(qk[:, t // 2, SEQ * (t % 2):SEQ * (t % 2) + SEQ], pj[:, t, 0:SEQ], ACT.Copy) \
                                .then_inc(bank_free[t], 1)
                    if s == 3 * KT - 1:
                        act.wait_ge(w_used, n0 + 3 * NCH)
                        past(act, c_vt, j)
                        f(kv[:, 1, :], pj[:, 1, :], ACT.Copy).then_inc(bank_free[1], 1)
                    if not first:
                        attend_c(j - 1, s)
                    norm_q_c(j, s)

            body_c(0, True)
            body_c(1)
            with act.Fori(2, C_KV) as j:
                body_c(j)

            for i, fb, kts, n0 in out_blocks():
                for kt in kts:
                    if kt % 2 == 0 and n0 + (kt - kts[0]) // 2 + AHEAD < 4 * NCH:
                        c = n0 + (kt - kts[0]) // 2 + AHEAD
                        split_hi(N_O1 + c, c)
                    if i == 0:
                        o_hi(3, kt, N_O1 - NCH)
                    if i == 3 and kt >= EARLY - 4:
                        o_hi(3, kt + 4, N_O1 - NCH)
                    if i < 4:
                        attend_c(C_KV - 1, EARLY * i + kt)
                if i >= 4:
                    squares(2, fb, 2 * KT + 4 * fb, SEQ)
            root_of_mean(2, SEQ)

        @block.gpsimd
        def _(pool):
            for layer in range(2):
                pool.wait_ge(ss_inv, layer + 1)
                for k in range(KT):
                    i = KT * layer + k
                    past(pool, h_lat, i - 1)
                    past(pool, h_ctx, i - 1)
                    if layer == 0 and k == 0:
                        pool.wait_ge(ss_add, KT)
                    pool.tensor_tensor(tmp_r[:, k % 2, :], stream[:, k, :], prob[:, 2, :], ALU.mult) \
                        .then_inc(h_norm, 1)

        @block.vector
        def _(ve):
            def tt(out_, a, b, op):
                return ve.tensor_tensor(out_, a, b, op)

            ve.memset(st(R_EPS), EPS)
            ve.memset(prob[:, 1, :], 0.0).then_inc(zeroed, 1)
            ve.memset(s_parts[:, :].bitcast(F32), 0.0).then_inc(zeroed, 1)
            ve.wait_ge(consts_loaded, 32)
            tt(st(R_PROD, 1), sm(S_DL), sm(S_DL + 1), ALU.mult)
            tt(st(R_PROD + 1, 1), sm(S_DL + 2), sm(S_DL + 3), ALU.mult).then_inc(setup_v, 1)
            ve.tensor_scalar(st(R_SUB), sm(S_SUBLN), 1.0 - LAMBDA_INIT, None, ALU.mult).then_inc(setup_v, 1)
            ve.wait_ge(zeroed, 1)

            def add_square(count, k, n):
                ve.wait_ge(ss_sq, count)
                past(ve, ss_add, count - 1)
                tt(prob[:, 1, 0:n], prob[:, 1, 0:n], tmp_r[:, k % 2, 0:n], ALU.add).then_inc(ss_add, 1)

            def mod0_out(g):
                col = (M_SCALE0, M_SHIFT0)[g % 2] + 4 * (g // 2)
                ve.wait_ge(row_spread, g + 1)
                for v in range(2):
                    last = tt(modv[:, v, col:col + 4], ov[:, 0:8].rearrange("p (f v) -> p v f", v=2)[:, v, :],
                              small[:, S_B + col:S_B + col + 4], ALU.add)
                last.then_inc(mod0_read, 1)
                if g % 2 == 1:
                    col = M_SCALE0 + 4 * (g // 2)
                    ve.wait_ge(mod0_read, g + 1)
                    for v in range(2):
                        ve.scalar_tensor_tensor(modv[:, v, col:col + 4], modv[:, v, col:col + 4], 1.0,
                                                sm(S_G + 4 * (g // 2), 4), ALU.add, ALU.mult) \
                            .then_inc(scale_ready, 1)

            def copy_rows(g):
                ve.wait_ge(w_used, mod_end[g])
                past(ve, row_spread, g - 1)
                ve.tensor_copy(m_acc[0:4, g % 2, :], (tr, sa)[g % 2][0:4, :]).then_inc(row_copied, 1)

            def finish_scale(layer):
                c0 = M_SCALE1
                for v in range(2):
                    ve.scalar_tensor_tensor(modv[:, v, c0:c0 + 16], modv[:, v, c0:c0 + 16], 1.0,
                                            sm(S_G + 16 * layer, 16), ALU.add, ALU.mult).then_inc(scale_ready, 1)
                ve.wait_ge(scale_ready, 2 * PAIRS + 2)

            def split_lo(n, c, width=CH):
                ve.wait_ge(w_hi_done, n + 1)
                s = c % WSLOTS
                tt(w_lo[:, s, 0:width], w_raw[:, s, 0:width], w_hi[:, s, 0:width].bitcast(F32), ALU.subtract) \
                    .then_inc(w_lo_done, 1)

            def h_tile(layer, k):
                i = KT * layer + k
                c_scale, c_shift = ((M_SCALE0, M_SHIFT0), (M_SCALE1, M_SHIFT1))[layer]
                past(ve, act_hi_done, act_count(layer, k) - 1)
                past(ve, act_lo_done, act_count(layer, k) - 1)
                ve.wait_ge(h_norm, i + 1)
                if layer == 0:
                    ve.wait_ge(scale_ready, 2 * (k // 4 + 1))
                ve.tensor_scalar(tmp_o[:, k % 2, 0:SEQ], tmp_r[:, k % 2, 0:SEQ],
                                 modv[:, 0, c_scale + k:c_scale + k + 1], modv[:, 0, c_shift + k:c_shift + k + 1],
                                 ALU.mult, ALU.add).then_inc(h_lat, 1)

            def act_count(layer, k):
                return 2 * KT * layer + k

            def h_lo(layer, k):
                i = act_count(layer, k)
                ve.wait_ge(act_hi_done, i + 1)
                ve.wait_ge(h_ctx, KT * layer + k + 1)
                tt(act_lo[:, k, :], tmp_o[:, k % 2, :], act_hi[:, k, :].bitcast(F32), ALU.subtract) \
                    .then_inc(act_lo_done, 1)

            def mod_chunk(it, c, vectors=2):
                ve.wait_ge(m_loaded[c % MSLOTS], (2 * NCH // 4) * 16 * it + 16 * (c // MSLOTS + 1))
                if c == 0:
                    past(ve, m_sum, it)
                for k2 in range(2):
                    for v in range(vectors):
                        k = 2 * c + k2
                        src, coef, acc = m_raw[:, c % MSLOTS, 512 * k2:512 * k2 + 512], st(R_S + 2 * k + v), m_acc[:, v, :]
                        if k == 0:
                            ins = ve.tensor_scalar(acc, src, coef, None, ALU.mult)
                        else:
                            ve.wait_ge((m_lat, m_ctx)[v], 2 * NCH * it + k)
                            ins = ve.scalar_tensor_tensor(acc, src, coef, acc, ALU.mult, ALU.add)
                        ins.then_inc((m_lat, m_ctx)[v], 1)

            def mod_out(it, vectors=2):
                ve.wait_ge(m_sum, it + 1)
                for v in range(vectors):
                    last = ve.tensor_tensor(modv[:, v, bass.ds(4 * it + 4 * MOD0_GROUPS, 4)], sa[:, 4 * v:4 * v + 4],
                                            small[:, bass.ds(4 * it + 4 * MOD0_GROUPS + S_B, 4)], ALU.add)
                last.then_inc(m_out, 1)

            def lat(ap):
                return ap[:, :, 0:SEQ]

            def rows(ap, n):
                return ap.unsqueeze(1).to_broadcast([P, n, SEQ])

            def attend_a(a, s):
                if s == 0:
                    if not (isinstance(a, int) and a == 0):
                        mod_out(a - 1)
                    ve.wait_ge(a_rot, a + 1)
                    past(ve, a_out, a)
                    rotated = tr[:, :].rearrange("p (i t) -> p i t", i=2)
                    held = tmp_o[:, 0, :].rearrange("p (i t) -> p i t", i=2)
                    tt(held, rotated, rows(trig[:, 1, :], 2), ALU.mult).then_inc(a_tmp, 1)
                    tt(lat(qk), lat(qk), rows(trig[:, 0, :], 2), ALU.mult).then_inc(a_cos, 1)
                    ve.wait_ge(a_tmp, a + 1)
                    ve.wait_ge(a_cos, a + 1)
                    tt(lat(qk), lat(qk), held, ALU.add).then_inc(a_rope, 1)
                if s in (4, 6, 8, 10):
                    combine_a(a, (s - 4) // 2)
                if s in (2, 4, 6, 8):
                    q = (s - 2) // 2
                    nk = T if q < 2 else CTX
                    for m, bank in enumerate((sa, sc)):
                        ve.wait_ge(a_s, 8 * a + 2 * q + m + 1)
                        ve.tensor_reduce(st(R_NEG + m), bank[:, 0:nk], AX_X, ALU.max, negate=True).then_inc(a_max, 1)
                if s == 14:
                    ve.wait_ge(a_root, a + 1)
                    ve.reciprocal(tmp_r[:, 1, :], tmp_r[:, 1, :]).then_inc(a_inv, 1)
                    ve.wait_ge(a_inv, a + 1)
                    ve.scalar_tensor_tensor(tmp_o[:, 1, :], ov[:, :], st(R_SUB), tmp_r[:, 1, :], ALU.mult,
                                            ALU.mult).then_inc(a_y, 1)
                    ve.wait_ge(a_y, a + 1)
                    tile = stream[:, bass.ds(a, 1), :]
                    tt(tile, tile, tmp_o[:, 1:2, :], ALU.mult).then_inc(a_out, 1)

            def combine_a(a, q):
                nk = T if q < 2 else CTX
                n = 4 * a + q
                ve.wait_ge(a_exp, 8 * a + 2 * q + 2)
                ve.reciprocal(st(R_REC, 2), st(R_SUM, 2)).then_inc(a_rec, 1)
                ve.wait_ge(a_rec, n + 1)
                tt(st(R_C2), st(R_REC + 1), st(R_LAM), ALU.mult).then_inc(a_c2, 1)
                ve.wait_ge(a_c2, n + 1)
                ve.tensor_scalar(prob[:, 1, 0:nk], prob[:, 1, 0:nk], st(R_C2), None, ALU.mult).then_inc(a_p2, 1)
                ve.wait_ge(a_p2, n + 1)
                past(ve, a_t, n)
                ve.scalar_tensor_tensor(prob[:, 2, 0:nk], prob[:, 0, 0:nk], st(R_REC), prob[:, 1, 0:nk], ALU.mult,
                                        ALU.subtract).then_inc(a_p, 1)

            def retain_b(b, s):
                if s == 0:
                    past(ve, b_y, 2 * b)
                    ve.tensor_scalar(tmp_r[:, 0, :], aux[:, 1, :], stat[:, bass.ds(R_LG + 4 + b, 1)], None, ALU.mult) \
                        .then_inc(b_argb, 1)
                    ve.wait_ge(b_argb, b + 1)
                    ve.scalar_tensor_tensor(tmp_r[:, 0, :], aux[:, 0, :], stat[:, bass.ds(R_LG + b, 1)],
                                            tmp_r[:, 0, :], ALU.mult, ALU.add).then_inc(b_arg, 1)
                    mod_out(7 + b)
                    ve.wait_ge(b_expc, 2 * b + 2)
                    tt(prob[:, 1, :], prob[:, 1, :], tmp_r[:, 1, :], ALU.add).then_inc(b_dc, 1)
                    ve.wait_ge(b_expi, b + 1)
                    tt(prob[:, 0, :], prob[:, 0, :], aux[:, 2, :], ALU.add).then_inc(b_di, 1)
                if s in (3, 4, 7):
                    i = (3, 4, 7).index(s)
                    ve.wait_ge(b_s, 3 * b + i + 1)
                    if i == 0:
                        ve.wait_ge(b_di, b + 1)
                        ve.wait_ge(b_dc, b + 1)
                        if isinstance(b, int) and b == 0:
                            ve.wait_ge(a_o, 2 * A_HEADS)
                        past(ve, b_o, 2 * b)
                    dst = pt[:, i // 2, 2 * (i % 2):2 * (i % 2) + 2, :]
                    tt(dst, (sa, sc, sa)[i][:, :].rearrange("p (i t) -> p i t", i=2),
                       prob[:, (0, 1, 0)[i], :].rearrange("p (i t) -> p i t", i=2), ALU.mult).then_inc(b_pt, 1)
                if s == 12:
                    ve.wait_ge(b_mean, b + 1)
                    for e in range(2):
                        ve.scalar_tensor_tensor(tmp_o[:, e, :], sa[:, :], -1.0 / (2 * B_DIM), tmp_o[:, e, :],
                                                ALU.mult, ALU.add).then_inc(b_xc, 1)
                if s == 17:
                    ve.wait_ge(b_root, b + 1)
                    ve.reciprocal(prob[:, 2, :], prob[:, 2, :]).then_inc(b_inv, 1)
                    ve.wait_ge(b_inv, b + 1)
                    ve.wait_ge(b_var, b + 1)
                    for e in range(2):
                        ve.scalar_tensor_tensor(tmp_r[:, e, :], tmp_o[:, e, :], small[:, bass.ds(S_GN + 2 * b + e, 1)],
                                                prob[:, 2, :], ALU.mult, ALU.mult).then_inc(b_y, 1)
                    for e in range(2):
                        ve.wait_ge(b_y, 2 * b + e + 1)
                        tile = stream[:, bass.ds(2 * b + 8 + e, 1), :]
                        tt(tile, tile, tmp_r[:, e:e + 1, :], ALU.mult).then_inc(b_out, 1)

            def norm_q_c(j, s):
                if s == 36:
                    ve.wait_ge(cq_root, 2 * j + 2)
                    ve.reciprocal(tmp_r[:, :, :], tmp_r[:, :, :]).then_inc(cq_inv, 1)
                    ve.wait_ge(cq_inv, j + 1)
                    ve.scalar_tensor_tensor(qk[:, :, :], qk[:, :, :], sm(S_QK), tmp_r[:, :, :], ALU.mult, ALU.mult) \
                        .then_inc(cq_n, 1)
                if s == 41:
                    for i, bank in enumerate((sa, sc)):
                        ve.wait_ge(cq_rot, 2 * j + i + 1)
                        tt(tmp_o[:, i, :].rearrange("p (g t) -> p g t", g=2),
                           bank[:, :].rearrange("p (g t) -> p g t", g=2), rows(trig[:, 1, :], 2), ALU.mult) \
                            .then_inc(cq_sin, 1)
                    heads = qk[:, :, :].rearrange("p i (g t) -> p (i g) t", g=2)
                    tt(heads, heads, rows(trig[:, 0, :], 4), ALU.mult).then_inc(cq_cos, 1)
                    ve.wait_ge(cq_cos, j + 1)
                    ve.wait_ge(cq_sin, 2 * j + 2)
                    tt(qk[:, :, :], qk[:, :, :], tmp_o[:, :, :], ALU.add).then_inc(cq_rope, 1)

            def attend_c(j, s):
                if s == 0:
                    mod_out(12 + j, 1)
                if s == 2:
                    ve.wait_ge(ck_root, j + 1)
                    ve.reciprocal(tmp_r[:, 0, :], tmp_r[:, 0, :]).then_inc(ck_inv, 1)
                    ve.wait_ge(ck_inv, j + 1)
                    ve.scalar_tensor_tensor(kv[:, 0, :], kv[:, 0, :], sm(S_QK + 1), tmp_r[:, 0, :], ALU.mult,
                                            ALU.mult).then_inc(ck_n, 1)
                if s == 5:
                    ve.wait_ge(ck_rot, j + 1)
                    ve.wait_ge(ck_ss, j + 1)
                    tt(tmp_o[:, 0, 0:SEQ], sc[:, 0:SEQ], trig[:, 1, :], ALU.mult).then_inc(ck_sin, 1)
                    tt(kv[:, 0, 0:SEQ], kv[:, 0, 0:SEQ], trig[:, 0, :], ALU.mult).then_inc(ck_cos, 1)
                    ve.wait_ge(ck_sin, j + 1)
                    ve.wait_ge(ck_cos, j + 1)
                    tt(kv[:, 0, 0:SEQ], kv[:, 0, 0:SEQ], tmp_o[:, 0, 0:SEQ], ALU.add).then_inc(ck_rope, 1)
                if s >= 9 and (s - 9) % 2 == 0 and (s - 9) // 2 < 8:
                    u = (s - 9) // 2
                    ve.wait_ge(c_exp, 8 * j + u + 1)
                    ve.reciprocal(st(R_REC + u % 2), st(R_SUM + u % 2)).then_inc(c_rec, 1)
                    ve.wait_ge(c_rec, 8 * j + u + 1)
                    ve.tensor_scalar(prob[:, u % 2, :], prob[:, u % 2, :], st(R_REC + u % 2), None, ALU.mult) \
                        .then_inc(c_p, 1)
                if s >= 8 and s % 2 == 0 and (s - 8) // 2 < 8:
                    u = (s - 8) // 2
                    ve.wait_ge(c_s, 8 * j + u + 1)
                    ve.tensor_reduce(st(R_NEG + u % 2), (sa, sc)[u % 2][:, :], AX_X, ALU.max, negate=True) \
                        .then_inc(c_max, 1)
                if s >= 14 and (s - 14) % 4 == 0 and (s - 14) // 4 < 4:
                    g = (s - 14) // 4
                    ve.wait_ge(c_o, 4 * j + g + 1)
                    tile = stream[:, bass.ds(4 * j + g, 1), SEQ:T]
                    tt(tile, tile, ov[:, 0:SEQ].unsqueeze(1), ALU.mult).then_inc(c_out, 1)

            def evac_a(h):
                ve.wait_ge(proj_done[0], h + 1)
                past(ve, a_s, 8 * h)
                ve.tensor_scalar(qk[:, 0, :], pj[:, 0, :], A_DIM ** -0.5, None, ALU.mult).then_inc(bank_free[0], 1)
                ve.wait_ge(proj_done[2], h + 1)
                past(ve, a_vt, h)
                ve.tensor_copy(kv[:, 0, :], pj[:, 2, :]).then_inc(bank_free[2], 1)

            ve.wait_ge(s_ready, KT)
            for k in range(KT):
                tt(s_parts[:, 4 * k + 2:4 * k + 4], st(R_S + 2 * k, 2), s_parts[:, 4 * k:4 * k + 2].bitcast(F32),
                   ALU.subtract).then_inc(s_ready, 1)
            for n in range(AHEAD):
                split_lo(n, n)
            ve.wait_ge(trig_loaded, 16)
            mod_end = {what: n0 + NCH for kind, what, n0 in prologue() if kind == "mod"}
            copied = 0
            for kind, what, n0 in prologue():
                for c in range(NCH if kind == "mod" else 2):
                    split_lo(n0 + c + AHEAD, n0 + c + AHEAD)
                    if kind == "mod" and what < 2:
                        add_square(NCH * what + c + 1, c, T)
                    if c == 0 and copied < MOD0_GROUPS and n0 >= mod_end[copied]:
                        copy_rows(copied)
                    if c == 1 and copied < MOD0_GROUPS and n0 >= mod_end[copied]:
                        mod0_out(copied)
                        copied += 1
                    if kind == "mod" and what == 2 and c == 0:
                        ve.wait_ge(setup_a, 2)
                        ve.scalar_tensor_tensor(st(R_LAM), st(R_EXP2), LAMBDA_INIT, st(R_EXP2 + 1), ALU.add,
                                                ALU.subtract)
                        ve.tensor_scalar(st(R_LG, 8), st(R_LG, 8), -1.0, None, ALU.mult).then_inc(setup_v, 1)
                    if kind == "mod" and what == 2 and c == 2:
                        ve.wait_ge(ss_root, 1)
                        ve.reciprocal(prob[:, 2, :], prob[:, 2, :]).then_inc(ss_inv, 1)
                    if kind == "mod" and what >= 2 and what % 2 == 0 and c >= 4:
                        h_tile(0, 2 * (what - 2) + c - 4)
                        h_lo(0, 2 * (what - 2) + c - 4)
                if kind == "head" and what == 4 * (PAIRS - 2):
                    for k in range(KT - 4, KT):
                        h_tile(0, k)
                        h_lo(0, k)
            evac_a(0)

            def body_a(h, a):
                n0 = N_A + NCH * h
                for kt in range(KT):
                    if kt % 2 == 0:
                        split_lo(n0 + kt // 2 + AHEAD, kt // 2 + AHEAD)
                    if kt == KT - 1:
                        evac_a(h)
                    attend_a(a, kt)
                    if kt % 2 == 1:
                        mod_chunk(h - 1, kt // 2)

            body_a(1, 0)
            with ve.Fori(2, A_HEADS) as h:
                body_a(h, h - 1)

            def body_b(b, first=False):
                n0 = N_B + 2 * NCH * b
                for s in range(2 * KT):
                    if s % 2 == 0:
                        c = s // 2 + AHEAD
                        split_lo(n0 + c, c, 768 if c < 2 * NCH else CH)
                    if s == KT - 1:
                        ve.wait_ge(proj_done[0], 8 + 2 * b + 1)
                        if first:
                            ve.wait_ge(a_s, 8 * A_HEADS)
                            ve.wait_ge(a_vt, A_HEADS)
                        else:
                            ve.wait_ge(b_s, 3 * b)
                            ve.wait_ge(b_vt, 2 * b)
                        ve.tensor_copy(qk[:, 0, :], pj[:, 0, :]).then_inc(bank_free[0], 1)
                        ve.wait_ge(w_used, n0 + NCH)
                        ve.tensor_copy(kv[:, 0, :], pj[:, 2, :]).then_inc(bank_free[2], 1)
                    if s == 2 * KT - 1:
                        ve.wait_ge(proj_done[0], 8 + 2 * b + 2)
                        ve.tensor_copy(kv[:, 1, :], pj[:, 0, :]).then_inc(bank_free[0], 1)
                    if not first:
                        retain_b(b - 1, s)
                    elif s < KT:
                        attend_a(A_HEADS - 1, s)
                    if s % 4 == 3:
                        mod_chunk(7 + b, s // 4)

            ve.wait_ge(dist_loaded, 16)
            body_b(0, True)
            body_b(1)
            with ve.Fori(2, B_HEADS) as b:
                body_b(b)

            def residual(layer, i, fb, n):
                for t in range(4):
                    if t < 3:
                        ve.wait_ge(proj_done[t], done_out(layer, i, t) + 1)
                    else:
                        ve.wait_ge(w_used, (N_O0, N_O1)[layer] + block_end[i])
                    for v in range(n // 256):
                        cols = slice(256 * v, 256 * v + 256)
                        tile = stream[:, 4 * fb + t, cols]
                        old = aux[:, t, cols] if layer == 0 and i < 4 else tile
                        col = (M_GATE0, M_GATE1)[layer] + 4 * fb + t
                        ve.scalar_tensor_tensor(tile, pj[:, t, cols], modv[:, v, col:col + 1], old, ALU.mult,
                                                ALU.add).then_inc(x1_lat if v < n // 256 - 1 else bank_free[t], 1)
                if i >= 4:
                    for t in range(4):
                        add_square(KT * (layer + 1) + 4 * fb + t + 1, t, n)

            block_end = {i: n0 + len(kts) // 2 for i, fb, kts, n0 in out_blocks()}

            def o_lo(i, k):
                n = KT * i + k
                ve.wait_ge(act_hi_done, n + 1)
                cols = slice(0, T) if i == 1 else slice(SEQ, T)
                width = T if i == 1 else SEQ
                tt(act_lo[:, k, 0:width], stream[:, k, cols], act_hi[:, k, 0:width].bitcast(F32), ALU.subtract) \
                    .then_inc(act_lo_done, 1)

            for i, fb, kts, n0 in out_blocks():
                for kt in kts:
                    if kt % 2 == 0:
                        c = n0 + (kt - kts[0]) // 2
                        split_lo(N_O0 + c + AHEAD, c + AHEAD)
                    if i == 0:
                        o_lo(1, kt)
                    if i == 3 and kt >= EARLY - 4:
                        o_lo(1, kt + 4)
                    if i < 4:
                        retain_b(B_HEADS - 1, EARLY * i + kt)
                        if kt % 2 == 1 and c < 2 * NCH and c % 2 == 0:
                            mod_chunk(11, c // 2)
                if i < 4:
                    ve.wait_ge(xr_loaded, 16 * (fb + 1))
                if i == 3:
                    ve.wait_ge(b_dc, B_HEADS)
                    ve.memset(prob[:, 1, :], 0.0).then_inc(zeroed, 1)
                    ve.wait_ge(zeroed, 3)
                    mod_out(11)
                    ve.wait_ge(m_out, 12)
                residual(0, i, fb, T)
            finish_scale(1)
            ve.wait_ge(ss_root, 2)
            ve.reciprocal(prob[:, 2, :], prob[:, 2, :]).then_inc(ss_inv, 1)

            def body_c(j, first=False):
                n0 = N_C + 3 * NCH * j
                for s in range(3 * KT):
                    if first and s < KT:
                        h_tile(1, s)
                    if s % 2 == 0:
                        c = s // 2 + AHEAD
                        split_lo(n0 + c, c, CH // 2 if 2 * NCH <= c < 3 * NCH else CH)
                    if first and s < KT:
                        h_lo(1, s)
                    if s == 2 * KT - 1:
                        for t in (0, 2):
                            ve.wait_ge(proj_done[t], done_c(j, 1, t) + 1)
                            past(ve, c_s, 8 * j)
                            ve.tensor_copy(qk[:, t // 2, 0:SEQ], pj[:, t, 0:SEQ]).then_inc(bank_free[t], 1)
                    if s == 3 * KT - 1:
                        ve.wait_ge(proj_done[0], done_c(j, 2, 0) + 1)
                        ve.tensor_copy(kv[:, 0, :], pj[:, 0, :]).then_inc(bank_free[0], 1)
                    if not first:
                        attend_c(j - 1, s)
                    norm_q_c(j, s)
                    if s % 6 == 1:
                        mod_chunk(12 + j, s // 6, 1)

            ve.tensor_scalar(sm(S_QK), sm(S_QK), C_DIM ** -0.5, None, ALU.mult).then_inc(setup_v, 1)
            ve.wait_ge(setup_v, 4)
            ve.wait_ge(trig_loaded, 32)
            body_c(0, True)
            body_c(1)
            with ve.Fori(2, C_KV) as j:
                body_c(j)

            for i, fb, kts, n0 in out_blocks():
                for kt in kts:
                    c = n0 + (kt - kts[0]) // 2 + AHEAD
                    if kt % 2 == 0 and c < 4 * NCH:
                        split_lo(N_O1 + c, c)
                    if i == 0:
                        o_lo(3, kt)
                    if i == 3 and kt >= EARLY - 4:
                        o_lo(3, kt + 4)
                    if i < 4:
                        attend_c(C_KV - 1, EARLY * i + kt)
                if i == 3:
                    ve.wait_ge(c_t, 8 * C_KV)
                    ve.memset(prob[:, 1, :], 0.0).then_inc(zeroed, 1)
                    ve.wait_ge(zeroed, 4)
                residual(1, i, fb, SEQ)
            ve.wait_ge(ss_root, 3)
            ve.reciprocal(prob[:, 2, 0:SEQ], prob[:, 2, 0:SEQ]).then_inc(ss_inv, 1)
            ve.wait_ge(ss_inv, 3)
            for k in range(KT):
                tile = stream[:, k, 0:SEQ]
                ve.scalar_tensor_tensor(tile, tile, sm(S_FN + k), prob[:, 2, 0:SEQ], ALU.mult, ALU.mult) \
                    .then_inc(out_ready, 1)


def _rotation(dim):
    axis, half = dim // 2, dim // 4
    m = np.zeros((P, P), np.float32)
    for f in range(P):
        if f % axis < half:
            m[f + half, f] = -1.0
        else:
            m[f - half, f] = 1.0
    return m


def _angles(dim):
    axis, half = dim // 2, dim // 4
    tok = np.arange(SEQ)
    pos = np.stack([tok // GRID_W, tok % GRID_W]).astype(np.float32)
    inv = (ROPE_THETA ** (-np.arange(0, axis, 2, dtype=np.float32) / np.float32(axis))).astype(np.float32)
    ang = np.zeros((P, SEQ), np.float32)
    for f in range(P):
        ang[f] = pos[(f % dim) // axis] * inv[f % axis % half]
    return np.stack([np.cos(ang), np.sin(ang)], 1).astype(np.float32)


def _distances():
    k = np.arange(256).reshape(2, P).transpose(1, 0)[:, :, None]
    q = np.arange(256)[None, None, :]
    d = [np.maximum(q - k, 0), np.maximum(k - q, 0), (q == k) * 1, 256 + q - k, 256 - q + k]
    return np.stack([v.reshape(P, 512) for v in d], 1).astype(np.float32)


def kernel(**inputs):
    import concourse.bacc as _bacc
    from concourse.bass_utils import run_bass_kernel_spmd as _run

    a = {k: np.asarray(v) for k, v in inputs.items()}

    def chunks(w, blocks):
        cols = [np.concatenate([w[:, s:s + n] for s, n in b], 1) for b in blocks]
        return np.ascontiguousarray(np.concatenate(
            [b.reshape(NCH, 2, P, -1).transpose(0, 2, 1, 3).reshape(NCH, P, -1) for b in cols], 0))

    ev, od = a["ev_w_in"][0], a["od_w_in"][0]
    mod_order = [(0, 1), (0, 0), (0, 2), (1, 1), (1, 0), (1, 2)]
    four = [[(512 * i, 512)] for i in range(4)]
    w_mod = np.concatenate([chunks(a["w_mod"][l][:, 2048 * t:2048 * t + 2048], four) for l, t in mod_order[2:]], 0)
    b_mod = np.concatenate([a["b_mod"][l, 2048 * t:2048 * t + 2048].reshape(16, P) for l, t in mod_order], 0).T
    w_b = []
    for b in range(B_HEADS):
        q, k, v, g = 4096 + 128 * b, 4608 + 128 * b, 5120 + 256 * b, 6144 + 256 * b
        w_b += [[(q, 128), (k, 128), (v, 128)], [(v + 128, 128), (g, 256)]]
    w_c = []
    for j in range(C_KV):
        w_c += [[(3072 + 512 * j, 512)], [(512 * j, 512)], [(2048 + 128 * j, 128), (2560 + 128 * j, 128)]]
    w_all = np.zeros((N_END, P, CH), np.float32)

    def place(n, part):
        w_all[n:n + len(part), :, 0:part.shape[-1]] = part

    heads_a = [[(1024 * i + 128 * h, 128) for i in range(4)] for h in range(A_HEADS)]
    first_head = chunks(ev, heads_a[0:1])
    for kind, what, n0 in prologue():
        if kind == "mod":
            t = 1 - what % 2
            place(n0, chunks(a["w_mod"][0], [[(2048 * t + 512 * (what // 2), 512)]]))
        else:
            place(n0, first_head[what // 2:what // 2 + 2])
    place(N_A + NCH, chunks(ev, heads_a[1:]))
    for i, block in enumerate(w_b):
        place(N_B + NCH * i, chunks(ev, [block]))
    for i, block in enumerate(w_c):
        place(N_C + NCH * i, chunks(od, [block]))
    for start, w in ((N_O0, a["ev_w_out"][0]), (N_O1, a["od_w_out"][0])):
        for i, fb, kts, n0 in out_blocks():
            place(start + n0, chunks(w, four[fb:fb + 1])[kts[0] // 2:kts[-1] // 2 + 1])
    small = np.zeros((P, S_END), np.float32)
    small[:, S_C:S_C + 32] = np.stack([a["c"][0].reshape(16, P).T, a["c_ctx"].reshape(16, P).T], -1).reshape(P, 32)
    small[:, S_G:S_G + 32] = a["norm_g"].reshape(32, P).T
    small[:, S_B:S_B + 96] = b_mod
    small[:, S_SUBLN] = a["diff_subln"][0]
    small[:, S_DECAY:S_DECAY + 8] = a["ret_decay"][0].reshape(1, 8)
    small[:, S_GN:S_GN + 8] = a["ret_gn"][0].reshape(8, P).T
    small[:, S_QK:S_QK + 2] = a["qk_norm"][0].T
    small[:, S_FN:S_FN + 16] = a["final_norm"].reshape(16, P).T
    small[0:A_DIM, S_DL:S_DL + 4] = a["diff_lambda"][0].T
    small[0:4, S_SEL:S_SEL + 2] = [[1, 0], [0, 1], [1, 0], [0, 1]]
    arrays = {
        "x_t": np.ascontiguousarray(np.concatenate([a["x"][0], a["ctx"][0]], 0).T).reshape(KT, P, T),
        "w_mod": w_mod,
        "w_all": w_all,
        "small_in": small,
        "mats_in": np.stack([_rotation(A_DIM), _rotation(C_DIM), np.ones((P, P), np.float32),
                             np.eye(P, dtype=np.float32)], 1),
        "trig_in": np.stack([_angles(A_DIM), _angles(C_DIM)], 0),
        "dist_in": _distances(),
    }
    arrays = {k: np.ascontiguousarray(v) for k, v in arrays.items()}
    nc = _bacc.Bacc("TRN2", target_bir_lowering=False, num_devices=1)
    args = [nc.dram_tensor(k, v.shape, F32, kind="ExternalInput").ap() for k, v in arrays.items()]
    args.append(nc.dram_tensor("out_t", (KT, P, SEQ), F32, kind="ExternalOutput").ap())
    bass_hybrid_backbone(nc, *args)
    r = _run(nc, [arrays], core_ids=[0])
    got = np.asarray(r.results[0]["out_t"])
    return np.ascontiguousarray(got.reshape(D_MODEL, SEQ).T).reshape(1, SEQ, D_MODEL)
```

```python
import math
from contextlib import ExitStack

import numpy as np

import concourse.bass as bass
from concourse import mybir

F32 = mybir.dt.float32
F32R = mybir.dt.float32r
ALU = mybir.AluOpType
ACT = mybir.ActivationFunctionType
AX_X = mybir.AxisListType.X

P = 128
D_MODEL = 2048
SEQ = 256
CTX = 256
T = SEQ + CTX
GRID_W = 64
ROPE_THETA = 10000.0
EPS = 1e-6
KT = D_MODEL // P
NCH = KT // 2
CH = 2 * 512
A_HEADS, A_DIM = 8, 64
B_HEADS, B_DIM = 4, 128
C_HEADS, C_KV, C_DIM = 16, 4, 128
C_GROUP = C_HEADS // C_KV
LAMBDA_INIT = 0.8 - 0.6 * math.exp(-0.3 * 0)
WSLOTS, MSLOTS = 4, 2
AHEAD = 3

MOD0_GROUPS = 8
PAIRS = 4
FIRST_SQUARE = 4
N_A = NCH * MOD0_GROUPS
N_B = N_A + NCH * A_HEADS
N_O0 = N_B + 2 * NCH * B_HEADS
N_C = N_O0 + NCH * 4
N_O1 = N_C + 3 * NCH * C_KV
N_END = N_O1 + NCH * 4
EARLY = 12

S_C, S_G, S_B, S_SUBLN, S_DECAY, S_GN, S_QK, S_FN, S_DL = 0, 32, 64, 160, 161, 169, 177, 179, 195
S_SEL = 199
S_END = 201
(R_S, R_LG, R_LAM, R_EXP2, R_PROD, R_NEG, R_SUM, R_REC, R_C2, R_SUB, R_EPS, R_RMS) = (
    0, 32, 40, 41, 43, 45, 47, 49, 51, 52, 53, 54)
R_END = 62
M_SCALE0, M_SHIFT0, M_GATE0, M_SCALE1, M_SHIFT1, M_GATE1 = (16 * i for i in range(6))


def prologue():
    head = iter(range(NCH))
    for g in range(MOD0_GROUPS):
        for c in range(NCH):
            yield "mod", g, c
        if 3 <= g:
            yield "head", 0, next(head)
    for c in head:
        yield "head", 0, c


def input_runs():
    heads = [n for n, (kind, what, c) in enumerate(prologue()) if kind == "head"]
    runs = {heads[0] - 4: (0, 1)}
    for i in range(1, NCH - 2):
        runs[heads[i - 1]] = (2 * i, 2 * i + 1)
    runs[heads[NCH - 3]] = (KT - 4, KT - 1)
    return runs


def out_blocks():
    for i in range(8):
        first = i < 4
        yield (i, i % 4, range(EARLY) if first else range(EARLY, KT),
               EARLY // 2 * i if first else 4 * (EARLY // 2) + (KT - EARLY) // 2 * (i - 4))


def bass_hybrid_backbone(nc, x_t, w_mod, w_all, small_in, mats_in, trig_in,
                         dist_in, out):
    ctx = ExitStack()
    with ctx:
        def sb(name, shape, dt=F32):
            return ctx.enter_context(nc.sbuf_tensor(name, shape, dt))

        def sem(name):
            return ctx.enter_context(nc.semaphore(name))

        w_raw = sb("w_raw", [P, WSLOTS, CH])
        w_hi = sb("w_hi", [P, WSLOTS, CH], F32R)
        w_lo = sb("w_lo", [P, WSLOTS, CH], F32R)
        m_raw = sb("m_raw", [P, MSLOTS, CH])
        m_acc = sb("m_acc", [P, 2, 512])
        act_hi = sb("act_hi", [P, KT, T], F32R)
        act_lo = sb("act_lo", [P, KT, T], F32R)
        stream = sb("stream", [P, KT, T])
        mats = sb("mats", [P, 4, P])
        trig = sb("trig", [P, 2, SEQ])
        aux = sb("aux", [P, 5, 512])
        qk = sb("qk", [P, 2, T])
        kv = sb("kv", [P, 2, T])
        v_tok = sb("v_tok", [P, 4, 256])
        pt = sb("pt", [P, 2, 4, 256])
        prob = sb("prob", [P, 3, 512])
        tmp_o = sb("tmp_o", [P, 2, 512])
        tmp_r = sb("tmp_r", [P, 2, 512])
        small = sb("small", [P, S_END])
        stat = sb("stat", [P, R_END])
        modv = sb("modv", [P, 2, 96])
        s_parts = sb("s_parts", [P, 4 * KT + P], F32R)

        pj = ctx.enter_context(nc.psum_tensor("pj", [P, 4, 512], F32))
        sa = ctx.enter_context(nc.psum_tensor("sa", [P, 512], F32))
        sc = ctx.enter_context(nc.psum_tensor("sc", [P, 512], F32))
        tr = ctx.enter_context(nc.psum_tensor("tr", [P, 512], F32))
        ov = ctx.enter_context(nc.psum_tensor("ov", [P, 512], F32))

        vector_parts = s_parts[:, 0:4 * KT].rearrange("p (k v) -> p k v", v=4)
        rot_a, rot_c, ones, ident = (mats[:, i, :] for i in range(4))

        normed = [tmp_r[:, 0, :], tmp_r[:, 1, :], kv[:, 0, :], kv[:, 1, :]]
        modulated = [tmp_o[:, 0, :], tmp_o[:, 1, :], qk[:, 0, :], qk[:, 1, :]]
        depth = len(normed)

        def st(c, n=1):
            return stat[:, c:c + n]

        def sm(c, n=1):
            return small[:, c:c + n]

        consts_loaded, dist_loaded = sem("consts_loaded"), sem("dist_loaded")
        x_loaded = [sem(f"x_loaded{i}") for i in range(4)]
        w_loaded = [sem(f"w_loaded{i}") for i in range(WSLOTS)]
        m_loaded = [sem(f"m_loaded{i}") for i in range(MSLOTS)]
        xr_loaded = sem("xr_loaded")
        trig_loaded = sem("trig_loaded")
        out_stored = sem("out_stored")
        w_hi_done, w_lo_done, w_used = sem("w_hi_done"), sem("w_lo_done"), sem("w_used")
        row_copied, row_spread, mod0_read = sem("row_copied"), sem("row_spread"), sem("mod0_read")
        m_lat, m_ctx, m_sum, m_out = sem("m_lat"), sem("m_ctx"), sem("m_sum"), sem("m_out")
        setup_v, setup_a, setup_p = sem("setup_v"), sem("setup_a"), sem("setup_p")
        s_whole, s_ready, zeroed = sem("s_whole"), sem("s_ready"), sem("zeroed")
        ss_sq, ss_add, ss_sum, ss_root, ss_rec, ss_spread, ss_inv = (
            sem("ss_sq"), sem("ss_add"), sem("ss_sum"), sem("ss_root"), sem("ss_rec"), sem("ss_spread"), sem("ss_inv"))
        h_norm, h_lat, h_ctx = sem("h_norm"), sem("h_lat"), sem("h_ctx")
        act_hi_done, act_lo_done = sem("act_hi_done"), sem("act_lo_done")
        scale_ready = sem("scale_ready")
        proj_done = [sem(f"proj_done{i}") for i in range(4)]
        bank_free = [sem(f"bank_free{i}") for i in range(4)]
        x1_lat = sem("x1_lat")
        out_ready = sem("out_ready")
        a_rot, a_vt, a_vtok, a_tmp, a_cos, a_rope = (sem("a_rot"), sem("a_vt"), sem("a_vtok"), sem("a_tmp"),
                                                     sem("a_cos"), sem("a_rope"))
        a_s, a_max, a_exp, a_rec, a_c2, a_p2, a_p = (sem("a_s"), sem("a_max"), sem("a_exp"), sem("a_rec"),
                                                     sem("a_c2"), sem("a_p2"), sem("a_p"))
        a_t, a_pt, a_o, a_sq, a_ss, a_root, a_inv, a_spread, a_y, a_out = (
            sem("a_t"), sem("a_pt"), sem("a_o"), sem("a_sq"), sem("a_ss"), sem("a_root"), sem("a_inv"),
            sem("a_spread"), sem("a_y"), sem("a_out"))
        b_vt, b_vtok, b_argb, b_arg, b_expi, b_expc, b_di, b_dc = (
            sem("b_vt"), sem("b_vtok"), sem("b_argb"), sem("b_arg"), sem("b_expi"), sem("b_expc"), sem("b_di"),
            sem("b_dc"))
        b_s, b_pt, b_o, b_ocopy, b_mean, b_xc, b_sq, b_var, b_root, b_inv, b_spread, b_y, b_out = (
            sem("b_s"), sem("b_pt"), sem("b_o"), sem("b_ocopy"), sem("b_mean"), sem("b_xc"), sem("b_sq"),
            sem("b_var"), sem("b_root"), sem("b_inv"), sem("b_spread"), sem("b_y"), sem("b_out"))
        cq_sq, cq_ss, cq_root, cq_inv, cq_spread, cq_n, cq_rot, cq_sin, cq_cos, cq_rope = (
            sem("cq_sq"), sem("cq_ss"), sem("cq_root"), sem("cq_inv"), sem("cq_spread"),
            sem("cq_n"), sem("cq_rot"), sem("cq_sin"), sem("cq_cos"), sem("cq_rope"))
        ck_sq, ck_ss, ck_root, ck_inv, ck_spread, ck_n, ck_rot, ck_sin, ck_cos, ck_rope = (
            sem("ck_sq"), sem("ck_ss"), sem("ck_root"), sem("ck_inv"), sem("ck_spread"),
            sem("ck_n"), sem("ck_rot"), sem("ck_sin"), sem("ck_cos"), sem("ck_rope"))
        b_gate, c_gate = sem("b_gate"), sem("c_gate")
        c_vt, c_vtok, c_s, c_max, c_exp, c_rec, c_p, c_t, c_pt, c_o, c_out = (
            sem("c_vt"), sem("c_vtok"), sem("c_s"), sem("c_max"), sem("c_exp"), sem("c_rec"), sem("c_p"),
            sem("c_t"), sem("c_pt"), sem("c_o"), sem("c_out"))

        block = ctx.enter_context(nc.Block())

        def past(eng, s, value):
            if not isinstance(value, int) or value > 0:
                eng.wait_ge(s, value)

        mod_end = {what: n + 1 for n, (kind, what, c) in enumerate(prologue()) if kind == "mod" and c == NCH - 1}

        runs = input_runs()
        turn_at = [mod_end[g] + (g < 3) for g in range(MOD0_GROUPS)]

        def evacs_a(h, t):
            return h

        def evacs_b(b, blk, t):
            return 8 + 2 * b + blk if t < 3 else 8

        def evacs_o0(i, t):
            return 16 + i if t < 3 else 8 + i

        def evacs_c(j, blk, t):
            return 24 + 3 * j + blk if t < 2 else (24 if t == 2 else 16) + 2 * j + blk

        def evacs_o1(i, t):
            return 36 + i if t < 2 else (32 if t == 2 else 24) + i

        def done_c(j, blk, t):
            return {0: 24 + 3 * j + blk, 1: 24 + 2 * j + blk, 2: 16 + 2 * j + blk}[t]

        def done_out(layer, i, t):
            return ((16, 16, 8), (36, 32, 24))[layer][t] + i

        @block.sync
        def _(sp):
            sp.dma_start(small[:, :], small_in).then_inc(consts_loaded, 16)
            sp.dma_start(mats[:, :, :], mats_in).then_inc(consts_loaded, 16)

            def load_w(n, c, width=CH):
                if isinstance(n, int) and n >= N_END:
                    return
                past(sp, w_lo_done, n - WSLOTS + 1)
                sp.dma_start(w_raw[:, c % WSLOTS, 0:width], w_all[n, :, 0:width]).then_inc(w_loaded[c % WSLOTS], 16)

            def load_m(it, c):
                ops = 2 * NCH * it + 2 * (c - 1)
                past(sp, m_lat, ops)
                past(sp, m_ctx, ops)
                sp.dma_start(m_raw[:, c % MSLOTS, :], w_mod[NCH * it + c]) \
                    .then_inc(m_loaded[c % MSLOTS], 16)

            def load_m_lat(it, c):
                sp.wait_ge(m_lat, 2 * NCH * it + 2 * (c - 1))
                if isinstance(it, int) and c < MSLOTS:
                    sp.wait_ge(m_ctx, 2 * NCH * it + 2 * (c - 1))
                sp.dma_start(m_raw[:, c % MSLOTS, :], w_mod[NCH * it + c]) \
                    .then_inc(m_loaded[c % MSLOTS], 16)

            for n in range(WSLOTS):
                load_w(n, n)
            for n in range(WSLOTS, FIRST_SQUARE + KT):
                if n % WSLOTS == 2:
                    q = n // WSLOTS - 1
                    sp.dma_start(stream[:, 4 * q:4 * q + 4, :], x_t[4 * q:4 * q + 4].rearrange("k p t -> p k t")) \
                        .then_inc(x_loaded[q], 16)
                load_w(n, n)
            with sp.Fori((FIRST_SQUARE + KT) // WSLOTS, (N_A + NCH) // WSLOTS) as i:
                for c in range(WSLOTS):
                    load_w(WSLOTS * i + c, c)
            sp.dma_start(trig[:, :, :], trig_in[0]).then_inc(trig_loaded, 16)
            for c in range(AHEAD):
                load_w(N_A + NCH + c, c)
            sp.dma_start(aux[:, :, :], dist_in).then_inc(dist_loaded, 16)

            def body_a(h):
                for c in range(NCH):
                    load_w(N_A + NCH * h + c + AHEAD, c + AHEAD)
                    load_m(h - 1, c)

            def body_b(b):
                for c in range(2 * NCH):
                    load_w(N_B + 2 * NCH * b + c + AHEAD, c + AHEAD, 768 if c + AHEAD < 2 * NCH else CH)
                    if c % 2 == 0:
                        load_m(7 + b, c // 2)

            body_a(1)
            with sp.Fori(2, A_HEADS) as h:
                body_a(h)
            body_b(0)
            with sp.Fori(1, B_HEADS) as b:
                body_b(b)
            for i, fb, kts, n0 in out_blocks():
                for c in range(len(kts) // 2):
                    load_w(N_O0 + n0 + c + AHEAD, n0 + c + AHEAD)
                    if i < 4 and n0 + c < 2 * NCH and (n0 + c) % 2 == 0:
                        load_m(11, (n0 + c) // 2)
                if i < 4:
                    if i == 0:
                        sp.wait_ge(b_dc, B_HEADS)
                        sp.wait_ge(b_di, B_HEADS)
                    else:
                        sp.wait_ge(bank_free[3], evacs_o0(i, 3))
                    sp.dma_start(aux[:, 0:4, :], x_t[4 * fb:4 * fb + 4].rearrange("k p t -> p k t")) \
                        .then_inc(xr_loaded, 16)
            sp.wait_ge(a_rope, A_HEADS)
            sp.dma_start(trig[:, :, :], trig_in[1]).then_inc(trig_loaded, 16)

            def body_c(j, first=False):
                for c in range(3 * NCH):
                    load_w(N_C + 3 * NCH * j + c + AHEAD, c + AHEAD,
                           CH // 2 if 2 * NCH <= c + AHEAD < 3 * NCH else CH)
                    if first and c >= NCH and c % 2 == 0:
                        load_m_lat(12 + j, (c - NCH) // 2)
                    elif not first and c % 3 == 0:
                        load_m_lat(12 + j, c // 3)

            body_c(0, True)
            with sp.Fori(1, C_KV) as j:
                body_c(j)
            with sp.Fori(0, 7) as i:
                for c in range(AHEAD, WSLOTS + AHEAD):
                    load_w(N_O1 + WSLOTS * i + c, c)
            load_w(N_END - 1, 3)
            for q in range(4):
                sp.wait_ge(out_ready, 4 * (q + 1))
                sp.dma_start(out[4 * q:4 * q + 4].rearrange("k p t -> p k t"), stream[:, 4 * q:4 * q + 4, 0:SEQ]) \
                    .then_inc(out_stored, 16)
            sp.wait_ge(out_stored, 64)

        @block.tensor
        def _(pe):
            mm, tp = pe.matmul, pe.transpose

            pe.wait_ge(setup_v, 1)
            pe.wait_ge(consts_loaded, 32)
            mm(sc[:, 0:2], ones[0:64, :], stat[0:64, R_PROD:R_PROD + 2], start=True, stop=True).then_inc(setup_p, 1)

            def mod_rows(g, c, n):
                if c == 0:
                    if g == 0:
                        pe.wait_ge(s_ready, 2)
                    past(pe, row_copied, g - 1)
                pe.wait_ge(w_lo_done, n + 1)
                slot = n % WSLOTS
                for k2 in range(2):
                    k = 2 * c + k2
                    for part in (w_hi, w_lo):
                        last = mm((tr, sa)[g % 2][:, :], s_parts[:, 4 * k:4 * k + P],
                                  part[:, slot, 512 * k2:512 * k2 + 512], start=(k == 0 and part is w_hi),
                                  stop=(k == KT - 1 and part is w_lo))
                last.then_inc(w_used, 1)

            def spread_rows(g):
                pe.wait_ge(row_copied, g + 1)
                past(pe, mod0_read, g)
                for f in range(4):
                    last = mm(ov[:, 2 * f:2 * f + 2], m_acc[0:4, g % 2, P * f:P * f + P], small[0:4, S_SEL:S_SEL + 2],
                              start=True, stop=True)
                last.then_inc(row_spread, 1)

            def project(n0, kt, ntiles, ncols, free_count, act_base=None, kts=range(KT), slot0=0):
                c, k2 = (kt - kts[0]) // 2, kt % 2
                slot, width = (slot0 + c) % WSLOTS, P * ntiles
                if k2 == 0:
                    pe.wait_ge(w_lo_done, n0 + c + 1)
                if act_base is not None:
                    pe.wait_ge(act_lo_done, act_base + kt + 1)
                for t in range(ntiles):
                    if kt == kts[0]:
                        past(pe, bank_free[t], free_count(t))
                    cols = slice(k2 * width + P * t, k2 * width + P * t + P)
                    acc = pj[:, t, 0:ncols]
                    wh, wl = w_hi[:, slot, cols], w_lo[:, slot, cols]
                    mm(acc, wh, act_hi[:, kt, 0:ncols], start=(kt == kts[0]), stop=False)
                    mm(acc, wh, act_lo[:, kt, 0:ncols], start=False, stop=False)
                    last = mm(acc, wl, act_hi[:, kt, 0:ncols], start=False, stop=(kt == kts[-1]))
                    if kt == kts[-1] and t < ntiles - 1:
                        last.then_inc(proj_done[t], 1)
                if k2 == 1:
                    last.then_inc(w_used, 1)

            def token_sums(dst, tiles):
                for i, parts in enumerate(tiles):
                    for n, part in enumerate(parts):
                        last = mm(dst[:, i:i + 1], part, ones[:, 0:1], start=(n == 0), stop=(n == len(parts) - 1))
                return last

            def spread(banks, n):
                for i in range(n):
                    last = tp(banks[i // 4][:, P * (i % 4):P * (i % 4) + P],
                              st(R_RMS + i).to_broadcast([P, P]), ident)
                return last

            def sum_mod(it):
                pe.wait_ge(m_lat, 2 * NCH * (it + 1))
                pe.wait_ge(m_ctx, 2 * NCH * (it + 1))
                for v in range(2):
                    for f in range(4):
                        last = mm(sa[:, 4 * v + f:4 * v + f + 1], m_acc[:, v, P * f:P * f + P], ones[:, 0:1],
                                  start=True, stop=True)
                last.then_inc(m_sum, 1)

            def sum_mod_lat(it):
                pe.wait_ge(m_lat, 2 * NCH * (it + 1))
                for f in range(4):
                    last = mm(sa[:, f:f + 1], m_acc[:, 0, P * f:P * f + P], ones[:, 0:1], start=True, stop=True)
                last.then_inc(m_sum, 1)

            def attend_a(a, s):
                if s == 0:
                    if isinstance(a, int) and a == 0:
                        pe.wait_ge(row_copied, MOD0_GROUPS)
                        pe.wait_ge(mod0_read, MOD0_GROUPS)
                        pe.wait_ge(ss_inv, 1)
                    pe.wait_ge(bank_free[0], a + 1)
                    pe.wait_ge(bank_free[1], a + 1)
                    pe.wait_ge(bank_free[2], a + 1)
                    past(pe, a_y, a)
                    for i in range(2):
                        last = mm(tr[:, 256 * i:256 * i + 256], rot_a, qk[:, i, 0:SEQ], start=True, stop=True)
                    last.then_inc(a_rot, 1)
                    past(pe, a_out, a)
                    for i in range(4):
                        last = tp(ov[:, P * i:P * i + P], kv[:, 0, P * i:P * i + P], ident)
                    last.then_inc(a_vt, 1)
                if s == 1 and not (isinstance(a, int) and a == 0):
                    pe.wait_ge(a_exp, 8 * a)
                    sum_mod(a - 1)
                if s in (2, 4, 6, 8) and s >= 6:
                    transposes_a(a, (s - 6) // 2)
                if s in (2, 4, 6, 8):
                    q = (s - 2) // 2
                    if q == 0:
                        pe.wait_ge(a_rope, a + 1)
                        past(pe, m_out, a)
                    else:
                        pe.wait_ge(a_exp, 8 * a + 2 * q)
                    keys = slice(0, T) if q < 2 else slice(SEQ, T)
                    nk = T if q < 2 else CTX
                    for m, bank in enumerate((sa, sc)):
                        rows = slice(64 * m, 64 * m + 64)
                        mm(bank[:, 0:nk], qk[rows, 0, P * q:P * q + P], qk[rows, 1, keys], start=True, stop=True) \
                            .then_inc(a_s, 1)
                if s == 10:
                    transposes_a(a, 2)
                    pe.wait_ge(a_vtok, a + 1)
                    pe.wait_ge(a_pt, 4 * a + 2)
                    for i in range(4):
                        last = mm(ov[:, 0:SEQ], v_tok[:, i, 0:P], pt[:, 0, i, :], start=(i == 0), stop=(i == 3))
                    last.then_inc(a_o, 1)
                if s == 12:
                    transposes_a(a, 3)
                if s == 13:
                    pe.wait_ge(a_pt, 4 * a + 4)
                    for i in range(2):
                        last = mm(ov[:, SEQ:T], v_tok[:, 2 + i, 0:P], pt[:, 1, i, :], start=(i == 0), stop=(i == 1))
                    last.then_inc(a_o, 1)
                if s == 14:
                    pe.wait_ge(a_sq, a + 1)
                    pe.wait_ge(a_exp, 8 * a + 8)
                    token_sums(sc, [[tmp_r[:, 0, P * i:P * i + P]] for i in range(4)]).then_inc(a_ss, 1)
                if s == 15:
                    pe.wait_ge(a_inv, a + 1)
                    pe.wait_ge(a_pt, 4 * a + 4)
                    spread([tr], 4).then_inc(a_spread, 1)

            def transposes_a(a, q):
                pe.wait_ge(a_p, 4 * a + q + 1)
                past(pe, a_pt, 4 * a + q)
                for i in range(4 if q < 2 else 2):
                    last = tp(tr[:, P * i:P * i + P], prob[:, 2, P * i:P * i + P], ident)
                last.then_inc(a_t, 1)

            def retain_b(b, s):
                if s == 0:
                    if isinstance(b, int) and b == 0:
                        pe.wait_ge(a_exp, 8 * A_HEADS)
                    past(pe, b_xc, 2 * b)
                    sum_mod(7 + b)
                    pe.wait_ge(bank_free[0], 8 + 2 * b + 2)
                    pe.wait_ge(bank_free[1], 8 + 2 * b + 1)
                    pe.wait_ge(bank_free[2], 8 + 2 * b + 1)
                    if isinstance(b, int) and b == 0:
                        pe.wait_ge(a_out, A_HEADS)
                    past(pe, b_ocopy, 2 * b)
                    for e, bank in enumerate((tr, ov)):
                        for i in range(4):
                            last = tp(bank[:, P * i:P * i + P], kv[:, e, P * i:P * i + P], ident)
                        last.then_inc(b_vt, 1)
                if s == 1:
                    pe.wait_ge(m_out, 8 + b)
                    for i in range(2):
                        last = mm(sa[:, 256 * i:256 * i + 256], qk[:, 1, P * i:P * i + P], qk[:, 0, 0:SEQ],
                                  start=True, stop=True)
                    last.then_inc(b_s, 1)
                if s == 2:
                    past(pe, b_y, 2 * b)
                    if isinstance(b, int) and b == 0:
                        pe.wait_ge(a_exp, 8 * A_HEADS)
                    for i in range(2):
                        last = mm(sc[:, 256 * i:256 * i + 256], qk[:, 1, SEQ + P * i:SEQ + P * i + P],
                                  qk[:, 0, 0:SEQ], start=True, stop=True)
                    last.then_inc(b_s, 1)
                if s == 6:
                    pe.wait_ge(b_pt, 3 * b + 1)
                    for i in range(2):
                        last = mm(sa[:, 256 * i:256 * i + 256], qk[:, 1, SEQ + P * i:SEQ + P * i + P],
                                  qk[:, 0, SEQ:T], start=True, stop=True)
                    last.then_inc(b_s, 1)
                if s == 9:
                    pe.wait_ge(b_pt, 3 * b + 3)
                    pe.wait_ge(b_vtok, 2 * b + 2)
                    for e, bank in enumerate((tr, ov)):
                        ecols = slice(P * e, P * e + P)
                        for i in range(4):
                            mm(bank[:, 0:SEQ], v_tok[:, i, ecols], pt[:, i // 4, i % 4, :], start=(i == 0),
                               stop=(i == 3))
                        for i in range(2):
                            last = mm(bank[:, SEQ:T], v_tok[:, 2 + i, ecols], pt[:, 1, i, :], start=(i == 0),
                                      stop=(i == 1))
                        last.then_inc(b_o, 1)
                if s == 12:
                    pe.wait_ge(b_ocopy, 2 * b + 2)
                    pe.wait_ge(b_pt, 3 * b + 3)
                    for e in range(2):
                        last = mm(sa[:, :], ones, tmp_o[:, e, :], start=(e == 0), stop=(e == 1))
                    last.then_inc(b_mean, 1)
                if s == 16:
                    pe.wait_ge(b_sq, 2 * b + 2)
                    token_sums(sc, [[tmp_r[:, e, P * i:P * i + P] for e in range(2)] for i in range(4)]) \
                        .then_inc(b_var, 1)
                if s == 18:
                    pe.wait_ge(b_inv, b + 1)
                    spread([sc], 4).then_inc(b_spread, 1)

            def norm_q_c(j, s):
                if s == 35:
                    pe.wait_ge(cq_sq, 2 * j + 2)
                    past(pe, c_exp, 8 * j)
                    token_sums(sa, [[tmp_o[:, i // 4, P * (i % 4):P * (i % 4) + P]] for i in range(8)]) \
                        .then_inc(cq_ss, 1)
                if s == 38:
                    pe.wait_ge(cq_inv, j + 1)
                    spread([sa, sc], 8).then_inc(cq_spread, 1)
                if s == 41:
                    pe.wait_ge(cq_n, 2 * j + 2)
                    for i, bank in enumerate((sa, sc)):
                        mm(bank[:, :], rot_c, qk[:, i, :], start=True, stop=True).then_inc(cq_rot, 1)

            def attend_c(j, s):
                if s == 0:
                    pe.wait_ge(cq_sin, 2 * j + 2)
                    sum_mod_lat(12 + j)
                if s == 1:
                    pe.wait_ge(ck_sq, j + 1)
                    pe.wait_ge(m_out, 13 + j)
                    token_sums(sa, [[tmp_o[:, 0, P * i:P * i + P]] for i in range(4)]).then_inc(ck_ss, 1)
                    past(pe, c_out, 4 * j)
                    for i in range(4):
                        last = tp(ov[:, P * i:P * i + P], kv[:, 1, P * i:P * i + P], ident)
                    last.then_inc(c_vt, 1)
                if s == 3:
                    pe.wait_ge(ck_inv, j + 1)
                    spread([sa], 4).then_inc(ck_spread, 1)
                if s == 6:
                    pe.wait_ge(ck_n, j + 1)
                    mm(sc[:, 0:SEQ], rot_c, kv[:, 0, 0:SEQ], start=True, stop=True).then_inc(ck_rot, 1)
                if s >= 11 and (s - 11) % 2 == 0 and (s - 11) // 2 < 8:
                    u = (s - 11) // 2
                    pe.wait_ge(c_p, 8 * j + u + 1)
                    past(pe, c_pt, 8 * j + u)
                    for i in range(4):
                        last = tp(tr[:, P * i:P * i + P], prob[:, u % 2, P * i:P * i + P], ident)
                    last.then_inc(c_t, 1)
                if s >= 8 and s % 2 == 0 and (s - 8) // 2 < 8:
                    u = (s - 8) // 2
                    g, q = u // 2, u % 2
                    if u == 0:
                        pe.wait_ge(ck_rope, j + 1)
                        pe.wait_ge(cq_rope, j + 1)
                        pe.wait_ge(ck_n, j + 1)
                    if u >= 2:
                        pe.wait_ge(c_exp, 8 * j + u - 1)
                    bank = (sa, sc)[u % 2]
                    qcol = 256 * (g % 2) + P * q
                    mm(bank[:, :], qk[:, g // 2, qcol:qcol + P], kv[:, 0, :], start=True, stop=True) \
                        .then_inc(c_s, 1)
                if s >= 14 and (s - 14) % 4 == 0 and (s - 14) // 4 < 4:
                    g = (s - 14) // 4
                    pe.wait_ge(c_pt, 8 * j + 2 * g + 2)
                    if g == 0:
                        pe.wait_ge(c_vtok, j + 1)
                    past(pe, c_out, 4 * j + g)
                    for i in range(4):
                        last = mm(ov[:, 0:SEQ], v_tok[:, i, 0:P], pt[:, g % 2, i, :], start=(i == 0), stop=(i == 3))
                    last.then_inc(c_o, 1)

            def spread_inverse(i, n):
                token_sums(sc, [[prob[:, 1, P * t:P * t + P]] for t in range(n // P)]).then_inc(ss_sum, 1)
                pe.wait_ge(ss_rec, i + 1)
                spread([sc], n // P).then_inc(ss_spread, 1)

            for n, (kind, what, c) in enumerate(prologue()):
                if kind == "mod":
                    mod_rows(what, c, n)
                else:
                    for kt in (2 * c, 2 * c + 1):
                        project(n - c, kt, 4, T, lambda t: 0, 0, slot0=n - c)
                for g in range(MOD0_GROUPS):
                    if n == turn_at[g]:
                        spread_rows(g)
                if n == FIRST_SQUARE + KT + 1:
                    pe.wait_ge(setup_a, 2)
                    pe.wait_ge(ss_add, KT)
                    token_sums(sc, [[prob[:, 1, P * t:P * t + P]] for t in range(4)]).then_inc(ss_sum, 1)
                if n == FIRST_SQUARE + KT + 2:
                    pe.wait_ge(ss_rec, 1)
                    spread([sc], 4).then_inc(ss_spread, 1)

            def body_a(h, a):
                for kt in range(KT):
                    project(N_A + NCH * h, kt, 4, T, lambda t: evacs_a(h, t))
                    attend_a(a, kt)

            body_a(1, 0)
            with pe.Fori(2, A_HEADS) as h:
                body_a(h, h - 1)

            def body_b(b, first=False):
                for s in range(2 * KT):
                    blk, kt = s // KT, s % KT
                    project(N_B + 2 * NCH * b + NCH * blk, kt, 3, T, lambda t: evacs_b(b, blk, t))
                    if not first:
                        retain_b(b - 1, s)
                    elif s < KT:
                        attend_a(A_HEADS - 1, s)

            body_b(0, True)
            body_b(1)
            with pe.Fori(2, B_HEADS) as b:
                body_b(b)

            for i, fb, kts, n0 in out_blocks():
                for kt in kts:
                    project(N_O0 + n0, kt, 4, T, lambda t: evacs_o0(i, t), KT if i in (0, 4) else None, kts, n0)
                    if i < 4:
                        retain_b(B_HEADS - 1, EARLY * i + kt)
                if i == 3:
                    pe.wait_ge(b_xc, 2 * B_HEADS)
                    sum_mod(11)
            pe.wait_ge(m_out, 12)
            pe.wait_ge(ss_add, 2 * KT)
            pe.wait_ge(b_y, 2 * B_HEADS)
            spread_inverse(1, T)

            def body_c(j, first=False):
                for s in range(3 * KT):
                    blk, kt = s // KT, s % KT
                    n0 = N_C + 3 * NCH * j + NCH * blk
                    project(n0, kt, 4 if blk < 2 else 2, SEQ if blk < 2 else T, lambda t: evacs_c(j, blk, t),
                            2 * KT if first and blk == 0 else None)
                    if not first:
                        attend_c(j - 1, s)
                    norm_q_c(j, s)

            body_c(0, True)
            body_c(1)
            with pe.Fori(2, C_KV) as j:
                body_c(j)
            for i, fb, kts, n0 in out_blocks():
                for kt in kts:
                    project(N_O1 + n0, kt, 4, SEQ, lambda t: evacs_o1(i, t), 3 * KT if i in (0, 4) else None, kts,
                            n0)
                    if i < 4:
                        attend_c(C_KV - 1, EARLY * i + kt)
            pe.wait_ge(ss_add, 3 * KT)
            spread_inverse(2, SEQ)

        @block.scalar
        def _(act):
            f = act.activation
            act.wait_ge(consts_loaded, 32)
            f(st(R_S, 32), sm(S_C, 32), ACT.Silu).then_inc(s_whole, 1)
            act.wait_ge(s_whole, 1)
            act.wait_ge(zeroed, 2)
            f(vector_parts[:, :, 0:2], st(R_S, 32).rearrange("p (k v) -> p k v", v=2), ACT.Copy).then_inc(s_ready, 1)
            act.wait_ge(setup_p, 1)
            f(st(R_EXP2, 2), sc[:, 0:2], ACT.Exp).then_inc(setup_a, 1)
            f(st(R_LG, 8), sm(S_DECAY, 8), ACT.Exp).then_inc(setup_a, 1)

            def root_of_mean(i, n):
                act.wait_ge(ss_sum, i + 1)
                act.wait_ge(setup_v, 2)
                f(st(R_RMS, n // P), sc[:, 0:n // P], ACT.Sqrt, bias=st(R_EPS), scale=1.0 / D_MODEL) \
                    .then_inc(ss_root, 1)

            def keep_inverse(i):
                act.wait_ge(ss_spread, i + 1)
                f(prob[:, 2, :], sc[:, :], ACT.Copy).then_inc(ss_inv, 1)

            def split_hi(n, c, width=CH):
                past(act, w_used, n - WSLOTS + 1)
                act.wait_ge(w_loaded[c % WSLOTS], loads(n, c))
                f(w_hi[:, c % WSLOTS, 0:width], w_raw[:, c % WSLOTS, 0:width], ACT.Copy).then_inc(w_hi_done, 1)

            def loads(n, c):
                return (n - c % WSLOTS) * (16 // WSLOTS) + 16

            def act_split(i, k, full):
                f(act_hi[:, k, 0:full.shape[-1]], full, ACT.Copy).then_inc(act_hi_done, 1)

            def h_half(layer, k):
                i = KT * layer + k
                c_scale, c_shift = ((M_SCALE0, M_SHIFT0), (M_SCALE1, M_SHIFT1))[layer]
                act.wait_ge(h_norm, i + 1)
                act.wait_ge(scale_ready, 2 * (k // 4 + 1) if layer == 0 else 2 * PAIRS + 2)
                past(act, act_lo_done, 2 * KT * layer + k - depth + 1)
                f(modulated[k % depth][:, SEQ:T], normed[k % depth][:, SEQ:T], ACT.Identity,
                  bias=modv[:, 1, c_shift + k:c_shift + k + 1], scale=modv[:, 1, c_scale + k:c_scale + k + 1]) \
                    .then_inc(h_ctx, 1)

            def h_step(layer, k, first, last):
                if k == first:
                    h_half(layer, k)
                if k < last:
                    h_half(layer, k + 1)
                act.wait_ge(h_ctx, KT * layer + k + 1)
                act.wait_ge(h_lat, KT * layer + k + 1)
                act_split(layer, k, modulated[k % depth])

            def attend_a(a, s):
                if s == 0:
                    act.wait_ge(a_vt, a + 1)
                    f(v_tok[:, :, 0:P], ov[:, :].rearrange("p (i d) -> p i d", i=4), ACT.Copy).then_inc(a_vtok, 1)
                if s in (6, 8, 10, 12):
                    q = (s - 6) // 2
                    act.wait_ge(a_t, 4 * a + q + 1)
                    n = 4 if q < 2 else 2
                    f(pt[:, q // 2, 0:n, P * (q % 2):P * (q % 2) + P],
                      tr[:, 0:P * n].rearrange("p (i d) -> p i d", i=n), ACT.Copy).then_inc(a_pt, 1)
                if s in (2, 4, 6, 8):
                    q = (s - 2) // 2
                    nk = T if q < 2 else CTX
                    past(act, a_p, 4 * a + q)
                    for m, bank in enumerate((sa, sc)):
                        act.wait_ge(a_max, 8 * a + 2 * q + m + 1)
                        f(prob[:, m, 0:nk], bank[:, 0:nk], ACT.Exp, bias=st(R_NEG + m), accum_out=st(R_SUM + m)) \
                            .then_inc(a_exp, 1)
                if s == 13:
                    act.wait_ge(a_o, 2 * a + 2)
                    past(act, a_y, a)
                    f(tmp_r[:, 0, :], ov[:, :], ACT.Square).then_inc(a_sq, 1)
                if s == 14:
                    act.wait_ge(a_ss, a + 1)
                    f(st(R_RMS, 4), sc[:, 0:4], ACT.Sqrt, bias=st(R_EPS), scale=1.0 / (2 * A_DIM)) \
                        .then_inc(a_root, 1)

            def retain_b(b, s):
                if s == 0:
                    past(act, b_pt, 3 * b)
                    past(act, b_y, 2 * b)
                    if isinstance(b, int) and b == 0:
                        act.wait_ge(a_t, 4 * A_HEADS)
                        act.wait_ge(a_out, A_HEADS)
                    f(prob[:, 1, :], aux[:, 3, :], ACT.Exp, scale=stat[:, lg_col(b, 0)]).then_inc(b_expc, 1)
                    f(tmp_r[:, 1, :], aux[:, 4, :], ACT.Exp, scale=stat[:, lg_col(b, 1)]).then_inc(b_expc, 1)
                    act.wait_ge(b_arg, b + 1)
                    f(prob[:, 0, :], tmp_r[:, 0, :], ACT.Exp).then_inc(b_expi, 1)
                    for e, bank in enumerate((tr, ov)):
                        act.wait_ge(b_vt, 2 * b + e + 1)
                        f(v_tok[:, :, P * e:P * e + P], bank[:, :].rearrange("p (i d) -> p i d", i=4), ACT.Copy) \
                            .then_inc(b_vtok, 1)
                if s == 4:
                    gates = stream[:, bass.ds(2 * b + 8, 2), :]
                    act.wait_ge(bank_free[1], 8 + 2 * b + 2)
                    act.wait_ge(bank_free[2], 8 + 2 * b + 2)
                    f(gates, gates, ACT.Silu).then_inc(b_gate, 1)
                if s == 9:
                    for e, bank in enumerate((tr, ov)):
                        act.wait_ge(b_o, 2 * b + e + 1)
                        f(tmp_o[:, e, :], bank[:, :], ACT.Copy).then_inc(b_ocopy, 1)
                if s == 13:
                    for e in range(2):
                        act.wait_ge(b_xc, 2 * b + e + 1)
                        f(tmp_r[:, e, :], tmp_o[:, e, :], ACT.Square).then_inc(b_sq, 1)
                if s == 16:
                    act.wait_ge(b_var, b + 1)
                    f(st(R_RMS, 4), sc[:, 0:4], ACT.Sqrt, bias=st(R_EPS), scale=1.0 / (2 * B_DIM)) \
                        .then_inc(b_root, 1)

            def lg_col(b, direction):
                return bass.ds(R_LG + 4 * direction + b, 1)

            def norm_q_c(j, s):
                if s == 32:
                    for i in range(2):
                        act.wait_ge(bank_free[1 + 2 * i], evacs_c(j, 1, 1 + 2 * i) + 1)
                        act.wait_ge(bank_free[2 * i], evacs_c(j, 1, 2 * i) + 1)
                        if i == 0:
                            past(act, ck_sin, j)
                        f(tmp_o[:, i, :], qk[:, i, :], ACT.Square).then_inc(cq_sq, 1)
                if s == 35:
                    act.wait_ge(cq_ss, j + 1)
                    f(st(R_RMS, 8), sa[:, 0:8], ACT.Sqrt, bias=st(R_EPS), scale=1.0 / C_DIM).then_inc(cq_root, 1)

            def attend_c(j, s):
                if s == 0:
                    act.wait_ge(bank_free[0], evacs_c(j, 2, 0) + 1)
                    act.wait_ge(cq_rope, j + 1)
                    f(tmp_o[:, 0, :], kv[:, 0, :], ACT.Square).then_inc(ck_sq, 1)
                if s == 1:
                    act.wait_ge(ck_ss, j + 1)
                    f(st(R_RMS, 4), sa[:, 0:4], ACT.Sqrt, bias=st(R_EPS), scale=1.0 / C_DIM).then_inc(ck_root, 1)
                    act.wait_ge(c_vt, j + 1)
                    f(v_tok[:, :, 0:P], ov[:, :].rearrange("p (i d) -> p i d", i=4), ACT.Copy).then_inc(c_vtok, 1)
                if s >= 11 and (s - 11) % 2 == 0 and (s - 11) // 2 < 8:
                    u = (s - 11) // 2
                    g, q = u // 2, u % 2
                    act.wait_ge(c_t, 8 * j + u + 1)
                    past(act, c_o, 4 * j + max(g - 1, 0))
                    f(pt[:, g % 2, :, P * q:P * q + P], tr[:, :].rearrange("p (i d) -> p i d", i=4), ACT.Copy) \
                        .then_inc(c_pt, 1)
                if s >= 8 and s % 2 == 0 and (s - 8) // 2 < 8:
                    u = (s - 8) // 2
                    act.wait_ge(c_max, 8 * j + u + 1)
                    past(act, c_t, 8 * j + max(u - 1, 0))
                    f(prob[:, u % 2, :], (sa, sc)[u % 2][:, :], ACT.Exp, bias=st(R_NEG + u % 2),
                      accum_out=st(R_SUM + u % 2)).then_inc(c_exp, 1)

            def evac_a(h):
                act.wait_ge(proj_done[1], h + 1)
                past(act, a_s, 8 * h)
                f(qk[:, 1, :], pj[:, 1, :], ACT.Copy).then_inc(bank_free[1], 1)
                act.wait_ge(w_used, N_A + NCH * (h + 1))
                f(stream[:, bass.ds(h, 1), :], pj[:, 3:4, :], ACT.Silu).then_inc(bank_free[3], 1)

            for n in range(AHEAD):
                split_hi(n, n)
            for n, (kind, what, c) in enumerate(prologue()):
                split_hi(n + AHEAD, n + AHEAD)
                k = n - FIRST_SQUARE
                if 0 <= k < KT:
                    act.wait_ge(x_loaded[k // 4], 16)
                    past(act, ss_add, k - depth + 1)
                    f(normed[k % depth], stream[:, k, :], ACT.Square).then_inc(ss_sq, 1)
                if n == FIRST_SQUARE + KT + 1:
                    root_of_mean(0, T)
                if n == FIRST_SQUARE + KT + 2:
                    keep_inverse(0)
                if n in runs:
                    first, last = runs[n]
                    for k in range(first, last + 1):
                        h_step(0, k, first, last)
            evac_a(0)

            def body_a(h, a):
                n0 = N_A + NCH * h
                for kt in range(KT):
                    if kt % 2 == 0:
                        split_hi(n0 + kt // 2 + AHEAD, kt // 2 + AHEAD)
                    if kt == KT - 1:
                        evac_a(h)
                    attend_a(a, kt)

            body_a(1, 0)
            with act.Fori(2, A_HEADS) as h:
                body_a(h, h - 1)

            def body_b(b, first=False):
                n0 = N_B + 2 * NCH * b
                for s in range(2 * KT):
                    if s % 2 == 0:
                        c = s // 2 + AHEAD
                        split_hi(n0 + c, c, 768 if c < 2 * NCH else CH)
                    if s == KT - 1:
                        act.wait_ge(proj_done[1], 8 + 2 * b + 1)
                        if first:
                            act.wait_ge(a_s, 8 * A_HEADS)
                        else:
                            act.wait_ge(b_s, 3 * b)
                        f(qk[:, 1, :], pj[:, 1, :], ACT.Copy, scale=B_DIM ** -0.5).then_inc(bank_free[1], 1)
                    if s == 2 * KT - 1:
                        act.wait_ge(proj_done[1], 8 + 2 * b + 2)
                        f(stream[:, bass.ds(2 * b + 8, 1), :], pj[:, 1:2, :], ACT.Copy).then_inc(bank_free[1], 1)
                        act.wait_ge(w_used, n0 + 2 * NCH)
                        f(stream[:, bass.ds(2 * b + 9, 1), :], pj[:, 2:3, :], ACT.Copy).then_inc(bank_free[2], 1)
                    if not first:
                        retain_b(b - 1, s)
                    elif s < KT:
                        attend_a(A_HEADS - 1, s)

            body_b(0, True)
            body_b(1)
            with act.Fori(2, B_HEADS) as b:
                body_b(b)

            def squares(i, fb, tiles, n):
                for t in range(4):
                    if i == 1:
                        act.wait_ge(x1_lat, 4 * (4 + fb) + t + 1)
                    act.wait_ge(bank_free[t], (evacs_o0, evacs_o1)[i - 1](4 + fb, t) + 1)
                    act.wait_ge(ss_add, tiles + t - 1)
                    f(tmp_r[:, t % 2:t % 2 + 1, 0:n], tiles_of(tiles - KT * i, t, n), ACT.Square).then_inc(ss_sq, 1)

            def tiles_of(first, t, n):
                return stream[:, bass.ds(first + t, 1), 0:n]

            def o_hi(i, k, n_last):
                act.wait_ge(w_used, n_last + k // 2 + 1)
                if i == 1:
                    act.wait_ge(*((a_out, k + 1) if k < A_HEADS else (b_out, k - A_HEADS + 1)))
                    act_split(i, k, stream[:, k, :])
                else:
                    act.wait_ge(c_out, k + 1)
                    act_split(i, k, stream[:, k, SEQ:T])

            for k in range(4):
                o_hi(1, k, N_O0 - NCH)
            for i, fb, kts, n0 in out_blocks():
                for kt in kts:
                    if kt % 2 == 0:
                        c = n0 + (kt - kts[0]) // 2 + AHEAD
                        split_hi(N_O0 + c, c)
                    if i == 0 and kt + 4 < EARLY:
                        o_hi(1, kt + 4, N_O0 - NCH)
                    if i == 3 and kt >= EARLY - 4:
                        o_hi(1, kt + 4, N_O0 - NCH)
                    if i < 4:
                        retain_b(B_HEADS - 1, EARLY * i + kt)
                if i >= 4:
                    squares(1, fb, KT + 4 * fb, T)
            root_of_mean(1, T)
            keep_inverse(1)
            for k in range(4):
                h_step(1, k, 0, KT - 1)

            def body_c(j, first=False):
                n0 = N_C + 3 * NCH * j
                for s in range(3 * KT):
                    if first and s + 4 < KT:
                        h_step(1, s + 4, 0, KT - 1)
                    if s % 2 == 0:
                        c = s // 2 + AHEAD
                        split_hi(n0 + c, c, CH // 2 if 2 * NCH <= c < 3 * NCH else CH)
                    if s == KT - 1:
                        for t in (1, 3):
                            if t < 3:
                                act.wait_ge(proj_done[t], done_c(j, 0, t) + 1)
                            else:
                                act.wait_ge(w_used, n0 + NCH)
                            f(stream[:, bass.ds(4 * j + t, 1), SEQ:T], pj[:, t:t + 1, 0:SEQ], ACT.Copy) \
                                .then_inc(bank_free[t], 1)
                    if s == KT + 4:
                        for t in range(4):
                            act.wait_ge(bank_free[t], evacs_c(j, 0, t) + 1)
                        gates = stream[:, bass.ds(4 * j, 4), SEQ:T]
                        f(gates, gates, ACT.Silu).then_inc(c_gate, 1)
                    if s == 2 * KT - 1:
                        for t in (1, 3):
                            if t < 3:
                                act.wait_ge(proj_done[t], done_c(j, 1, t) + 1)
                            else:
                                act.wait_ge(w_used, n0 + 2 * NCH)
                            past(act, c_s, 8 * j)
                            f(qk[:, t // 2, SEQ * (t % 2):SEQ * (t % 2) + SEQ], pj[:, t, 0:SEQ], ACT.Copy) \
                                .then_inc(bank_free[t], 1)
                    if s == 3 * KT - 1:
                        act.wait_ge(w_used, n0 + 3 * NCH)
                        past(act, c_vt, j)
                        f(kv[:, 1, :], pj[:, 1, :], ACT.Copy).then_inc(bank_free[1], 1)
                    if not first:
                        attend_c(j - 1, s)
                    norm_q_c(j, s)

            body_c(0, True)
            body_c(1)
            with act.Fori(2, C_KV) as j:
                body_c(j)

            for k in range(4):
                o_hi(3, k, N_O1 - NCH)
            for i, fb, kts, n0 in out_blocks():
                for kt in kts:
                    if kt % 2 == 0 and n0 + (kt - kts[0]) // 2 + AHEAD < 4 * NCH:
                        c = n0 + (kt - kts[0]) // 2 + AHEAD
                        split_hi(N_O1 + c, c)
                    if i == 0 and kt + 4 < EARLY:
                        o_hi(3, kt + 4, N_O1 - NCH)
                    if i == 3 and kt >= EARLY - 4:
                        o_hi(3, kt + 4, N_O1 - NCH)
                    if i < 4:
                        attend_c(C_KV - 1, EARLY * i + kt)
                if i >= 4:
                    squares(2, fb, 2 * KT + 4 * fb, SEQ)
            root_of_mean(2, SEQ)

        @block.gpsimd
        def _(pool):
            pool.wait_ge(zeroed, 1)
            for k in range(KT):
                pool.wait_ge(ss_sq, k + 1)
                past(pool, ss_add, k)
                pool.tensor_tensor(prob[:, 1, :], prob[:, 1, :], normed[k % depth], ALU.add).then_inc(ss_add, 1)
            for layer in range(2):
                pool.wait_ge(ss_inv, layer + 1)
                for k in range(KT):
                    i = KT * layer + k
                    past(pool, h_lat, i - depth + 1)
                    past(pool, h_ctx, i - depth + 1)
                    pool.tensor_tensor(normed[k % depth], stream[:, k, :], prob[:, 2, :], ALU.mult) \
                        .then_inc(h_norm, 1)

        @block.vector
        def _(ve):
            def tt(out_, a, b, op):
                return ve.tensor_tensor(out_, a, b, op)

            ve.memset(st(R_EPS), EPS)
            ve.memset(prob[:, 1, :], 0.0).then_inc(zeroed, 1)
            ve.memset(s_parts[:, :].bitcast(F32), 0.0).then_inc(zeroed, 1)
            ve.wait_ge(consts_loaded, 32)
            tt(st(R_PROD, 1), sm(S_DL), sm(S_DL + 1), ALU.mult)
            tt(st(R_PROD + 1, 1), sm(S_DL + 2), sm(S_DL + 3), ALU.mult).then_inc(setup_v, 1)
            ve.tensor_scalar(st(R_SUB), sm(S_SUBLN), 1.0 - LAMBDA_INIT, None, ALU.mult).then_inc(setup_v, 1)
            ve.wait_ge(zeroed, 1)

            def add_square(count, k, n):
                ve.wait_ge(ss_sq, count)
                past(ve, ss_add, count - 1)
                tt(prob[:, 1, 0:n], prob[:, 1, 0:n], tmp_r[:, k % 2, 0:n], ALU.add).then_inc(ss_add, 1)

            def mod0_out(g):
                col = (M_SCALE0, M_SHIFT0)[g % 2] + 4 * (g // 2)
                ve.wait_ge(row_spread, g + 1)
                for v in range(2):
                    last = tt(modv[:, v, col:col + 4], ov[:, 0:8].rearrange("p (f v) -> p v f", v=2)[:, v, :],
                              small[:, S_B + col:S_B + col + 4], ALU.add)
                last.then_inc(mod0_read, 1)
                if g % 2 == 1:
                    col = M_SCALE0 + 4 * (g // 2)
                    ve.wait_ge(mod0_read, g + 1)
                    for v in range(2):
                        ve.scalar_tensor_tensor(modv[:, v, col:col + 4], modv[:, v, col:col + 4], 1.0,
                                                sm(S_G + 4 * (g // 2), 4), ALU.add, ALU.mult) \
                            .then_inc(scale_ready, 1)

            def copy_rows(g):
                ve.wait_ge(w_used, mod_end[g])
                past(ve, row_spread, g - 1)
                ve.tensor_copy(m_acc[0:4, g % 2, :], (tr, sa)[g % 2][0:4, :]).then_inc(row_copied, 1)

            def finish_scale(layer):
                c0 = M_SCALE1
                for v in range(2):
                    ve.scalar_tensor_tensor(modv[:, v, c0:c0 + 16], modv[:, v, c0:c0 + 16], 1.0,
                                            sm(S_G + 16 * layer, 16), ALU.add, ALU.mult).then_inc(scale_ready, 1)
                ve.wait_ge(scale_ready, 2 * PAIRS + 2)

            def split_lo(n, c, width=CH):
                ve.wait_ge(w_hi_done, n + 1)
                s = c % WSLOTS
                tt(w_lo[:, s, 0:width], w_raw[:, s, 0:width], w_hi[:, s, 0:width].bitcast(F32), ALU.subtract) \
                    .then_inc(w_lo_done, 1)

            def h_tile(layer, k):
                i = KT * layer + k
                c_scale, c_shift = ((M_SCALE0, M_SHIFT0), (M_SCALE1, M_SHIFT1))[layer]
                past(ve, act_hi_done, act_count(layer, k) - depth + 1)
                past(ve, act_lo_done, act_count(layer, k) - depth + 1)
                ve.wait_ge(h_norm, i + 1)
                if layer == 0:
                    ve.wait_ge(scale_ready, 2 * (k // 4 + 1))
                ve.tensor_scalar(modulated[k % depth][:, 0:SEQ], normed[k % depth][:, 0:SEQ],
                                 modv[:, 0, c_scale + k:c_scale + k + 1], modv[:, 0, c_shift + k:c_shift + k + 1],
                                 ALU.mult, ALU.add).then_inc(h_lat, 1)

            def act_count(layer, k):
                return 2 * KT * layer + k

            def h_lo(layer, k):
                i = act_count(layer, k)
                ve.wait_ge(act_hi_done, i + 1)
                ve.wait_ge(h_ctx, KT * layer + k + 1)
                tt(act_lo[:, k, :], modulated[k % depth], act_hi[:, k, :].bitcast(F32), ALU.subtract) \
                    .then_inc(act_lo_done, 1)

            def mod_chunk(it, c, vectors=2):
                ve.wait_ge(m_loaded[c % MSLOTS], (2 * NCH // 4) * 16 * it + 16 * (c // MSLOTS + 1))
                if c == 0:
                    past(ve, m_sum, it)
                for k2 in range(2):
                    for v in range(vectors):
                        k = 2 * c + k2
                        src, coef, acc = m_raw[:, c % MSLOTS, 512 * k2:512 * k2 + 512], st(R_S + 2 * k + v), m_acc[:, v, :]
                        if k == 0:
                            ins = ve.tensor_scalar(acc, src, coef, None, ALU.mult)
                        else:
                            ve.wait_ge((m_lat, m_ctx)[v], 2 * NCH * it + k)
                            ins = ve.scalar_tensor_tensor(acc, src, coef, acc, ALU.mult, ALU.add)
                        ins.then_inc((m_lat, m_ctx)[v], 1)

            def mod_out(it, vectors=2):
                ve.wait_ge(m_sum, it + 1)
                for v in range(vectors):
                    last = ve.tensor_tensor(modv[:, v, bass.ds(4 * it + 4 * MOD0_GROUPS, 4)], sa[:, 4 * v:4 * v + 4],
                                            small[:, bass.ds(4 * it + 4 * MOD0_GROUPS + S_B, 4)], ALU.add)
                last.then_inc(m_out, 1)

            def lat(ap):
                return ap[:, :, 0:SEQ]

            def rows(ap, n):
                return ap.unsqueeze(1).to_broadcast([P, n, SEQ])

            def h_step(layer, k, first, last):
                if k == first:
                    h_tile(layer, k)
                if k < last:
                    h_tile(layer, k + 1)
                h_lo(layer, k)

            def attend_a(a, s):
                if s == 1 and not (isinstance(a, int) and a == 0):
                    mod_out(a - 1)
                if s == 0:
                    ve.wait_ge(a_rot, a + 1)
                    past(ve, a_out, a)
                    rotated = tr[:, :].rearrange("p (i t) -> p i t", i=2)
                    held = tmp_o[:, 0, :].rearrange("p (i t) -> p i t", i=2)
                    tt(held, rotated, rows(trig[:, 1, :], 2), ALU.mult).then_inc(a_tmp, 1)
                    tt(lat(qk), lat(qk), rows(trig[:, 0, :], 2), ALU.mult).then_inc(a_cos, 1)
                    ve.wait_ge(a_tmp, a + 1)
                    ve.wait_ge(a_cos, a + 1)
                    tt(lat(qk), lat(qk), held, ALU.add).then_inc(a_rope, 1)
                if s in (4, 6, 8, 10):
                    combine_a(a, (s - 4) // 2)
                if s in (2, 4, 6, 8):
                    q = (s - 2) // 2
                    nk = T if q < 2 else CTX
                    for m, bank in enumerate((sa, sc)):
                        ve.wait_ge(a_s, 8 * a + 2 * q + m + 1)
                        ve.tensor_reduce(st(R_NEG + m), bank[:, 0:nk], AX_X, ALU.max, negate=True).then_inc(a_max, 1)
                if s == 14:
                    ve.wait_ge(a_root, a + 1)
                    ve.reciprocal(st(R_RMS, 4), st(R_RMS, 4)).then_inc(a_inv, 1)
                if s == 15:
                    ve.wait_ge(a_spread, a + 1)
                    tile = stream[:, bass.ds(a, 1), :]
                    tt(tile, tile, tr[:, :].unsqueeze(1), ALU.mult).then_inc(a_y, 1)
                    ve.wait_ge(a_y, a + 1)
                    ve.scalar_tensor_tensor(tile, ov[:, :].unsqueeze(1), st(R_SUB), tile, ALU.mult, ALU.mult) \
                        .then_inc(a_out, 1)

            def combine_a(a, q):
                nk = T if q < 2 else CTX
                n = 4 * a + q
                ve.wait_ge(a_exp, 8 * a + 2 * q + 2)
                ve.reciprocal(st(R_REC, 2), st(R_SUM, 2)).then_inc(a_rec, 1)
                ve.wait_ge(a_rec, n + 1)
                tt(st(R_C2), st(R_REC + 1), st(R_LAM), ALU.mult).then_inc(a_c2, 1)
                ve.wait_ge(a_c2, n + 1)
                ve.tensor_scalar(prob[:, 1, 0:nk], prob[:, 1, 0:nk], st(R_C2), None, ALU.mult).then_inc(a_p2, 1)
                ve.wait_ge(a_p2, n + 1)
                past(ve, a_t, n)
                ve.scalar_tensor_tensor(prob[:, 2, 0:nk], prob[:, 0, 0:nk], st(R_REC), prob[:, 1, 0:nk], ALU.mult,
                                        ALU.subtract).then_inc(a_p, 1)

            def retain_b(b, s):
                if s == 0:
                    past(ve, b_y, 2 * b)
                    ve.tensor_scalar(tmp_r[:, 0, :], aux[:, 1, :], stat[:, bass.ds(R_LG + 4 + b, 1)], None, ALU.mult) \
                        .then_inc(b_argb, 1)
                    ve.wait_ge(b_argb, b + 1)
                    ve.scalar_tensor_tensor(tmp_r[:, 0, :], aux[:, 0, :], stat[:, bass.ds(R_LG + b, 1)],
                                            tmp_r[:, 0, :], ALU.mult, ALU.add).then_inc(b_arg, 1)
                    mod_out(7 + b)
                    ve.wait_ge(b_expc, 2 * b + 2)
                    tt(prob[:, 1, :], prob[:, 1, :], tmp_r[:, 1, :], ALU.add).then_inc(b_dc, 1)
                    ve.wait_ge(b_expi, b + 1)
                    tt(prob[:, 0, :], prob[:, 0, :], aux[:, 2, :], ALU.add).then_inc(b_di, 1)
                if s in (3, 4, 7):
                    i = (3, 4, 7).index(s)
                    ve.wait_ge(b_s, 3 * b + i + 1)
                    if i == 0:
                        ve.wait_ge(b_di, b + 1)
                        ve.wait_ge(b_dc, b + 1)
                        if isinstance(b, int) and b == 0:
                            ve.wait_ge(a_o, 2 * A_HEADS)
                        past(ve, b_o, 2 * b)
                    dst = pt[:, i // 2, 2 * (i % 2):2 * (i % 2) + 2, :]
                    tt(dst, (sa, sc, sa)[i][:, :].rearrange("p (i t) -> p i t", i=2),
                       prob[:, (0, 1, 0)[i], :].rearrange("p (i t) -> p i t", i=2), ALU.mult).then_inc(b_pt, 1)
                if s == 12:
                    ve.wait_ge(b_mean, b + 1)
                    for e in range(2):
                        ve.scalar_tensor_tensor(tmp_o[:, e, :], sa[:, :], -1.0 / (2 * B_DIM), tmp_o[:, e, :],
                                                ALU.mult, ALU.add).then_inc(b_xc, 1)
                if s == 17:
                    ve.wait_ge(b_root, b + 1)
                    ve.reciprocal(st(R_RMS, 4), st(R_RMS, 4)).then_inc(b_inv, 1)
                if s == 18:
                    ve.wait_ge(b_gate, b + 1)
                    ve.wait_ge(b_spread, b + 1)
                    for e in range(2):
                        ve.scalar_tensor_tensor(tmp_r[:, e, :], tmp_o[:, e, :], small[:, bass.ds(S_GN + 2 * b + e, 1)],
                                                sc[:, :], ALU.mult, ALU.mult).then_inc(b_y, 1)
                    for e in range(2):
                        ve.wait_ge(b_y, 2 * b + e + 1)
                        tile = stream[:, bass.ds(2 * b + 8 + e, 1), :]
                        tt(tile, tile, tmp_r[:, e:e + 1, :], ALU.mult).then_inc(b_out, 1)

            def norm_q_c(j, s):
                if s == 36:
                    ve.wait_ge(cq_root, j + 1)
                    ve.reciprocal(st(R_RMS, 8), st(R_RMS, 8)).then_inc(cq_inv, 1)
                if s == 38:
                    ve.wait_ge(cq_spread, j + 1)
                    for i, bank in enumerate((sa, sc)):
                        ve.scalar_tensor_tensor(qk[:, i, :], qk[:, i, :], sm(S_QK), bank[:, :], ALU.mult, ALU.mult) \
                            .then_inc(cq_n, 1)
                if s == 41:
                    for i, bank in enumerate((sa, sc)):
                        ve.wait_ge(cq_rot, 2 * j + i + 1)
                        tt(tmp_o[:, i, :].rearrange("p (g t) -> p g t", g=2),
                           bank[:, :].rearrange("p (g t) -> p g t", g=2), rows(trig[:, 1, :], 2), ALU.mult) \
                            .then_inc(cq_sin, 1)
                    heads = qk[:, :, :].rearrange("p i (g t) -> p (i g) t", g=2)
                    tt(heads, heads, rows(trig[:, 0, :], 4), ALU.mult).then_inc(cq_cos, 1)
                    ve.wait_ge(cq_cos, j + 1)
                    ve.wait_ge(cq_sin, 2 * j + 2)
                    tt(qk[:, :, :], qk[:, :, :], tmp_o[:, :, :], ALU.add).then_inc(cq_rope, 1)

            def attend_c(j, s):
                if s == 0:
                    mod_out(12 + j, 1)
                if s == 2:
                    ve.wait_ge(ck_root, j + 1)
                    ve.reciprocal(st(R_RMS, 4), st(R_RMS, 4)).then_inc(ck_inv, 1)
                if s == 3:
                    ve.wait_ge(ck_spread, j + 1)
                    ve.scalar_tensor_tensor(kv[:, 0, :], kv[:, 0, :], sm(S_QK + 1), sa[:, :], ALU.mult,
                                            ALU.mult).then_inc(ck_n, 1)
                if s == 6:
                    ve.wait_ge(ck_rot, j + 1)
                    ve.wait_ge(ck_ss, j + 1)
                    tt(tmp_o[:, 0, 0:SEQ], sc[:, 0:SEQ], trig[:, 1, :], ALU.mult).then_inc(ck_sin, 1)
                    tt(kv[:, 0, 0:SEQ], kv[:, 0, 0:SEQ], trig[:, 0, :], ALU.mult).then_inc(ck_cos, 1)
                    ve.wait_ge(ck_sin, j + 1)
                    ve.wait_ge(ck_cos, j + 1)
                    tt(kv[:, 0, 0:SEQ], kv[:, 0, 0:SEQ], tmp_o[:, 0, 0:SEQ], ALU.add).then_inc(ck_rope, 1)
                if s >= 9 and (s - 9) % 2 == 0 and (s - 9) // 2 < 8:
                    u = (s - 9) // 2
                    ve.wait_ge(c_exp, 8 * j + u + 1)
                    ve.reciprocal(st(R_REC + u % 2), st(R_SUM + u % 2)).then_inc(c_rec, 1)
                    ve.wait_ge(c_rec, 8 * j + u + 1)
                    ve.tensor_scalar(prob[:, u % 2, :], prob[:, u % 2, :], st(R_REC + u % 2), None, ALU.mult) \
                        .then_inc(c_p, 1)
                if s >= 8 and s % 2 == 0 and (s - 8) // 2 < 8:
                    u = (s - 8) // 2
                    ve.wait_ge(c_s, 8 * j + u + 1)
                    ve.tensor_reduce(st(R_NEG + u % 2), (sa, sc)[u % 2][:, :], AX_X, ALU.max, negate=True) \
                        .then_inc(c_max, 1)
                if s >= 14 and (s - 14) % 4 == 0 and (s - 14) // 4 < 4:
                    g = (s - 14) // 4
                    ve.wait_ge(c_o, 4 * j + g + 1)
                    if g == 0:
                        ve.wait_ge(c_gate, j + 1)
                    tile = stream[:, bass.ds(4 * j + g, 1), SEQ:T]
                    tt(tile, tile, ov[:, 0:SEQ].unsqueeze(1), ALU.mult).then_inc(c_out, 1)

            def evac_a(h):
                ve.wait_ge(proj_done[0], h + 1)
                past(ve, a_s, 8 * h)
                ve.tensor_scalar(qk[:, 0, :], pj[:, 0, :], A_DIM ** -0.5, None, ALU.mult).then_inc(bank_free[0], 1)
                ve.wait_ge(proj_done[2], h + 1)
                past(ve, a_vt, h)
                ve.tensor_copy(kv[:, 0, :], pj[:, 2, :]).then_inc(bank_free[2], 1)

            ve.wait_ge(s_ready, 1)
            tt(vector_parts[:, :, 2:4], st(R_S, 32).rearrange("p (k v) -> p k v", v=2),
               vector_parts[:, :, 0:2].bitcast(F32), ALU.subtract).then_inc(s_ready, 1)
            for n in range(AHEAD):
                split_lo(n, n)
            for n, (kind, what, c) in enumerate(prologue()):
                for g in range(MOD0_GROUPS):
                    if n == mod_end[g]:
                        copy_rows(g)
                    if n == turn_at[g] + 1:
                        mod0_out(g)
                split_lo(n + AHEAD, n + AHEAD)
                if kind == "mod" and what == 2 and c == 0:
                    ve.wait_ge(setup_a, 2)
                    ve.scalar_tensor_tensor(st(R_LAM), st(R_EXP2), LAMBDA_INIT, st(R_EXP2 + 1), ALU.add,
                                            ALU.subtract)
                    ve.tensor_scalar(st(R_LG, 8), st(R_LG, 8), -1.0, None, ALU.mult).then_inc(setup_v, 1)
                if n == FIRST_SQUARE + KT + 1:
                    ve.wait_ge(ss_root, 1)
                    ve.reciprocal(st(R_RMS, 4), st(R_RMS, 4)).then_inc(ss_rec, 1)
                if n in runs:
                    first, last = runs[n]
                    for k in range(first, last + 1):
                        h_step(0, k, first, last)
            evac_a(0)

            def body_a(h, a):
                n0 = N_A + NCH * h
                for kt in range(KT):
                    if kt % 2 == 0:
                        split_lo(n0 + kt // 2 + AHEAD, kt // 2 + AHEAD)
                    if kt == KT - 1:
                        evac_a(h)
                    attend_a(a, kt)
                    if kt % 2 == 1:
                        mod_chunk(h - 1, kt // 2)

            ve.wait_ge(trig_loaded, 16)
            body_a(1, 0)
            with ve.Fori(2, A_HEADS) as h:
                body_a(h, h - 1)

            def body_b(b, first=False):
                n0 = N_B + 2 * NCH * b
                for s in range(2 * KT):
                    if s % 2 == 0:
                        c = s // 2 + AHEAD
                        split_lo(n0 + c, c, 768 if c < 2 * NCH else CH)
                    if s == KT - 1:
                        ve.wait_ge(proj_done[0], 8 + 2 * b + 1)
                        if first:
                            ve.wait_ge(a_s, 8 * A_HEADS)
                            ve.wait_ge(a_vt, A_HEADS)
                        else:
                            ve.wait_ge(b_s, 3 * b)
                            ve.wait_ge(b_vt, 2 * b)
                        ve.tensor_copy(qk[:, 0, :], pj[:, 0, :]).then_inc(bank_free[0], 1)
                        ve.wait_ge(w_used, n0 + NCH)
                        ve.tensor_copy(kv[:, 0, :], pj[:, 2, :]).then_inc(bank_free[2], 1)
                    if s == 2 * KT - 1:
                        ve.wait_ge(proj_done[0], 8 + 2 * b + 2)
                        ve.tensor_copy(kv[:, 1, :], pj[:, 0, :]).then_inc(bank_free[0], 1)
                    if not first:
                        retain_b(b - 1, s)
                    elif s < KT:
                        attend_a(A_HEADS - 1, s)
                    if s % 4 == 1:
                        mod_chunk(7 + b, s // 4)

            ve.wait_ge(dist_loaded, 16)
            body_b(0, True)
            body_b(1)
            with ve.Fori(2, B_HEADS) as b:
                body_b(b)

            def residual(layer, i, fb, n):
                for t in range(4):
                    if t < 3:
                        ve.wait_ge(proj_done[t], done_out(layer, i, t) + 1)
                    else:
                        ve.wait_ge(w_used, (N_O0, N_O1)[layer] + block_end[i])
                    for v in range(n // 256):
                        cols = slice(256 * v, 256 * v + 256)
                        tile = stream[:, 4 * fb + t, cols]
                        old = aux[:, t, cols] if layer == 0 and i < 4 else tile
                        col = (M_GATE0, M_GATE1)[layer] + 4 * fb + t
                        ve.scalar_tensor_tensor(tile, pj[:, t, cols], modv[:, v, col:col + 1], old, ALU.mult,
                                                ALU.add).then_inc(x1_lat if v < n // 256 - 1 else bank_free[t], 1)
                if i >= 4:
                    for t in range(4):
                        add_square(KT * (layer + 1) + 4 * fb + t + 1, t, n)

            block_end = {i: n0 + len(kts) // 2 for i, fb, kts, n0 in out_blocks()}

            def o_lo(i, k):
                n = KT * i + k
                ve.wait_ge(act_hi_done, n + 1)
                cols = slice(0, T) if i == 1 else slice(SEQ, T)
                width = T if i == 1 else SEQ
                tt(act_lo[:, k, 0:width], stream[:, k, cols], act_hi[:, k, 0:width].bitcast(F32), ALU.subtract) \
                    .then_inc(act_lo_done, 1)

            for k in range(4):
                o_lo(1, k)
            for i, fb, kts, n0 in out_blocks():
                for kt in kts:
                    if kt % 2 == 0:
                        c = n0 + (kt - kts[0]) // 2
                        split_lo(N_O0 + c + AHEAD, c + AHEAD)
                    if i == 0 and kt + 4 < EARLY:
                        o_lo(1, kt + 4)
                    if i == 3 and kt >= EARLY - 4:
                        o_lo(1, kt + 4)
                    if i < 4:
                        retain_b(B_HEADS - 1, EARLY * i + kt)
                        if kt % 2 == 1 and c < 2 * NCH and c % 2 == 0:
                            mod_chunk(11, c // 2)
                if i < 4:
                    ve.wait_ge(xr_loaded, 16 * (fb + 1))
                if i == 3:
                    ve.wait_ge(b_dc, B_HEADS)
                    ve.memset(prob[:, 1, :], 0.0).then_inc(zeroed, 1)
                    ve.wait_ge(zeroed, 3)
                    mod_out(11)
                    ve.wait_ge(m_out, 12)
                residual(0, i, fb, T)
            finish_scale(1)
            ve.wait_ge(ss_root, 2)
            ve.reciprocal(st(R_RMS, 4), st(R_RMS, 4)).then_inc(ss_rec, 1)
            for k in range(4):
                h_step(1, k, 0, KT - 1)

            def body_c(j, first=False):
                n0 = N_C + 3 * NCH * j
                for s in range(3 * KT):
                    if first and s + 4 < KT:
                        h_step(1, s + 4, 0, KT - 1)
                    if s % 2 == 0:
                        c = s // 2 + AHEAD
                        split_lo(n0 + c, c, CH // 2 if 2 * NCH <= c < 3 * NCH else CH)
                    if s == KT - 1:
                        for t in (0, 2):
                            ve.wait_ge(proj_done[t], done_c(j, 0, t) + 1)
                            ve.tensor_copy(stream[:, bass.ds(4 * j + t, 1), SEQ:T], pj[:, t:t + 1, 0:SEQ]) \
                                .then_inc(bank_free[t], 1)
                    if s == 2 * KT - 1:
                        for t in (0, 2):
                            ve.wait_ge(proj_done[t], done_c(j, 1, t) + 1)
                            past(ve, c_s, 8 * j)
                            ve.tensor_copy(qk[:, t // 2, 0:SEQ], pj[:, t, 0:SEQ]).then_inc(bank_free[t], 1)
                    if s == 3 * KT - 1:
                        ve.wait_ge(proj_done[0], done_c(j, 2, 0) + 1)
                        ve.tensor_copy(kv[:, 0, :], pj[:, 0, :]).then_inc(bank_free[0], 1)
                    if not first:
                        attend_c(j - 1, s)
                    norm_q_c(j, s)
                    if first and s >= KT and s % 4 == 1:
                        mod_chunk(12 + j, (s - KT) // 4, 1)
                    elif not first and s % 6 == 1:
                        mod_chunk(12 + j, s // 6, 1)

            ve.tensor_scalar(sm(S_QK), sm(S_QK), C_DIM ** -0.5, None, ALU.mult).then_inc(setup_v, 1)
            ve.wait_ge(setup_v, 4)
            ve.wait_ge(trig_loaded, 32)
            body_c(0, True)
            body_c(1)
            with ve.Fori(2, C_KV) as j:
                body_c(j)

            for k in range(4):
                o_lo(3, k)
            for i, fb, kts, n0 in out_blocks():
                for kt in kts:
                    c = n0 + (kt - kts[0]) // 2 + AHEAD
                    if kt % 2 == 0 and c < 4 * NCH:
                        split_lo(N_O1 + c, c)
                    if i == 0 and kt + 4 < EARLY:
                        o_lo(3, kt + 4)
                    if i == 3 and kt >= EARLY - 4:
                        o_lo(3, kt + 4)
                    if i < 4:
                        attend_c(C_KV - 1, EARLY * i + kt)
                if i == 3:
                    ve.wait_ge(c_t, 8 * C_KV)
                    ve.memset(prob[:, 1, :], 0.0).then_inc(zeroed, 1)
                    ve.wait_ge(zeroed, 4)
                residual(1, i, fb, SEQ)
            ve.wait_ge(ss_root, 3)
            ve.reciprocal(st(R_RMS, SEQ // P), st(R_RMS, SEQ // P)).then_inc(ss_rec, 1)
            ve.wait_ge(ss_spread, 3)
            for k in range(KT):
                tile = stream[:, k, 0:SEQ]
                ve.scalar_tensor_tensor(tile, tile, sm(S_FN + k), sc[:, 0:SEQ], ALU.mult, ALU.mult) \
                    .then_inc(out_ready, 1)


def _rotation(dim):
    axis, half = dim // 2, dim // 4
    m = np.zeros((P, P), np.float32)
    for f in range(P):
        if f % axis < half:
            m[f + half, f] = -1.0
        else:
            m[f - half, f] = 1.0
    return m


def _angles(dim):
    axis, half = dim // 2, dim // 4
    tok = np.arange(SEQ)
    pos = np.stack([tok // GRID_W, tok % GRID_W]).astype(np.float32)
    inv = (ROPE_THETA ** (-np.arange(0, axis, 2, dtype=np.float32) / np.float32(axis))).astype(np.float32)
    ang = np.zeros((P, SEQ), np.float32)
    for f in range(P):
        ang[f] = pos[(f % dim) // axis] * inv[f % axis % half]
    return np.stack([np.cos(ang), np.sin(ang)], 1).astype(np.float32)


def _distances():
    k = np.arange(256).reshape(2, P).transpose(1, 0)[:, :, None]
    q = np.arange(256)[None, None, :]
    d = [np.maximum(q - k, 0), np.maximum(k - q, 0), (q == k) * 1, 256 + q - k, 256 - q + k]
    return np.stack([v.reshape(P, 512) for v in d], 1).astype(np.float32)


def kernel(**inputs):
    import concourse.bacc as _bacc
    from concourse.bass_utils import run_bass_kernel_spmd as _run

    a = {k: np.asarray(v) for k, v in inputs.items()}

    def chunks(w, blocks):
        cols = [np.concatenate([w[:, s:s + n] for s, n in b], 1) for b in blocks]
        return np.ascontiguousarray(np.concatenate(
            [b.reshape(NCH, 2, P, -1).transpose(0, 2, 1, 3).reshape(NCH, P, -1) for b in cols], 0))

    ev, od = a["ev_w_in"][0], a["od_w_in"][0]
    mod_order = [(0, 1), (0, 0), (0, 2), (1, 1), (1, 0), (1, 2)]
    four = [[(512 * i, 512)] for i in range(4)]
    w_mod = np.concatenate([chunks(a["w_mod"][l][:, 2048 * t:2048 * t + 2048], four) for l, t in mod_order[2:]], 0)
    b_mod = np.concatenate([a["b_mod"][l, 2048 * t:2048 * t + 2048].reshape(16, P) for l, t in mod_order], 0).T
    w_b = []
    for b in range(B_HEADS):
        q, k, v, g = 4096 + 128 * b, 4608 + 128 * b, 5120 + 256 * b, 6144 + 256 * b
        w_b += [[(q, 128), (k, 128), (v, 128)], [(v + 128, 128), (g, 256)]]
    w_c = []
    for j in range(C_KV):
        w_c += [[(3072 + 512 * j, 512)], [(512 * j, 512)], [(2048 + 128 * j, 128), (2560 + 128 * j, 128)]]
    w_all = np.zeros((N_END, P, CH), np.float32)

    def place(n, part):
        w_all[n:n + len(part), :, 0:part.shape[-1]] = part

    heads_a = [[(1024 * i + 128 * h, 128) for i in range(4)] for h in range(A_HEADS)]
    first_head = chunks(ev, heads_a[0:1])
    for n, (kind, what, c) in enumerate(prologue()):
        if kind == "mod":
            third = 1 - what % 2
            cols = 2048 * third + 512 * (what // 2)
            if c == 0:
                place(n, chunks(a["w_mod"][0], [[(cols, 512)]]))
        else:
            place(n, first_head[c:c + 1])
    place(N_A + NCH, chunks(ev, heads_a[1:]))
    for i, block in enumerate(w_b):
        place(N_B + NCH * i, chunks(ev, [block]))
    for i, block in enumerate(w_c):
        place(N_C + NCH * i, chunks(od, [block]))
    for start, w in ((N_O0, a["ev_w_out"][0]), (N_O1, a["od_w_out"][0])):
        for i, fb, kts, n0 in out_blocks():
            place(start + n0, chunks(w, four[fb:fb + 1])[kts[0] // 2:kts[-1] // 2 + 1])
    small = np.zeros((P, S_END), np.float32)
    small[:, S_C:S_C + 32] = np.stack([a["c"][0].reshape(16, P).T, a["c_ctx"].reshape(16, P).T], -1).reshape(P, 32)
    small[:, S_G:S_G + 32] = a["norm_g"].reshape(32, P).T
    small[:, S_B:S_B + 96] = b_mod
    small[:, S_SUBLN] = a["diff_subln"][0]
    small[:, S_DECAY:S_DECAY + 8] = a["ret_decay"][0].reshape(1, 8)
    small[:, S_GN:S_GN + 8] = a["ret_gn"][0].reshape(8, P).T
    small[:, S_QK:S_QK + 2] = a["qk_norm"][0].T
    small[:, S_FN:S_FN + 16] = a["final_norm"].reshape(16, P).T
    small[0:A_DIM, S_DL:S_DL + 4] = a["diff_lambda"][0].T
    small[0:4, S_SEL:S_SEL + 2] = [[1, 0], [0, 1], [1, 0], [0, 1]]
    arrays = {
        "x_t": np.ascontiguousarray(np.concatenate([a["x"][0], a["ctx"][0]], 0).T).reshape(KT, P, T),
        "w_mod": w_mod,
        "w_all": w_all,
        "small_in": small,
        "mats_in": np.stack([_rotation(A_DIM), _rotation(C_DIM), np.ones((P, P), np.float32),
                             np.eye(P, dtype=np.float32)], 1),
        "trig_in": np.stack([_angles(A_DIM), _angles(C_DIM)], 0),
        "dist_in": _distances(),
    }
    arrays = {k: np.ascontiguousarray(v) for k, v in arrays.items()}
    nc = _bacc.Bacc("TRN2", target_bir_lowering=False, num_devices=1)
    args = [nc.dram_tensor(k, v.shape, F32, kind="ExternalInput").ap() for k, v in arrays.items()]
    args.append(nc.dram_tensor("out_t", (KT, P, SEQ), F32, kind="ExternalOutput").ap())
    bass_hybrid_backbone(nc, *args)
    r = _run(nc, [arrays], core_ids=[0])
    got = np.asarray(r.results[0]["out_t"])
    return np.ascontiguousarray(got.reshape(D_MODEL, SEQ).T).reshape(1, SEQ, D_MODEL)
```

```python
import math
from contextlib import ExitStack

import numpy as np

import concourse.bass as bass
from concourse import mybir

F32 = mybir.dt.float32
F32R = mybir.dt.float32r
ALU = mybir.AluOpType
ACT = mybir.ActivationFunctionType
AX_X = mybir.AxisListType.X

P = 128
D_MODEL = 2048
SEQ = 256
CTX = 256
T = SEQ + CTX
GRID_W = 64
ROPE_THETA = 10000.0
EPS = 1e-6
KT = D_MODEL // P
NCH = KT // 2
CH = 2 * 512
A_HEADS, A_DIM = 8, 64
B_HEADS, B_DIM = 4, 128
C_KV, C_DIM = 4, 128
LAMBDA_INIT = 0.8 - 0.6 * math.exp(-0.3 * 0)
WSLOTS, MSLOTS = 4, 2
AHEAD = 3

MOD0_GROUPS = 8
PAIRS = 4
FIRST_SQUARE = 4
N_A = NCH * MOD0_GROUPS
N_B = N_A + NCH * A_HEADS
N_O0 = N_B + 2 * NCH * B_HEADS
N_C = N_O0 + NCH * 4
N_O1 = N_C + 3 * NCH * C_KV
N_END = N_O1 + NCH * 4
MOD_SLOTS = {True: tuple(range(16, 48, 4)), False: (7, 9, 18, 22, 26, 28, 34, 43)}
LAT, CONTEXT = range(SEQ // P), range(SEQ // P, T // P)
ADDED_LAT, ADDED_CTX = 2 * KT, 2 * KT + 4
CTX_SUMS, CTX_SPREAD = 4, 6
CTX_TILE = {KT + 3 * (k // 2) + k % 2: k for k in range(KT)}
EARLY = 12

S_C, S_G, S_B, S_SUBLN, S_DECAY, S_GN, S_QK, S_FN, S_DL = 0, 32, 64, 160, 161, 169, 177, 179, 195
S_SEL = 199
S_END = 201
(R_S, R_LG, R_LAM, R_EXP2, R_PROD, R_NEG, R_SUM, R_REC, R_C2, R_SUB, R_EPS, R_RMS) = (
    0, 32, 40, 41, 43, 45, 47, 49, 51, 52, 53, 54)
R_END = 62
M_SCALE0, M_SHIFT0, M_GATE0, M_SCALE1, M_SHIFT1, M_GATE1 = (16 * i for i in range(6))


def prologue():
    head = iter(range(NCH))
    for g in range(MOD0_GROUPS):
        for c in range(NCH):
            yield "mod", g, c
        if 3 <= g:
            yield "head", 0, next(head)
    for c in head:
        yield "head", 0, c


def input_runs():
    heads = [n for n, (kind, what, c) in enumerate(prologue()) if kind == "head"]
    runs = {heads[0] - 4: (0, 1)}
    for i in range(1, NCH - 2):
        runs[heads[i - 1]] = (2 * i, 2 * i + 1)
    runs[heads[NCH - 3]] = (KT - 4, KT - 1)
    return runs


def out_blocks():
    for i in range(8):
        first = i < 4
        yield (i, i % 4, range(EARLY) if first else range(EARLY, KT),
               EARLY // 2 * i if first else 4 * (EARLY // 2) + (KT - EARLY) // 2 * (i - 4))


def bass_hybrid_backbone(nc, x_t, w_mod, w_all, small_in, mats_in, trig_in,
                         dist_in, out):
    ctx = ExitStack()
    with ctx:
        def sb(name, shape, dt=F32):
            return ctx.enter_context(nc.sbuf_tensor(name, shape, dt))

        def sem(name):
            return ctx.enter_context(nc.semaphore(name))

        w_raw = sb("w_raw", [P, WSLOTS, CH])
        w_hi = sb("w_hi", [P, WSLOTS, CH], F32R)
        w_lo = sb("w_lo", [P, WSLOTS, CH], F32R)
        m_raw = sb("m_raw", [P, MSLOTS, CH])
        m_acc = sb("m_acc", [P, 2, 512])
        act_hi = sb("act_hi", [P, KT, T], F32R)
        act_lo = sb("act_lo", [P, KT, T], F32R)
        stream = sb("stream", [P, KT, T])
        mats = sb("mats", [P, 4, P])
        trig = sb("trig", [P, 2, SEQ])
        aux_at = nc.sbuf_base
        aux = sb("aux", [P, 5, 512])
        qk_at = nc.sbuf_base
        qk = sb("qk", [P, 2, T])
        kv = sb("kv", [P, 2, T])
        v_tok_at = nc.sbuf_base
        v_tok = sb("v_tok", [P, 4, 256])
        pt_at = nc.sbuf_base
        pt = sb("pt", [P, 2, 4, 256])
        prob = sb("prob", [P, 3, 512])
        tmp_o_at = nc.sbuf_base
        tmp_o = sb("tmp_o", [P, 2, 512])
        tmp_r_at = nc.sbuf_base
        tmp_r = sb("tmp_r", [P, 2, 512])
        small = sb("small", [P, S_END])
        stat = sb("stat", [P, R_END])
        modv = sb("modv", [P, 2, 96])
        s_parts = sb("s_parts", [P, 4 * KT + P], F32R)

        op_hi = nc.alloc_sbuf_tensor_at("op_hi", [P, 2, 512], F32R, offset=aux_at)
        op_lo = nc.alloc_sbuf_tensor_at("op_lo", [P, 2, 512], F32R, offset=aux_at + 4 * 1024)
        k_hi = nc.alloc_sbuf_tensor_at("k_hi", [P, 512], F32R, offset=aux_at + 8 * 1024)
        k_lo = nc.alloc_sbuf_tensor_at("k_lo", [P, 512], F32R, offset=tmp_o_at + 4 * 512)

        pt_hi = nc.alloc_sbuf_tensor_at("pt_hi", [P, 2, 4, 256], F32R, offset=pt_at)
        v_parts = nc.alloc_sbuf_tensor_at("v_parts", [P, 4, 256], F32R, offset=v_tok_at)
        pt_lo = [nc.alloc_sbuf_tensor_at(f"pt_lo{i}", [P, 4, 256], F32R, offset=at)
                 for i, at in enumerate((tmp_r_at, qk_at))]

        pj = ctx.enter_context(nc.psum_tensor("pj", [P, 4, 512], F32))
        sa = ctx.enter_context(nc.psum_tensor("sa", [P, 512], F32))
        sc = ctx.enter_context(nc.psum_tensor("sc", [P, 512], F32))
        tr = ctx.enter_context(nc.psum_tensor("tr", [P, 512], F32))
        ov = ctx.enter_context(nc.psum_tensor("ov", [P, 512], F32))

        vector_parts = s_parts[:, 0:4 * KT].rearrange("p (k v) -> p k v", v=4)
        rot_a, rot_c, ones, ident = (mats[:, i, :] for i in range(4))

        normed = [tmp_r[:, 0, :], tmp_r[:, 1, :], kv[:, 0, :], kv[:, 1, :]]
        modulated = [tmp_o[:, 0, :], tmp_o[:, 1, :], qk[:, 0, :], qk[:, 1, :]]
        depth = len(normed)
        quarters = [(i // 2, slice(SEQ * (i % 2), SEQ * (i % 2) + SEQ)) for i in range(depth)]
        normed_ctx = [[b[:, SEQ:T] for b in normed], [tmp_r[:, i, cols] for i, cols in quarters]]
        modulated_ctx = [[b[:, SEQ:T] for b in modulated], [prob[:, i, cols] for i, cols in quarters]]

        def st(c, n=1):
            return stat[:, c:c + n]

        def sm(c, n=1):
            return small[:, c:c + n]

        consts_loaded, dist_loaded = sem("consts_loaded"), sem("dist_loaded")
        x_loaded = [sem(f"x_loaded{i}") for i in range(4)]
        w_loaded = [sem(f"w_loaded{i}") for i in range(WSLOTS)]
        m_loaded = [sem(f"m_loaded{i}") for i in range(MSLOTS)]
        xr_loaded = sem("xr_loaded")
        trig_loaded = sem("trig_loaded")
        out_stored = sem("out_stored")
        w_hi_done, w_lo_done, w_used = sem("w_hi_done"), sem("w_lo_done"), sem("w_used")
        row_copied, row_spread, mod0_read = sem("row_copied"), sem("row_spread"), sem("mod0_read")
        m_lat, m_ctx, m_sum, m_out = sem("m_lat"), sem("m_ctx"), sem("m_sum"), sem("m_out")
        setup_v, setup_a, setup_p = sem("setup_v"), sem("setup_a"), sem("setup_p")
        s_whole, s_ready, zeroed = sem("s_whole"), sem("s_ready"), sem("zeroed")
        ss_sq, ss_add, ss_sum, ss_root, ss_rec, ss_spread, ss_inv = (
            sem("ss_sq"), sem("ss_add"), sem("ss_sum"), sem("ss_root"), sem("ss_rec"), sem("ss_spread"), sem("ss_inv"))
        h_norm, h_lat, h_ctx = sem("h_norm"), sem("h_lat"), sem("h_ctx")
        act_hi_done, act_lo_done = sem("act_hi_done"), sem("act_lo_done")
        scale_ready = sem("scale_ready")
        proj_done = [sem(f"proj_done{i}") for i in range(4)]
        bank_free = [sem(f"bank_free{i}") for i in range(4)]
        x1_lat = sem("x1_lat")
        out_ready = sem("out_ready")
        a_rot, a_vt, a_vtok, a_tmp, a_cos, a_rope = (sem("a_rot"), sem("a_vt"), sem("a_vtok"), sem("a_tmp"),
                                                     sem("a_cos"), sem("a_rope"))
        a_s, a_max, a_exp, a_rec, a_c2, a_p2, a_p = (sem("a_s"), sem("a_max"), sem("a_exp"), sem("a_rec"),
                                                     sem("a_c2"), sem("a_p2"), sem("a_p"))
        a_t, a_pt, a_o, a_sq, a_ss, a_root, a_inv, a_spread, a_y, a_out = (
            sem("a_t"), sem("a_pt"), sem("a_o"), sem("a_sq"), sem("a_ss"), sem("a_root"), sem("a_inv"),
            sem("a_spread"), sem("a_y"), sem("a_out"))
        b_vt, b_vtok, b_argb, b_arg, b_expi, b_expc, b_di, b_dc = (
            sem("b_vt"), sem("b_vtok"), sem("b_argb"), sem("b_arg"), sem("b_expi"), sem("b_expc"), sem("b_di"),
            sem("b_dc"))
        b_s, b_pt, b_o, b_ocopy, b_mean, b_xc, b_sq, b_var, b_root, b_inv, b_spread, b_y, b_out = (
            sem("b_s"), sem("b_pt"), sem("b_o"), sem("b_ocopy"), sem("b_mean"), sem("b_xc"), sem("b_sq"),
            sem("b_var"), sem("b_root"), sem("b_inv"), sem("b_spread"), sem("b_y"), sem("b_out"))
        cq_sq, cq_ss, cq_root, cq_inv, cq_spread, cq_n, cq_rot, cq_sin, cq_cos, cq_rope = (
            sem("cq_sq"), sem("cq_ss"), sem("cq_root"), sem("cq_inv"), sem("cq_spread"),
            sem("cq_n"), sem("cq_rot"), sem("cq_sin"), sem("cq_cos"), sem("cq_rope"))
        ck_sq, ck_ss, ck_root, ck_inv, ck_spread, ck_n, ck_rot, ck_sin, ck_cos, ck_rope = (
            sem("ck_sq"), sem("ck_ss"), sem("ck_root"), sem("ck_inv"), sem("ck_spread"),
            sem("ck_n"), sem("ck_rot"), sem("ck_sin"), sem("ck_cos"), sem("ck_rope"))
        c_ptlo, c_vlo = sem("c_ptlo"), sem("c_vlo")
        b_gate, c_gate = sem("b_gate"), sem("c_gate")
        a_hi, a_lo, cq_hi, cq_lo, ck_hi, ck_lo = (sem("a_hi"), sem("a_lo"), sem("cq_hi"), sem("cq_lo"),
                                                  sem("ck_hi"), sem("ck_lo"))
        c_vt, c_vtok, c_s, c_max, c_exp, c_rec, c_p, c_t, c_pt, c_o, c_out = (
            sem("c_vt"), sem("c_vtok"), sem("c_s"), sem("c_max"), sem("c_exp"), sem("c_rec"), sem("c_p"),
            sem("c_t"), sem("c_pt"), sem("c_o"), sem("c_out"))

        block = ctx.enter_context(nc.Block())

        def past(eng, s, value):
            if not isinstance(value, int) or value > 0:
                eng.wait_ge(s, value)

        mod_end = {what: n + 1 for n, (kind, what, c) in enumerate(prologue()) if kind == "mod" and c == NCH - 1}

        runs = input_runs()

        def normed_context(layer, k):
            return 2 * KT * layer + k + 1

        turn_at = [mod_end[g] + (g < 3) for g in range(MOD0_GROUPS)]

        def evacs_a(h, t):
            return h

        def evacs_b(b, blk, t):
            return 8 + 2 * b + blk if t < 3 else 8

        def evacs_o0(i, t):
            return 16 + i if t < 3 else 8 + i

        def evacs_c(j, blk, t):
            return 24 + 3 * j + blk if t < 2 else (24 if t == 2 else 16) + 2 * j + blk

        def evacs_o1(i, t):
            return 36 + i if t < 2 else (32 if t == 2 else 24) + i

        def done_c(j, blk, t):
            return {0: 24 + 3 * j + blk, 1: 24 + 2 * j + blk, 2: 16 + 2 * j + blk}[t]

        def done_out(layer, i, t):
            return ((16, 16, 8), (36, 32, 24))[layer][t] + i

        @block.sync
        def _(sp):
            sp.dma_start(small[:, :], small_in).then_inc(consts_loaded, 16)
            sp.dma_start(mats[:, :, :], mats_in).then_inc(consts_loaded, 16)

            def load_w(n, c, width=CH):
                if isinstance(n, int) and n >= N_END:
                    return
                past(sp, w_lo_done, n - WSLOTS + 1)
                sp.dma_start(w_raw[:, c % WSLOTS, 0:width], w_all[n, :, 0:width]).then_inc(w_loaded[c % WSLOTS], 16)

            def load_m(it, c):
                ops = 2 * NCH * it + 2 * (c - 1)
                past(sp, m_lat, ops)
                past(sp, m_ctx, ops)
                sp.dma_start(m_raw[:, c % MSLOTS, :], w_mod[NCH * it + c]) \
                    .then_inc(m_loaded[c % MSLOTS], 16)

            def load_m_lat(it, c):
                sp.wait_ge(m_lat, 2 * NCH * it + 2 * (c - 1))
                if isinstance(it, int) and c < MSLOTS:
                    sp.wait_ge(m_ctx, 2 * NCH * it + 2 * (c - 1))
                sp.dma_start(m_raw[:, c % MSLOTS, :], w_mod[NCH * it + c]) \
                    .then_inc(m_loaded[c % MSLOTS], 16)

            for n in range(WSLOTS):
                load_w(n, n)
            for n in range(WSLOTS, FIRST_SQUARE + KT):
                if n % WSLOTS == 2:
                    q = n // WSLOTS - 1
                    sp.dma_start(stream[:, 4 * q:4 * q + 4, :], x_t[4 * q:4 * q + 4].rearrange("k p t -> p k t")) \
                        .then_inc(x_loaded[q], 16)
                load_w(n, n)
            with sp.Fori((FIRST_SQUARE + KT) // WSLOTS, (N_A + NCH) // WSLOTS) as i:
                for c in range(WSLOTS):
                    load_w(WSLOTS * i + c, c)
            sp.dma_start(trig[:, :, :], trig_in[0]).then_inc(trig_loaded, 16)
            for c in range(AHEAD):
                load_w(N_A + NCH + c, c)

            def body_a(h):
                for c in range(NCH):
                    load_w(N_A + NCH * h + c + AHEAD, c + AHEAD)
                    load_m(h - 1, c)

            def body_b(b):
                for c in range(2 * NCH):
                    if isinstance(b, int) and b == 0 and c == NCH:
                        sp.wait_ge(a_s, 8 * A_HEADS)
                        sp.dma_start(aux[:, :, :], dist_in).then_inc(dist_loaded, 16)
                    load_w(N_B + 2 * NCH * b + c + AHEAD, c + AHEAD, 768 if c + AHEAD < 2 * NCH else CH)
                    if c % 2 == 0:
                        load_m(7 + b, c // 2)

            body_a(1)
            with sp.Fori(2, A_HEADS) as h:
                body_a(h)
            body_b(0)
            with sp.Fori(1, B_HEADS) as b:
                body_b(b)
            for i, fb, kts, n0 in out_blocks():
                for c in range(len(kts) // 2):
                    load_w(N_O0 + n0 + c + AHEAD, n0 + c + AHEAD)
                    if i < 4 and n0 + c < 2 * NCH and (n0 + c) % 2 == 0:
                        load_m(11, (n0 + c) // 2)
                if i < 4:
                    if i == 0:
                        sp.wait_ge(b_dc, B_HEADS)
                        sp.wait_ge(b_di, B_HEADS)
                    else:
                        sp.wait_ge(bank_free[3], evacs_o0(i, 3))
                    sp.dma_start(aux[:, 0:4, :], x_t[4 * fb:4 * fb + 4].rearrange("k p t -> p k t")) \
                        .then_inc(xr_loaded, 16)
            sp.wait_ge(a_rope, A_HEADS)
            sp.dma_start(trig[:, :, :], trig_in[1]).then_inc(trig_loaded, 16)

            def body_c(j, first=False):
                for c in range(3 * NCH):
                    load_w(N_C + 3 * NCH * j + c + AHEAD, c + AHEAD,
                           CH // 2 if 2 * NCH <= c + AHEAD < 3 * NCH else CH)
                    for i, slot in enumerate(MOD_SLOTS[first]):
                        if c == slot // 2:
                            load_m_lat(12 + j, i)

            body_c(0, True)
            with sp.Fori(1, C_KV) as j:
                body_c(j)
            with sp.Fori(0, 7) as i:
                for c in range(AHEAD, WSLOTS + AHEAD):
                    load_w(N_O1 + WSLOTS * i + c, c)
            load_w(N_END - 1, 3)
            for q in range(4):
                sp.wait_ge(out_ready, 4 * (q + 1))
                sp.dma_start(out[4 * q:4 * q + 4].rearrange("k p t -> p k t"), stream[:, 4 * q:4 * q + 4, 0:SEQ]) \
                    .then_inc(out_stored, 16)
            sp.wait_ge(out_stored, 64)

        @block.tensor
        def _(pe):
            mm, tp = pe.matmul, pe.transpose

            pe.wait_ge(setup_v, 1)
            pe.wait_ge(consts_loaded, 32)
            mm(sc[:, 0:2], ones[0:64, :], stat[0:64, R_PROD:R_PROD + 2], start=True, stop=True).then_inc(setup_p, 1)

            def mod_rows(g, c, n):
                if c == 0:
                    if g == 0:
                        pe.wait_ge(s_ready, 2)
                    past(pe, row_copied, g - 1)
                pe.wait_ge(w_lo_done, n + 1)
                slot = n % WSLOTS
                for k2 in range(2):
                    k = 2 * c + k2
                    for part in (w_hi, w_lo):
                        last = mm((tr, sa)[g % 2][:, :], s_parts[:, 4 * k:4 * k + P],
                                  part[:, slot, 512 * k2:512 * k2 + 512], start=(k == 0 and part is w_hi),
                                  stop=(k == KT - 1 and part is w_lo))
                last.then_inc(w_used, 1)

            def spread_rows(g):
                pe.wait_ge(row_copied, g + 1)
                past(pe, mod0_read, g)
                for f in range(4):
                    last = mm(ov[:, 2 * f:2 * f + 2], m_acc[0:4, g % 2, P * f:P * f + P], small[0:4, S_SEL:S_SEL + 2],
                              start=True, stop=True)
                last.then_inc(row_spread, 1)

            def project(n0, kt, ntiles, ncols, free_count, act_base=None, kts=range(KT), slot0=0):
                c, k2 = (kt - kts[0]) // 2, kt % 2
                slot, width = (slot0 + c) % WSLOTS, P * ntiles
                if k2 == 0:
                    pe.wait_ge(w_lo_done, n0 + c + 1)
                if act_base is not None:
                    pe.wait_ge(act_lo_done, act_base + kt + 1)
                for t in range(ntiles):
                    if kt == kts[0]:
                        past(pe, bank_free[t], free_count(t))
                    cols = slice(k2 * width + P * t, k2 * width + P * t + P)
                    acc = pj[:, t, 0:ncols]
                    wh, wl = w_hi[:, slot, cols], w_lo[:, slot, cols]
                    mm(acc, wh, act_hi[:, kt, 0:ncols], start=(kt == kts[0]), stop=False)
                    mm(acc, wh, act_lo[:, kt, 0:ncols], start=False, stop=False)
                    last = mm(acc, wl, act_hi[:, kt, 0:ncols], start=False, stop=(kt == kts[-1]))
                    if kt == kts[-1] and t < ntiles - 1:
                        last.then_inc(proj_done[t], 1)
                if k2 == 1:
                    last.then_inc(w_used, 1)

            def three_passes(dst, w_high, w_low, a_high, a_low):
                mm(dst, w_high, a_high, start=True, stop=False)
                mm(dst, w_high, a_low, start=False, stop=False)
                return mm(dst, w_low, a_high, start=False, stop=True)

            def token_sums(dst, tiles):
                for i, parts in enumerate(tiles):
                    for n, part in enumerate(parts):
                        last = mm(dst[:, i:i + 1], part, ones[:, 0:1], start=(n == 0), stop=(n == len(parts) - 1))
                return last

            def spread(banks, columns):
                for i in columns:
                    last = tp(banks[i // 4][:, P * (i % 4):P * (i % 4) + P],
                              st(R_RMS + i).to_broadcast([P, P]), ident)
                return last

            def sum_mod(it):
                pe.wait_ge(m_lat, 2 * NCH * (it + 1))
                pe.wait_ge(m_ctx, 2 * NCH * (it + 1))
                for v in range(2):
                    for f in range(4):
                        last = mm(sa[:, 4 * v + f:4 * v + f + 1], m_acc[:, v, P * f:P * f + P], ones[:, 0:1],
                                  start=True, stop=True)
                last.then_inc(m_sum, 1)

            def sum_mod_lat(it):
                pe.wait_ge(m_lat, 2 * NCH * (it + 1))
                for f in range(4):
                    last = mm(sa[:, f:f + 1], m_acc[:, 0, P * f:P * f + P], ones[:, 0:1], start=True, stop=True)
                last.then_inc(m_sum, 1)

            def attend_a(a, s):
                if s == 0:
                    if isinstance(a, int) and a == 0:
                        pe.wait_ge(row_copied, MOD0_GROUPS)
                        pe.wait_ge(mod0_read, MOD0_GROUPS)
                        pe.wait_ge(ss_inv, 1)
                    pe.wait_ge(bank_free[0], a + 1)
                    pe.wait_ge(bank_free[1], a + 1)
                    pe.wait_ge(bank_free[2], a + 1)
                    past(pe, a_y, a)
                    for i in range(2):
                        last = mm(tr[:, 256 * i:256 * i + 256], rot_a, qk[:, i, 0:SEQ], start=True, stop=True)
                    last.then_inc(a_rot, 1)
                    past(pe, a_out, a)
                    for i in range(4):
                        last = tp(ov[:, P * i:P * i + P], kv[:, 0, P * i:P * i + P], ident)
                    last.then_inc(a_vt, 1)
                if s == 1 and not (isinstance(a, int) and a == 0):
                    pe.wait_ge(a_exp, 8 * a)
                    sum_mod(a - 1)
                if s in (2, 4, 6, 8) and s >= 6:
                    transposes_a(a, (s - 6) // 2)
                if s in (2, 4, 6, 8):
                    q = (s - 2) // 2
                    if q == 0:
                        pe.wait_ge(a_lo, 2 * a + 2)
                        past(pe, m_out, a)
                    else:
                        pe.wait_ge(a_exp, 8 * a + 2 * q)
                    keys = slice(0, T) if q < 2 else slice(SEQ, T)
                    nk = T if q < 2 else CTX
                    for m, bank in enumerate((sa, sc)):
                        rows, queries = slice(64 * m, 64 * m + 64), slice(P * q, P * q + P)
                        three_passes(bank[:, 0:nk], op_hi[rows, 0, queries], op_lo[rows, 0, queries],
                                     op_hi[rows, 1, keys], op_lo[rows, 1, keys]).then_inc(a_s, 1)
                if s == 10:
                    transposes_a(a, 2)
                    pe.wait_ge(a_vtok, a + 1)
                    pe.wait_ge(a_pt, 4 * a + 2)
                    for i in range(4):
                        last = mm(ov[:, 0:SEQ], v_tok[:, i, 0:P], pt[:, 0, i, :], start=(i == 0), stop=(i == 3))
                    last.then_inc(a_o, 1)
                if s == 12:
                    transposes_a(a, 3)
                if s == 13:
                    pe.wait_ge(a_pt, 4 * a + 4)
                    for i in range(2):
                        last = mm(ov[:, SEQ:T], v_tok[:, 2 + i, 0:P], pt[:, 1, i, :], start=(i == 0), stop=(i == 1))
                    last.then_inc(a_o, 1)
                if s == 14:
                    pe.wait_ge(a_sq, a + 1)
                    pe.wait_ge(a_exp, 8 * a + 8)
                    token_sums(sc, [[tmp_r[:, 0, P * i:P * i + P]] for i in range(4)]).then_inc(a_ss, 1)
                if s == 15:
                    pe.wait_ge(a_inv, a + 1)
                    pe.wait_ge(a_pt, 4 * a + 4)
                    spread([tr], range(4)).then_inc(a_spread, 1)

            def transposes_a(a, q):
                pe.wait_ge(a_p, 4 * a + q + 1)
                past(pe, a_pt, 4 * a + q)
                for i in range(4 if q < 2 else 2):
                    last = tp(tr[:, P * i:P * i + P], prob[:, 2, P * i:P * i + P], ident)
                last.then_inc(a_t, 1)

            def retain_b(b, s):
                if s == 0:
                    if isinstance(b, int) and b == 0:
                        pe.wait_ge(a_exp, 8 * A_HEADS)
                    past(pe, b_xc, 2 * b)
                    sum_mod(7 + b)
                    pe.wait_ge(bank_free[0], 8 + 2 * b + 2)
                    pe.wait_ge(bank_free[1], 8 + 2 * b + 1)
                    pe.wait_ge(bank_free[2], 8 + 2 * b + 1)
                    if isinstance(b, int) and b == 0:
                        pe.wait_ge(a_out, A_HEADS)
                    past(pe, b_ocopy, 2 * b)
                    for e, bank in enumerate((tr, ov)):
                        for i in range(4):
                            last = tp(bank[:, P * i:P * i + P], kv[:, e, P * i:P * i + P], ident)
                        last.then_inc(b_vt, 1)
                if s == 1:
                    pe.wait_ge(m_out, 8 + b)
                    for i in range(2):
                        last = mm(sa[:, 256 * i:256 * i + 256], qk[:, 1, P * i:P * i + P], qk[:, 0, 0:SEQ],
                                  start=True, stop=True)
                    last.then_inc(b_s, 1)
                if s == 2:
                    past(pe, b_y, 2 * b)
                    if isinstance(b, int) and b == 0:
                        pe.wait_ge(a_exp, 8 * A_HEADS)
                    for i in range(2):
                        last = mm(sc[:, 256 * i:256 * i + 256], qk[:, 1, SEQ + P * i:SEQ + P * i + P],
                                  qk[:, 0, 0:SEQ], start=True, stop=True)
                    last.then_inc(b_s, 1)
                if s == 6:
                    pe.wait_ge(b_pt, 3 * b + 1)
                    for i in range(2):
                        last = mm(sa[:, 256 * i:256 * i + 256], qk[:, 1, SEQ + P * i:SEQ + P * i + P],
                                  qk[:, 0, SEQ:T], start=True, stop=True)
                    last.then_inc(b_s, 1)
                if s == 9:
                    pe.wait_ge(b_pt, 3 * b + 3)
                    pe.wait_ge(b_vtok, 2 * b + 2)
                    for e, bank in enumerate((tr, ov)):
                        ecols = slice(P * e, P * e + P)
                        for i in range(4):
                            mm(bank[:, 0:SEQ], v_tok[:, i, ecols], pt[:, i // 4, i % 4, :], start=(i == 0),
                               stop=(i == 3))
                        for i in range(2):
                            last = mm(bank[:, SEQ:T], v_tok[:, 2 + i, ecols], pt[:, 1, i, :], start=(i == 0),
                                      stop=(i == 1))
                        last.then_inc(b_o, 1)
                if s == 12:
                    pe.wait_ge(b_ocopy, 2 * b + 2)
                    pe.wait_ge(b_pt, 3 * b + 3)
                    for e in range(2):
                        last = mm(sa[:, :], ones, tmp_o[:, e, :], start=(e == 0), stop=(e == 1))
                    last.then_inc(b_mean, 1)
                if s == 16:
                    pe.wait_ge(b_sq, 2 * b + 2)
                    token_sums(sc, [[tmp_r[:, e, P * i:P * i + P] for e in range(2)] for i in range(4)]) \
                        .then_inc(b_var, 1)
                if s == 18:
                    pe.wait_ge(b_inv, b + 1)
                    spread([sc], range(4)).then_inc(b_spread, 1)

            def norm_q_c(j, s):
                if s == 35:
                    pe.wait_ge(cq_sq, 2 * j + 2)
                    past(pe, c_exp, 8 * j)
                    token_sums(sa, [[tmp_o[:, i // 4, P * (i % 4):P * (i % 4) + P]] for i in range(8)]) \
                        .then_inc(cq_ss, 1)
                if s == 38:
                    pe.wait_ge(cq_inv, j + 1)
                    if isinstance(j, int) and j == 0:
                        pe.wait_ge(ss_inv, 3)
                    spread([sa, sc], range(8)).then_inc(cq_spread, 1)
                if s == 41:
                    pe.wait_ge(cq_n, 2 * j + 2)
                    for i, bank in enumerate((sa, sc)):
                        mm(bank[:, :], rot_c, qk[:, i, :], start=True, stop=True).then_inc(cq_rot, 1)

            def attend_c(j, s):
                if s == 0:
                    pe.wait_ge(cq_sin, 2 * j + 2)
                    sum_mod_lat(12 + j)
                if s == 1:
                    pe.wait_ge(ck_sq, j + 1)
                    pe.wait_ge(m_out, 13 + j)
                    token_sums(sa, [[tmp_o[:, 0, P * i:P * i + P]] for i in range(4)]).then_inc(ck_ss, 1)
                    past(pe, c_out, 4 * j)
                    for i in range(4):
                        last = tp(ov[:, P * i:P * i + P], kv[:, 1, P * i:P * i + P], ident)
                    last.then_inc(c_vt, 1)
                if s == 3:
                    pe.wait_ge(ck_inv, j + 1)
                    spread([sa], range(4)).then_inc(ck_spread, 1)
                if s == 5:
                    pe.wait_ge(ck_n, j + 1)
                    mm(sc[:, 0:SEQ], rot_c, kv[:, 0, 0:SEQ], start=True, stop=True).then_inc(ck_rot, 1)
                if s >= 11 and (s - 11) % 2 == 0 and (s - 11) // 2 < 8:
                    u = (s - 11) // 2
                    pe.wait_ge(c_p, 8 * j + u + 1)
                    past(pe, c_ptlo, 8 * j + u)
                    for i in range(4):
                        last = tp(tr[:, P * i:P * i + P], prob[:, u % 2, P * i:P * i + P], ident)
                    last.then_inc(c_t, 1)
                if s >= 8 and s % 2 == 0 and (s - 8) // 2 < 8:
                    u = (s - 8) // 2
                    g, q = u // 2, u % 2
                    if u == 0:
                        pe.wait_ge(ck_lo, j + 1)
                        pe.wait_ge(cq_lo, j + 1)
                        pe.wait_ge(ck_n, j + 1)
                    if u >= 2:
                        pe.wait_ge(c_exp, 8 * j + u - 1)
                    bank = (sa, sc)[u % 2]
                    qcol = 256 * (g % 2) + P * q
                    three_passes(bank[:, :], op_hi[:, g // 2, qcol:qcol + P], op_lo[:, g // 2, qcol:qcol + P],
                                 k_hi[:, :], k_lo[:, :]).then_inc(c_s, 1)
                if s >= 15 and (s - 15) % 4 == 0 and (s - 15) // 4 < 4:
                    g = (s - 15) // 4
                    pe.wait_ge(c_ptlo, 8 * j + 2 * g + 2)
                    if g == 0:
                        pe.wait_ge(c_vlo, j + 1)
                    past(pe, c_out, 4 * j + g)
                    for i in range(4):
                        v_hi, v_lo = v_parts[:, i, 0:P], v_parts[:, i, P:2 * P]
                        mm(ov[:, 0:SEQ], v_hi, pt_hi[:, g % 2, i, :], start=(i == 0), stop=False)
                        mm(ov[:, 0:SEQ], v_hi, pt_lo[g % 2][:, i, :], start=False, stop=False)
                        last = mm(ov[:, 0:SEQ], v_lo, pt_hi[:, g % 2, i, :], start=False, stop=(i == 3))
                    last.then_inc(c_o, 1)

            def norm_sums(tiles):
                token_sums(sc[:, tiles[0]:tiles[-1] + 1], [[prob[:, 1, P * t:P * t + P]] for t in tiles]) \
                    .then_inc(ss_sum, 1)

            def norm_spread(i, tiles):
                pe.wait_ge(ss_rec, i + 1)
                spread([sc], tiles).then_inc(ss_spread, 1)

            for n, (kind, what, c) in enumerate(prologue()):
                if kind == "mod":
                    mod_rows(what, c, n)
                else:
                    for kt in (2 * c, 2 * c + 1):
                        project(n - c, kt, 4, T, lambda t: 0, 0, slot0=n - c)
                for g in range(MOD0_GROUPS):
                    if n == turn_at[g]:
                        spread_rows(g)
                if n == FIRST_SQUARE + KT + 1:
                    pe.wait_ge(setup_a, 2)
                    pe.wait_ge(ss_add, KT)
                    norm_sums(range(4))
                if n == FIRST_SQUARE + KT + 2:
                    norm_spread(0, range(4))

            def body_a(h, a):
                for kt in range(KT):
                    project(N_A + NCH * h, kt, 4, T, lambda t: evacs_a(h, t))
                    attend_a(a, kt)

            body_a(1, 0)
            with pe.Fori(2, A_HEADS) as h:
                body_a(h, h - 1)

            def body_b(b, first=False):
                for s in range(2 * KT):
                    blk, kt = s // KT, s % KT
                    project(N_B + 2 * NCH * b + NCH * blk, kt, 3, T, lambda t: evacs_b(b, blk, t))
                    if not first:
                        retain_b(b - 1, s)
                    elif s < KT:
                        attend_a(A_HEADS - 1, s)

            body_b(0, True)
            body_b(1)
            with pe.Fori(2, B_HEADS) as b:
                body_b(b)

            for i, fb, kts, n0 in out_blocks():
                for kt in kts:
                    project(N_O0 + n0, kt, 4, T, lambda t: evacs_o0(i, t), KT if i in (0, 4) else None, kts, n0)
                    if i < 4:
                        retain_b(B_HEADS - 1, EARLY * i + kt)
                if i == 3:
                    pe.wait_ge(b_xc, 2 * B_HEADS)
                    sum_mod(11)
            pe.wait_ge(m_out, 12)
            pe.wait_ge(ss_add, ADDED_LAT)
            pe.wait_ge(b_y, 2 * B_HEADS)
            norm_sums(LAT)
            norm_spread(1, LAT)

            def body_c(j, first=False):
                for s in range(3 * KT):
                    blk, kt = s // KT, s % KT
                    n0 = N_C + 3 * NCH * j + NCH * blk
                    project(n0, kt, 4 if blk < 2 else 2, SEQ if blk < 2 else T, lambda t: evacs_c(j, blk, t),
                            {0: 2 * KT, 2: 3 * KT}.get(blk) if first else None)
                    if first and s == CTX_SUMS:
                        pe.wait_ge(ss_add, ADDED_CTX)
                        pe.wait_ge(ss_inv, 2)
                        norm_sums(CONTEXT)
                    if first and s == CTX_SPREAD:
                        norm_spread(2, CONTEXT)
                    if not first:
                        attend_c(j - 1, s)
                    norm_q_c(j, s)

            body_c(0, True)
            body_c(1)
            with pe.Fori(2, C_KV) as j:
                body_c(j)
            for i, fb, kts, n0 in out_blocks():
                for kt in kts:
                    project(N_O1 + n0, kt, 4, SEQ, lambda t: evacs_o1(i, t), 4 * KT if i in (0, 4) else None, kts,
                            n0)
                    if i < 4:
                        attend_c(C_KV - 1, EARLY * i + kt)
            pe.wait_ge(ss_add, ADDED_CTX + KT)
            norm_sums(LAT)
            norm_spread(3, LAT)

        @block.scalar
        def _(act):
            f = act.activation
            act.wait_ge(consts_loaded, 32)
            f(st(R_S, 32), sm(S_C, 32), ACT.Silu).then_inc(s_whole, 1)
            act.wait_ge(s_whole, 1)
            act.wait_ge(zeroed, 2)
            f(vector_parts[:, :, 0:2], st(R_S, 32).rearrange("p (k v) -> p k v", v=2), ACT.Copy).then_inc(s_ready, 1)
            act.wait_ge(setup_p, 1)
            f(st(R_EXP2, 2), sc[:, 0:2], ACT.Exp).then_inc(setup_a, 1)
            f(st(R_LG, 8), sm(S_DECAY, 8), ACT.Exp).then_inc(setup_a, 1)

            def root_of_mean(i, tiles):
                act.wait_ge(ss_sum, i + 1)
                act.wait_ge(setup_v, 2)
                f(st(R_RMS + tiles[0], len(tiles)), sc[:, tiles[0]:tiles[-1] + 1], ACT.Sqrt, bias=st(R_EPS),
                  scale=1.0 / D_MODEL) \
                    .then_inc(ss_root, 1)

            def keep_inverse(i, tiles):
                act.wait_ge(ss_spread, i + 1)
                cols = slice(P * tiles[0], P * tiles[-1] + P)
                f(prob[:, 2, cols], sc[:, cols], ACT.Copy).then_inc(ss_inv, 1)

            def split_hi(n, c, width=CH):
                past(act, w_used, n - WSLOTS + 1)
                act.wait_ge(w_loaded[c % WSLOTS], loads(n, c))
                f(w_hi[:, c % WSLOTS, 0:width], w_raw[:, c % WSLOTS, 0:width], ACT.Copy).then_inc(w_hi_done, 1)

            def loads(n, c):
                return (n - c % WSLOTS) * (16 // WSLOTS) + 16

            def act_split(k, full):
                f(act_hi[:, k, 0:full.shape[-1]], full, ACT.Copy).then_inc(act_hi_done, 1)

            def h_context(layer, k):
                c_scale, c_shift = ((M_SCALE0, M_SHIFT0), (M_SCALE1, M_SHIFT1))[layer]
                act.wait_ge(h_norm, normed_context(layer, k))
                act.wait_ge(scale_ready, 2 * (k // 4 + 1) if layer == 0 else 2 * PAIRS + 2)
                past(act, act_lo_done, 3 * KT * layer + k - depth + 1)
                f(modulated_ctx[layer][k % depth], normed_ctx[layer][k % depth], ACT.Identity,
                  bias=modv[:, 1, c_shift + k:c_shift + k + 1], scale=modv[:, 1, c_scale + k:c_scale + k + 1]) \
                    .then_inc(h_ctx, 1)

            def h_step(layer, k, first, last):
                if k == first:
                    h_context(layer, k)
                if k < last:
                    h_context(layer, k + 1)
                act.wait_ge(h_ctx, KT * layer + k + 1)
                act.wait_ge(h_lat, KT * layer + k + 1)
                if layer == 0:
                    f(act_hi[:, k, :], modulated[k % depth], ACT.Copy).then_inc(act_hi_done, 1)
                else:
                    f(act_hi[:, k, SEQ:T], modulated_ctx[1][k % depth], ACT.Copy).then_inc(act_hi_done, 1)

            def h_latents_hi(k):
                act.wait_ge(h_lat, KT + k + 1)
                f(act_hi[:, k, 0:SEQ], modulated[k % depth][:, 0:SEQ], ACT.Copy).then_inc(act_hi_done, 1)

            def attend_a(a, s):
                if s == 0:
                    act.wait_ge(a_vt, a + 1)
                    f(v_tok[:, :, 0:P], ov[:, :].rearrange("p (i d) -> p i d", i=4), ACT.Copy).then_inc(a_vtok, 1)
                if s == 1:
                    act.wait_ge(a_rope, a + 1)
                    for i in range(2):
                        f(op_hi[:, i, :], qk[:, i, :], ACT.Copy).then_inc(a_hi, 1)
                if s in (6, 8, 10, 12):
                    q = (s - 6) // 2
                    act.wait_ge(a_t, 4 * a + q + 1)
                    n = 4 if q < 2 else 2
                    f(pt[:, q // 2, 0:n, P * (q % 2):P * (q % 2) + P],
                      tr[:, 0:P * n].rearrange("p (i d) -> p i d", i=n), ACT.Copy).then_inc(a_pt, 1)
                if s in (2, 4, 6, 8):
                    q = (s - 2) // 2
                    nk = T if q < 2 else CTX
                    past(act, a_p, 4 * a + q)
                    for m, bank in enumerate((sa, sc)):
                        act.wait_ge(a_max, 8 * a + 2 * q + m + 1)
                        f(prob[:, m, 0:nk], bank[:, 0:nk], ACT.Exp, bias=st(R_NEG + m), accum_out=st(R_SUM + m)) \
                            .then_inc(a_exp, 1)
                if s == 13:
                    act.wait_ge(a_o, 2 * a + 2)
                    past(act, a_y, a)
                    f(tmp_r[:, 0, :], ov[:, :], ACT.Square).then_inc(a_sq, 1)
                if s == 14:
                    act.wait_ge(a_ss, a + 1)
                    f(st(R_RMS, 4), sc[:, 0:4], ACT.Sqrt, bias=st(R_EPS), scale=1.0 / (2 * A_DIM)) \
                        .then_inc(a_root, 1)

            def retain_b(b, s):
                if s == 0:
                    past(act, b_pt, 3 * b)
                    past(act, b_y, 2 * b)
                    if isinstance(b, int) and b == 0:
                        act.wait_ge(a_t, 4 * A_HEADS)
                        act.wait_ge(a_out, A_HEADS)
                    f(prob[:, 1, :], aux[:, 3, :], ACT.Exp, scale=stat[:, lg_col(b, 0)]).then_inc(b_expc, 1)
                    f(tmp_r[:, 1, :], aux[:, 4, :], ACT.Exp, scale=stat[:, lg_col(b, 1)]).then_inc(b_expc, 1)
                    act.wait_ge(b_arg, b + 1)
                    f(prob[:, 0, :], tmp_r[:, 0, :], ACT.Exp).then_inc(b_expi, 1)
                    for e, bank in enumerate((tr, ov)):
                        act.wait_ge(b_vt, 2 * b + e + 1)
                        f(v_tok[:, :, P * e:P * e + P], bank[:, :].rearrange("p (i d) -> p i d", i=4), ACT.Copy) \
                            .then_inc(b_vtok, 1)
                if s == 4:
                    gates = stream[:, bass.ds(2 * b + 8, 2), :]
                    act.wait_ge(bank_free[1], 8 + 2 * b + 2)
                    act.wait_ge(bank_free[2], 8 + 2 * b + 2)
                    f(gates, gates, ACT.Silu).then_inc(b_gate, 1)
                if s == 9:
                    for e, bank in enumerate((tr, ov)):
                        act.wait_ge(b_o, 2 * b + e + 1)
                        f(tmp_o[:, e, :], bank[:, :], ACT.Copy).then_inc(b_ocopy, 1)
                if s == 13:
                    for e in range(2):
                        act.wait_ge(b_xc, 2 * b + e + 1)
                        f(tmp_r[:, e, :], tmp_o[:, e, :], ACT.Square).then_inc(b_sq, 1)
                if s == 16:
                    act.wait_ge(b_var, b + 1)
                    f(st(R_RMS, 4), sc[:, 0:4], ACT.Sqrt, bias=st(R_EPS), scale=1.0 / (2 * B_DIM)) \
                        .then_inc(b_root, 1)

            def lg_col(b, direction):
                return bass.ds(R_LG + 4 * direction + b, 1)

            def norm_q_c(j, s):
                if s == 32:
                    for i in range(2):
                        act.wait_ge(bank_free[1 + 2 * i], evacs_c(j, 1, 1 + 2 * i) + 1)
                        act.wait_ge(bank_free[2 * i], evacs_c(j, 1, 2 * i) + 1)
                        if i == 0:
                            past(act, ck_sin, j)
                        f(tmp_o[:, i, :], qk[:, i, :], ACT.Square).then_inc(cq_sq, 1)
                if s == 35:
                    act.wait_ge(cq_ss, j + 1)
                    f(st(R_RMS, 8), sa[:, 0:8], ACT.Sqrt, bias=st(R_EPS), scale=1.0 / C_DIM).then_inc(cq_root, 1)

            def attend_c(j, s):
                if s == 0:
                    act.wait_ge(bank_free[0], evacs_c(j, 2, 0) + 1)
                    act.wait_ge(cq_rope, j + 1)
                    f(tmp_o[:, 0, :], kv[:, 0, :], ACT.Square).then_inc(ck_sq, 1)
                if s == 3:
                    act.wait_ge(cq_rope, j + 1)
                    f(op_hi[:, :, :], qk[:, :, :], ACT.Copy).then_inc(cq_hi, 1)
                if s == 6:
                    act.wait_ge(ck_rope, j + 1)
                    f(k_hi[:, :], kv[:, 0, :], ACT.Copy).then_inc(ck_hi, 1)
                if s == 1:
                    act.wait_ge(ck_ss, j + 1)
                    f(st(R_RMS, 4), sa[:, 0:4], ACT.Sqrt, bias=st(R_EPS), scale=1.0 / C_DIM).then_inc(ck_root, 1)
                    act.wait_ge(c_vt, j + 1)
                    f(v_parts[:, :, 0:P], ov[:, :].rearrange("p (i d) -> p i d", i=4), ACT.Copy).then_inc(c_vtok, 1)
                if s >= 11 and (s - 11) % 2 == 0 and (s - 11) // 2 < 8:
                    u = (s - 11) // 2
                    g, q = u // 2, u % 2
                    act.wait_ge(c_t, 8 * j + u + 1)
                    past(act, c_o, 4 * j + max(g - 1, 0))
                    f(pt_hi[:, g % 2, :, P * q:P * q + P], tr[:, :].rearrange("p (i d) -> p i d", i=4), ACT.Copy) \
                        .then_inc(c_pt, 1)
                if s >= 8 and s % 2 == 0 and (s - 8) // 2 < 8:
                    u = (s - 8) // 2
                    act.wait_ge(c_max, 8 * j + u + 1)
                    past(act, c_t, 8 * j + max(u - 1, 0))
                    f(prob[:, u % 2, :], (sa, sc)[u % 2][:, :], ACT.Exp, bias=st(R_NEG + u % 2),
                      accum_out=st(R_SUM + u % 2)).then_inc(c_exp, 1)

            def evac_a(h):
                act.wait_ge(proj_done[1], h + 1)
                past(act, a_s, 8 * h)
                f(qk[:, 1, :], pj[:, 1, :], ACT.Copy).then_inc(bank_free[1], 1)
                act.wait_ge(w_used, N_A + NCH * (h + 1))
                f(stream[:, bass.ds(h, 1), :], pj[:, 3:4, :], ACT.Silu).then_inc(bank_free[3], 1)

            for n in range(AHEAD):
                split_hi(n, n)
            for n, (kind, what, c) in enumerate(prologue()):
                split_hi(n + AHEAD, n + AHEAD)
                k = n - FIRST_SQUARE
                if 0 <= k < KT:
                    act.wait_ge(x_loaded[k // 4], 16)
                    past(act, ss_add, k - depth + 1)
                    f(normed[k % depth], stream[:, k, :], ACT.Square).then_inc(ss_sq, 1)
                if n == FIRST_SQUARE + KT + 1:
                    root_of_mean(0, range(4))
                if n == FIRST_SQUARE + KT + 2:
                    keep_inverse(0, range(4))
                if n in runs:
                    first, last = runs[n]
                    for k in range(first, last + 1):
                        h_step(0, k, first, last)
            evac_a(0)

            def body_a(h, a):
                n0 = N_A + NCH * h
                for kt in range(KT):
                    if kt % 2 == 0:
                        split_hi(n0 + kt // 2 + AHEAD, kt // 2 + AHEAD)
                    if kt == KT - 1:
                        evac_a(h)
                    attend_a(a, kt)

            body_a(1, 0)
            with act.Fori(2, A_HEADS) as h:
                body_a(h, h - 1)

            def body_b(b, first=False):
                n0 = N_B + 2 * NCH * b
                for s in range(2 * KT):
                    if s % 2 == 0:
                        c = s // 2 + AHEAD
                        split_hi(n0 + c, c, 768 if c < 2 * NCH else CH)
                    if s == KT - 1:
                        act.wait_ge(proj_done[1], 8 + 2 * b + 1)
                        if first:
                            act.wait_ge(a_s, 8 * A_HEADS)
                        else:
                            act.wait_ge(b_s, 3 * b)
                        f(qk[:, 1, :], pj[:, 1, :], ACT.Copy, scale=B_DIM ** -0.5).then_inc(bank_free[1], 1)
                    if s == 2 * KT - 1:
                        act.wait_ge(proj_done[1], 8 + 2 * b + 2)
                        f(stream[:, bass.ds(2 * b + 8, 1), :], pj[:, 1:2, :], ACT.Copy).then_inc(bank_free[1], 1)
                        act.wait_ge(w_used, n0 + 2 * NCH)
                        f(stream[:, bass.ds(2 * b + 9, 1), :], pj[:, 2:3, :], ACT.Copy).then_inc(bank_free[2], 1)
                    if not first:
                        retain_b(b - 1, s)
                    elif s < KT:
                        attend_a(A_HEADS - 1, s)

            body_b(0, True)
            body_b(1)
            with act.Fori(2, B_HEADS) as b:
                body_b(b)

            def squares(layer, fb, added, n):
                for t in range(4):
                    if layer == 0:
                        act.wait_ge(x1_lat, 4 * (4 + fb) + t + 1)
                    act.wait_ge(bank_free[t], (evacs_o0, evacs_o1)[layer](4 + fb, t) + 1)
                    act.wait_ge(ss_add, added + t - 1)
                    f(tmp_r[:, t % 2, 0:n], stream[:, 4 * fb + t, 0:n], ACT.Square).then_inc(ss_sq, 1)

            def last_squares(half):
                act.wait_ge(ss_add, 2 * KT - 4)
                cols = (slice(0, SEQ), slice(SEQ, T))[half]
                for t in range(4):
                    if half == 0:
                        act.wait_ge(x1_lat, 28 + t + 1)
                    else:
                        act.wait_ge(bank_free[t], evacs_o0(7, t) + 1)
                    f(normed[t][:, cols], stream[:, KT - 4 + t, cols], ACT.Square).then_inc(ss_sq, 1)

            def o_hi(i, k, n_last):
                act.wait_ge(w_used, n_last + k // 2 + 1)
                if i == 1:
                    act.wait_ge(*((a_out, k + 1) if k < A_HEADS else (b_out, k - A_HEADS + 1)))
                    act_split(k, stream[:, k, :])
                else:
                    act.wait_ge(c_out, k + 1)
                    act_split(k, stream[:, k, SEQ:T])

            for k in range(4):
                o_hi(1, k, N_O0 - NCH)
            for i, fb, kts, n0 in out_blocks():
                for kt in kts:
                    if kt % 2 == 0:
                        c = n0 + (kt - kts[0]) // 2 + AHEAD
                        split_hi(N_O0 + c, c)
                    if i == 0 and kt + 4 < EARLY:
                        o_hi(1, kt + 4, N_O0 - NCH)
                    if i == 3 and kt >= EARLY - 4:
                        o_hi(1, kt + 4, N_O0 - NCH)
                    if i < 4:
                        retain_b(B_HEADS - 1, EARLY * i + kt)
                if 4 <= i < 7:
                    squares(0, fb, KT + 4 * fb, T)
            last_squares(0)
            root_of_mean(1, LAT)
            keep_inverse(1, LAT)
            for k in range(4):
                h_latents_hi(k)
            last_squares(1)

            def body_c(j, first=False):
                n0 = N_C + 3 * NCH * j
                for s in range(3 * KT):
                    if first and s + 4 < KT:
                        h_latents_hi(s + 4)
                    if first and s == CTX_SUMS:
                        root_of_mean(2, CONTEXT)
                    if first and s == CTX_SPREAD:
                        keep_inverse(2, CONTEXT)
                    if s % 2 == 0:
                        c = s // 2 + AHEAD
                        split_hi(n0 + c, c, CH // 2 if 2 * NCH <= c < 3 * NCH else CH)
                    if s == KT - 1:
                        if first:
                            act.wait_ge(h_norm, normed_context(1, 3))
                        for t in (1, 3):
                            if t < 3:
                                act.wait_ge(proj_done[t], done_c(j, 0, t) + 1)
                            else:
                                act.wait_ge(w_used, n0 + NCH)
                            f(stream[:, bass.ds(4 * j + t, 1), SEQ:T], pj[:, t:t + 1, 0:SEQ], ACT.Copy) \
                                .then_inc(bank_free[t], 1)
                    if first and s in CTX_TILE:
                        h_step(1, CTX_TILE[s], 0, KT - 1)
                    if s == KT + 4:
                        for t in range(4):
                            act.wait_ge(bank_free[t], evacs_c(j, 0, t) + 1)
                        gates = stream[:, bass.ds(4 * j, 4), SEQ:T]
                        f(gates, gates, ACT.Silu).then_inc(c_gate, 1)
                    if s == 2 * KT - 1:
                        for t in (1, 3):
                            if t < 3:
                                act.wait_ge(proj_done[t], done_c(j, 1, t) + 1)
                            else:
                                act.wait_ge(w_used, n0 + 2 * NCH)
                            past(act, c_o, 4 * j)
                            f(qk[:, t // 2, SEQ * (t % 2):SEQ * (t % 2) + SEQ], pj[:, t, 0:SEQ], ACT.Copy) \
                                .then_inc(bank_free[t], 1)
                    if s == 3 * KT - 1:
                        act.wait_ge(w_used, n0 + 3 * NCH)
                        past(act, c_vt, j)
                        f(kv[:, 1, :], pj[:, 1, :], ACT.Copy).then_inc(bank_free[1], 1)
                    if not first:
                        attend_c(j - 1, s)
                    norm_q_c(j, s)

            body_c(0, True)
            body_c(1)
            with act.Fori(2, C_KV) as j:
                body_c(j)

            for k in range(4):
                o_hi(4, k, N_O1 - NCH)
            for i, fb, kts, n0 in out_blocks():
                for kt in kts:
                    if kt % 2 == 0 and n0 + (kt - kts[0]) // 2 + AHEAD < 4 * NCH:
                        c = n0 + (kt - kts[0]) // 2 + AHEAD
                        split_hi(N_O1 + c, c)
                    if i == 0 and kt + 4 < EARLY:
                        o_hi(4, kt + 4, N_O1 - NCH)
                    if i == 3 and kt >= EARLY - 4:
                        o_hi(4, kt + 4, N_O1 - NCH)
                    if i < 4:
                        attend_c(C_KV - 1, EARLY * i + kt)
                if i >= 4:
                    squares(1, fb, ADDED_CTX + 4 * fb, SEQ)
            root_of_mean(3, LAT)

        @block.gpsimd
        def _(pool):
            pool.wait_ge(zeroed, 1)
            for k in range(KT):
                pool.wait_ge(ss_sq, k + 1)
                past(pool, ss_add, k)
                pool.tensor_tensor(prob[:, 1, :], prob[:, 1, :], normed[k % depth], ALU.add).then_inc(ss_add, 1)
            pool.wait_ge(ss_inv, 1)
            for k in range(KT):
                past(pool, h_lat, k - depth + 1)
                past(pool, h_ctx, k - depth + 1)
                pool.tensor_tensor(normed[k % depth], stream[:, k, :], prob[:, 2, :], ALU.mult).then_inc(h_norm, 1)
            pool.wait_ge(ss_inv, 2)
            for k in range(KT):
                if k >= depth:
                    pool.wait_ge(h_lat, KT + k - depth + 1)
                pool.tensor_tensor(normed[k % depth][:, 0:SEQ], stream[:, k, 0:SEQ], prob[:, 2, 0:SEQ], ALU.mult) \
                    .then_inc(h_norm, 1)
            pool.wait_ge(ss_inv, 3)
            pool.wait_ge(h_lat, 2 * KT)
            for k in range(KT):
                if k >= depth:
                    pool.wait_ge(h_ctx, KT + k - depth + 1)
                pool.tensor_tensor(normed_ctx[1][k % depth], stream[:, k, SEQ:T], prob[:, 2, SEQ:T], ALU.mult) \
                    .then_inc(h_norm, 1)

        @block.vector
        def _(ve):
            def tt(out_, a, b, op):
                return ve.tensor_tensor(out_, a, b, op)

            ve.memset(st(R_EPS), EPS)
            ve.memset(prob[:, 1, :], 0.0).then_inc(zeroed, 1)
            ve.memset(s_parts[:, :].bitcast(F32), 0.0).then_inc(zeroed, 1)
            ve.wait_ge(consts_loaded, 32)
            tt(st(R_PROD, 1), sm(S_DL), sm(S_DL + 1), ALU.mult)
            tt(st(R_PROD + 1, 1), sm(S_DL + 2), sm(S_DL + 3), ALU.mult).then_inc(setup_v, 1)
            ve.tensor_scalar(st(R_SUB), sm(S_SUBLN), 1.0 - LAMBDA_INIT, None, ALU.mult).then_inc(setup_v, 1)
            ve.wait_ge(zeroed, 1)

            def add_square(count, k, n):
                ve.wait_ge(ss_sq, count)
                past(ve, ss_add, count - 1)
                tt(prob[:, 1, 0:n], prob[:, 1, 0:n], tmp_r[:, k % 2, 0:n], ALU.add).then_inc(ss_add, 1)

            def mod0_out(g):
                col = (M_SCALE0, M_SHIFT0)[g % 2] + 4 * (g // 2)
                ve.wait_ge(row_spread, g + 1)
                for v in range(2):
                    last = tt(modv[:, v, col:col + 4], ov[:, 0:8].rearrange("p (f v) -> p v f", v=2)[:, v, :],
                              small[:, S_B + col:S_B + col + 4], ALU.add)
                last.then_inc(mod0_read, 1)
                if g % 2 == 1:
                    col = M_SCALE0 + 4 * (g // 2)
                    ve.wait_ge(mod0_read, g + 1)
                    for v in range(2):
                        ve.scalar_tensor_tensor(modv[:, v, col:col + 4], modv[:, v, col:col + 4], 1.0,
                                                sm(S_G + 4 * (g // 2), 4), ALU.add, ALU.mult) \
                            .then_inc(scale_ready, 1)

            def copy_rows(g):
                ve.wait_ge(w_used, mod_end[g])
                past(ve, row_spread, g - 1)
                ve.tensor_copy(m_acc[0:4, g % 2, :], (tr, sa)[g % 2][0:4, :]).then_inc(row_copied, 1)

            def finish_scale(layer):
                c0 = M_SCALE1
                for v in range(2):
                    ve.scalar_tensor_tensor(modv[:, v, c0:c0 + 16], modv[:, v, c0:c0 + 16], 1.0,
                                            sm(S_G + 16 * layer, 16), ALU.add, ALU.mult).then_inc(scale_ready, 1)
                ve.wait_ge(scale_ready, 2 * PAIRS + 2)

            def split_lo(n, c, width=CH):
                ve.wait_ge(w_hi_done, n + 1)
                s = c % WSLOTS
                tt(w_lo[:, s, 0:width], w_raw[:, s, 0:width], w_hi[:, s, 0:width].bitcast(F32), ALU.subtract) \
                    .then_inc(w_lo_done, 1)

            def h_tile(layer, k):
                c_scale, c_shift = ((M_SCALE0, M_SHIFT0), (M_SCALE1, M_SHIFT1))[layer]
                past(ve, act_hi_done, 2 * KT * layer + k - depth + 1)
                past(ve, act_lo_done, 2 * KT * layer + k - depth + 1)
                ve.wait_ge(h_norm, KT * layer + k + 1)
                if layer == 0:
                    ve.wait_ge(scale_ready, 2 * (k // 4 + 1))
                ve.tensor_scalar(modulated[k % depth][:, 0:SEQ], normed[k % depth][:, 0:SEQ],
                                 modv[:, 0, c_scale + k:c_scale + k + 1], modv[:, 0, c_shift + k:c_shift + k + 1],
                                 ALU.mult, ALU.add).then_inc(h_lat, 1)

            def h_lo(k, cols, whole, splits):
                ve.wait_ge(act_hi_done, splits + 1)
                tt(act_lo[:, k, cols], whole, act_hi[:, k, cols].bitcast(F32), ALU.subtract) \
                    .then_inc(act_lo_done, 1)

            def mod_chunk(it, c, vectors=2):
                ve.wait_ge(m_loaded[c % MSLOTS], (2 * NCH // 4) * 16 * it + 16 * (c // MSLOTS + 1))
                if c == 0:
                    past(ve, m_sum, it)
                for k2 in range(2):
                    for v in range(vectors):
                        k = 2 * c + k2
                        src = m_raw[:, c % MSLOTS, 512 * k2:512 * k2 + 512]
                        coef, acc = st(R_S + 2 * k + v), m_acc[:, v, :]
                        if k == 0:
                            ins = ve.tensor_scalar(acc, src, coef, None, ALU.mult)
                        else:
                            ve.wait_ge((m_lat, m_ctx)[v], 2 * NCH * it + k)
                            ins = ve.scalar_tensor_tensor(acc, src, coef, acc, ALU.mult, ALU.add)
                        ins.then_inc((m_lat, m_ctx)[v], 1)

            def mod_out(it, vectors=2):
                ve.wait_ge(m_sum, it + 1)
                for v in range(vectors):
                    last = ve.tensor_tensor(modv[:, v, bass.ds(4 * it + 4 * MOD0_GROUPS, 4)], sa[:, 4 * v:4 * v + 4],
                                            small[:, bass.ds(4 * it + 4 * MOD0_GROUPS + S_B, 4)], ALU.add)
                last.then_inc(m_out, 1)

            def lat(ap):
                return ap[:, :, 0:SEQ]

            def rows(ap, n):
                return ap.unsqueeze(1).to_broadcast([P, n, SEQ])

            def h_step(layer, k, first, last):
                if k == first:
                    h_tile(layer, k)
                if k < last:
                    h_tile(layer, k + 1)
                if layer == 0:
                    ve.wait_ge(h_ctx, k + 1)
                    h_lo(k, slice(0, T), modulated[k % depth], k)
                else:
                    h_lo(k, slice(0, SEQ), modulated[k % depth][:, 0:SEQ], 2 * KT + k)

            def attend_a(a, s):
                if s == 1:
                    for i in range(2):
                        ve.wait_ge(a_hi, 2 * a + i + 1)
                        tt(op_lo[:, i, :], qk[:, i, :], op_hi[:, i, :].bitcast(F32), ALU.subtract) \
                            .then_inc(a_lo, 1)
                    if not (isinstance(a, int) and a == 0):
                        mod_out(a - 1)
                if s == 0:
                    ve.wait_ge(a_rot, a + 1)
                    past(ve, a_out, a)
                    rotated = tr[:, :].rearrange("p (i t) -> p i t", i=2)
                    held = tmp_o[:, 0, :].rearrange("p (i t) -> p i t", i=2)
                    tt(held, rotated, rows(trig[:, 1, :], 2), ALU.mult).then_inc(a_tmp, 1)
                    tt(lat(qk), lat(qk), rows(trig[:, 0, :], 2), ALU.mult).then_inc(a_cos, 1)
                    ve.wait_ge(a_tmp, a + 1)
                    ve.wait_ge(a_cos, a + 1)
                    tt(lat(qk), lat(qk), held, ALU.add).then_inc(a_rope, 1)
                if s in (4, 6, 8, 10):
                    combine_a(a, (s - 4) // 2)
                if s in (2, 4, 6, 8):
                    q = (s - 2) // 2
                    nk = T if q < 2 else CTX
                    for m, bank in enumerate((sa, sc)):
                        ve.wait_ge(a_s, 8 * a + 2 * q + m + 1)
                        ve.tensor_reduce(st(R_NEG + m), bank[:, 0:nk], AX_X, ALU.max, negate=True).then_inc(a_max, 1)
                if s == 14:
                    ve.wait_ge(a_root, a + 1)
                    ve.reciprocal(st(R_RMS, 4), st(R_RMS, 4)).then_inc(a_inv, 1)
                if s == 15:
                    ve.wait_ge(a_spread, a + 1)
                    tile = stream[:, bass.ds(a, 1), :]
                    tt(tile, tile, tr[:, :].unsqueeze(1), ALU.mult).then_inc(a_y, 1)
                    ve.wait_ge(a_y, a + 1)
                    ve.scalar_tensor_tensor(tile, ov[:, :].unsqueeze(1), st(R_SUB), tile, ALU.mult, ALU.mult) \
                        .then_inc(a_out, 1)

            def combine_a(a, q):
                nk = T if q < 2 else CTX
                n = 4 * a + q
                ve.wait_ge(a_exp, 8 * a + 2 * q + 2)
                ve.reciprocal(st(R_REC, 2), st(R_SUM, 2)).then_inc(a_rec, 1)
                ve.wait_ge(a_rec, n + 1)
                tt(st(R_C2), st(R_REC + 1), st(R_LAM), ALU.mult).then_inc(a_c2, 1)
                ve.wait_ge(a_c2, n + 1)
                ve.tensor_scalar(prob[:, 1, 0:nk], prob[:, 1, 0:nk], st(R_C2), None, ALU.mult).then_inc(a_p2, 1)
                ve.wait_ge(a_p2, n + 1)
                past(ve, a_t, n)
                ve.scalar_tensor_tensor(prob[:, 2, 0:nk], prob[:, 0, 0:nk], st(R_REC), prob[:, 1, 0:nk], ALU.mult,
                                        ALU.subtract).then_inc(a_p, 1)

            def retain_b(b, s):
                if s == 0:
                    past(ve, b_y, 2 * b)
                    ve.tensor_scalar(tmp_r[:, 0, :], aux[:, 1, :], stat[:, bass.ds(R_LG + 4 + b, 1)], None, ALU.mult) \
                        .then_inc(b_argb, 1)
                    ve.wait_ge(b_argb, b + 1)
                    ve.scalar_tensor_tensor(tmp_r[:, 0, :], aux[:, 0, :], stat[:, bass.ds(R_LG + b, 1)],
                                            tmp_r[:, 0, :], ALU.mult, ALU.add).then_inc(b_arg, 1)
                    mod_out(7 + b)
                    ve.wait_ge(b_expc, 2 * b + 2)
                    tt(prob[:, 1, :], prob[:, 1, :], tmp_r[:, 1, :], ALU.add).then_inc(b_dc, 1)
                    ve.wait_ge(b_expi, b + 1)
                    tt(prob[:, 0, :], prob[:, 0, :], aux[:, 2, :], ALU.add).then_inc(b_di, 1)
                if s in (3, 4, 7):
                    i = (3, 4, 7).index(s)
                    ve.wait_ge(b_s, 3 * b + i + 1)
                    if i == 0:
                        ve.wait_ge(b_di, b + 1)
                        ve.wait_ge(b_dc, b + 1)
                        if isinstance(b, int) and b == 0:
                            ve.wait_ge(a_o, 2 * A_HEADS)
                        past(ve, b_o, 2 * b)
                    dst = pt[:, i // 2, 2 * (i % 2):2 * (i % 2) + 2, :]
                    tt(dst, (sa, sc, sa)[i][:, :].rearrange("p (i t) -> p i t", i=2),
                       prob[:, (0, 1, 0)[i], :].rearrange("p (i t) -> p i t", i=2), ALU.mult).then_inc(b_pt, 1)
                if s == 12:
                    ve.wait_ge(b_mean, b + 1)
                    for e in range(2):
                        ve.scalar_tensor_tensor(tmp_o[:, e, :], sa[:, :], -1.0 / (2 * B_DIM), tmp_o[:, e, :],
                                                ALU.mult, ALU.add).then_inc(b_xc, 1)
                if s == 17:
                    ve.wait_ge(b_root, b + 1)
                    ve.reciprocal(st(R_RMS, 4), st(R_RMS, 4)).then_inc(b_inv, 1)
                if s == 18:
                    ve.wait_ge(b_gate, b + 1)
                    ve.wait_ge(b_spread, b + 1)
                    for e in range(2):
                        ve.scalar_tensor_tensor(tmp_r[:, e, :], tmp_o[:, e, :], small[:, bass.ds(S_GN + 2 * b + e, 1)],
                                                sc[:, :], ALU.mult, ALU.mult).then_inc(b_y, 1)
                    for e in range(2):
                        ve.wait_ge(b_y, 2 * b + e + 1)
                        tile = stream[:, bass.ds(2 * b + 8 + e, 1), :]
                        tt(tile, tile, tmp_r[:, e:e + 1, :], ALU.mult).then_inc(b_out, 1)

            def norm_q_c(j, s):
                if s == 36:
                    ve.wait_ge(cq_root, j + 1)
                    ve.reciprocal(st(R_RMS, 8), st(R_RMS, 8)).then_inc(cq_inv, 1)
                if s == 38:
                    ve.wait_ge(cq_spread, j + 1)
                    for i, bank in enumerate((sa, sc)):
                        ve.scalar_tensor_tensor(qk[:, i, :], qk[:, i, :], sm(S_QK), bank[:, :], ALU.mult, ALU.mult) \
                            .then_inc(cq_n, 1)
                if s == 41:
                    for i, bank in enumerate((sa, sc)):
                        ve.wait_ge(cq_rot, 2 * j + i + 1)
                        tt(tmp_o[:, i, :].rearrange("p (g t) -> p g t", g=2),
                           bank[:, :].rearrange("p (g t) -> p g t", g=2), rows(trig[:, 1, :], 2), ALU.mult) \
                            .then_inc(cq_sin, 1)
                    heads = qk[:, :, :].rearrange("p i (g t) -> p (i g) t", g=2)
                    tt(heads, heads, rows(trig[:, 0, :], 4), ALU.mult).then_inc(cq_cos, 1)
                    ve.wait_ge(cq_cos, j + 1)
                    ve.wait_ge(cq_sin, 2 * j + 2)
                    tt(qk[:, :, :], qk[:, :, :], tmp_o[:, :, :], ALU.add).then_inc(cq_rope, 1)

            def attend_c(j, s):
                if s == 0:
                    mod_out(12 + j, 1)
                if s == 2:
                    ve.wait_ge(ck_root, j + 1)
                    ve.reciprocal(st(R_RMS, 4), st(R_RMS, 4)).then_inc(ck_inv, 1)
                if s == 3:
                    ve.wait_ge(ck_spread, j + 1)
                    ve.scalar_tensor_tensor(kv[:, 0, :], kv[:, 0, :], sm(S_QK + 1), sa[:, :], ALU.mult,
                                            ALU.mult).then_inc(ck_n, 1)
                if s == 4:
                    ve.wait_ge(cq_hi, j + 1)
                    tt(op_lo[:, :, :], qk[:, :, :], op_hi[:, :, :].bitcast(F32), ALU.subtract).then_inc(cq_lo, 1)
                if s == 6:
                    ve.wait_ge(ck_hi, j + 1)
                    tt(k_lo[:, :], kv[:, 0, :], k_hi[:, :].bitcast(F32), ALU.subtract).then_inc(ck_lo, 1)
                if s == 5:
                    ve.wait_ge(ck_rot, j + 1)
                    ve.wait_ge(ck_ss, j + 1)
                    tt(tmp_o[:, 0, 0:SEQ], sc[:, 0:SEQ], trig[:, 1, :], ALU.mult).then_inc(ck_sin, 1)
                    tt(kv[:, 0, 0:SEQ], kv[:, 0, 0:SEQ], trig[:, 0, :], ALU.mult).then_inc(ck_cos, 1)
                    ve.wait_ge(ck_sin, j + 1)
                    ve.wait_ge(ck_cos, j + 1)
                    tt(kv[:, 0, 0:SEQ], kv[:, 0, 0:SEQ], tmp_o[:, 0, 0:SEQ], ALU.add).then_inc(ck_rope, 1)
                if s >= 9 and (s - 9) % 2 == 0 and (s - 9) // 2 < 8:
                    u = (s - 9) // 2
                    ve.wait_ge(c_exp, 8 * j + u + 1)
                    ve.reciprocal(st(R_REC + u % 2), st(R_SUM + u % 2)).then_inc(c_rec, 1)
                    ve.wait_ge(c_rec, 8 * j + u + 1)
                    ve.tensor_scalar(prob[:, u % 2, :], prob[:, u % 2, :], st(R_REC + u % 2), None, ALU.mult) \
                        .then_inc(c_p, 1)
                if s >= 8 and s % 2 == 0 and (s - 8) // 2 < 8:
                    u = (s - 8) // 2
                    ve.wait_ge(c_s, 8 * j + u + 1)
                    ve.tensor_reduce(st(R_NEG + u % 2), (sa, sc)[u % 2][:, :], AX_X, ALU.max, negate=True) \
                        .then_inc(c_max, 1)
                if s == 7:
                    ve.wait_ge(c_vtok, j + 1)
                    tt(v_parts[:, :, P:2 * P], ov[:, :].rearrange("p (i d) -> p i d", i=4),
                       v_parts[:, :, 0:P].bitcast(F32), ALU.subtract).then_inc(c_vlo, 1)
                if s >= 11 and (s - 11) % 2 == 0 and (s - 11) // 2 < 8:
                    u = (s - 11) // 2
                    g, q = u // 2, u % 2
                    ve.wait_ge(c_pt, 8 * j + u + 1)
                    past(ve, c_o, 4 * j + max(g - 1, 0))
                    queries = slice(P * q, P * q + P)
                    tt(pt_lo[g % 2][:, :, queries], tr[:, :].rearrange("p (i d) -> p i d", i=4),
                       pt_hi[:, g % 2, :, queries].bitcast(F32), ALU.subtract).then_inc(c_ptlo, 1)
                if s >= 15 and (s - 15) % 4 == 0 and (s - 15) // 4 < 4:
                    g = (s - 15) // 4
                    ve.wait_ge(c_o, 4 * j + g + 1)
                    if g == 0:
                        ve.wait_ge(c_gate, j + 1)
                    tile = stream[:, bass.ds(4 * j + g, 1), SEQ:T]
                    tt(tile, tile, ov[:, 0:SEQ].unsqueeze(1), ALU.mult).then_inc(c_out, 1)

            def evac_a(h):
                ve.wait_ge(proj_done[0], h + 1)
                past(ve, a_s, 8 * h)
                ve.tensor_scalar(qk[:, 0, :], pj[:, 0, :], A_DIM ** -0.5, None, ALU.mult).then_inc(bank_free[0], 1)
                ve.wait_ge(proj_done[2], h + 1)
                past(ve, a_vt, h)
                ve.tensor_copy(kv[:, 0, :], pj[:, 2, :]).then_inc(bank_free[2], 1)

            ve.wait_ge(s_ready, 1)
            tt(vector_parts[:, :, 2:4], st(R_S, 32).rearrange("p (k v) -> p k v", v=2),
               vector_parts[:, :, 0:2].bitcast(F32), ALU.subtract).then_inc(s_ready, 1)
            for n in range(AHEAD):
                split_lo(n, n)
            for n, (kind, what, c) in enumerate(prologue()):
                for g in range(MOD0_GROUPS):
                    if n == mod_end[g]:
                        copy_rows(g)
                split_lo(n + AHEAD, n + AHEAD)
                for g in range(MOD0_GROUPS):
                    if n == turn_at[g] + 1:
                        mod0_out(g)
                if kind == "mod" and what == 2 and c == 0:
                    ve.wait_ge(setup_a, 2)
                    ve.scalar_tensor_tensor(st(R_LAM), st(R_EXP2), LAMBDA_INIT, st(R_EXP2 + 1), ALU.add,
                                            ALU.subtract)
                    ve.tensor_scalar(st(R_LG, 8), st(R_LG, 8), -1.0, None, ALU.mult).then_inc(setup_v, 1)
                if n == FIRST_SQUARE + KT + 1:
                    ve.wait_ge(ss_root, 1)
                    ve.reciprocal(st(R_RMS, 4), st(R_RMS, 4)).then_inc(ss_rec, 1)
                if n in runs:
                    first, last = runs[n]
                    for k in range(first, last + 1):
                        h_step(0, k, first, last)
            evac_a(0)

            def body_a(h, a):
                n0 = N_A + NCH * h
                for kt in range(KT):
                    if kt % 2 == 0:
                        split_lo(n0 + kt // 2 + AHEAD, kt // 2 + AHEAD)
                    if kt == KT - 1:
                        evac_a(h)
                    attend_a(a, kt)
                    if kt % 2 == 1:
                        mod_chunk(h - 1, kt // 2)

            ve.wait_ge(trig_loaded, 16)
            body_a(1, 0)
            with ve.Fori(2, A_HEADS) as h:
                body_a(h, h - 1)

            def body_b(b, first=False):
                n0 = N_B + 2 * NCH * b
                for s in range(2 * KT):
                    if s % 2 == 0:
                        c = s // 2 + AHEAD
                        split_lo(n0 + c, c, 768 if c < 2 * NCH else CH)
                    if s == KT - 1:
                        ve.wait_ge(proj_done[0], 8 + 2 * b + 1)
                        if first:
                            ve.wait_ge(a_s, 8 * A_HEADS)
                            ve.wait_ge(a_vt, A_HEADS)
                        else:
                            ve.wait_ge(b_s, 3 * b)
                            ve.wait_ge(b_vt, 2 * b)
                        ve.tensor_copy(qk[:, 0, :], pj[:, 0, :]).then_inc(bank_free[0], 1)
                        ve.wait_ge(w_used, n0 + NCH)
                        ve.tensor_copy(kv[:, 0, :], pj[:, 2, :]).then_inc(bank_free[2], 1)
                    if s == 2 * KT - 1:
                        ve.wait_ge(proj_done[0], 8 + 2 * b + 2)
                        ve.tensor_copy(kv[:, 1, :], pj[:, 0, :]).then_inc(bank_free[0], 1)
                    if not first:
                        retain_b(b - 1, s)
                    elif s < KT:
                        attend_a(A_HEADS - 1, s)
                    if s % 4 == 1:
                        mod_chunk(7 + b, s // 4)

            body_b(0, True)
            ve.wait_ge(dist_loaded, 16)
            body_b(1)
            with ve.Fori(2, B_HEADS) as b:
                body_b(b)

            def last_residual(half):
                cols = (slice(0, SEQ), slice(SEQ, T))[half]
                for t in range(4):
                    if t < 3:
                        ve.wait_ge(proj_done[t], done_out(0, 7, t) + 1)
                    else:
                        ve.wait_ge(w_used, N_O0 + block_end[7])
                    tile, col = stream[:, KT - 4 + t, cols], M_GATE0 + KT - 4 + t
                    ve.scalar_tensor_tensor(tile, pj[:, t, cols], modv[:, half, col:col + 1], tile, ALU.mult,
                                            ALU.add).then_inc(bank_free[t] if half else x1_lat, 1)

            def last_sums(half):
                cols = (slice(0, SEQ), slice(SEQ, T))[half]
                for t in range(4):
                    count = 2 * KT - 4 + 4 * half + t
                    ve.wait_ge(ss_sq, count + 1)
                    ve.wait_ge(ss_add, count)
                    tt(prob[:, 1, cols], prob[:, 1, cols], normed[t][:, cols], ALU.add).then_inc(ss_add, 1)

            def residual(layer, i, fb, n):
                for t in range(4):
                    if t < 3:
                        ve.wait_ge(proj_done[t], done_out(layer, i, t) + 1)
                    else:
                        ve.wait_ge(w_used, (N_O0, N_O1)[layer] + block_end[i])
                    for v in range(n // 256):
                        cols = slice(256 * v, 256 * v + 256)
                        tile = stream[:, 4 * fb + t, cols]
                        old = aux[:, t, cols] if layer == 0 and i < 4 else tile
                        col = (M_GATE0, M_GATE1)[layer] + 4 * fb + t
                        ve.scalar_tensor_tensor(tile, pj[:, t, cols], modv[:, v, col:col + 1], old, ALU.mult,
                                                ALU.add).then_inc(x1_lat if v < n // 256 - 1 else bank_free[t], 1)
                if i >= 4:
                    for t in range(4):
                        add_square((KT, ADDED_CTX)[layer] + 4 * fb + t + 1, t, n)

            block_end = {i: n0 + len(kts) // 2 for i, fb, kts, n0 in out_blocks()}

            def o_lo(i, k):
                n = KT * i + k
                ve.wait_ge(act_hi_done, n + 1)
                cols = slice(0, T) if i == 1 else slice(SEQ, T)
                width = T if i == 1 else SEQ
                tt(act_lo[:, k, 0:width], stream[:, k, cols], act_hi[:, k, 0:width].bitcast(F32), ALU.subtract) \
                    .then_inc(act_lo_done, 1)

            for k in range(4):
                o_lo(1, k)
            for i, fb, kts, n0 in out_blocks():
                for kt in kts:
                    if kt % 2 == 0:
                        c = n0 + (kt - kts[0]) // 2
                        split_lo(N_O0 + c + AHEAD, c + AHEAD)
                    if i == 0 and kt + 4 < EARLY:
                        o_lo(1, kt + 4)
                    if i == 3 and kt >= EARLY - 4:
                        o_lo(1, kt + 4)
                    if i < 4:
                        retain_b(B_HEADS - 1, EARLY * i + kt)
                        if kt % 2 == 1 and c < 2 * NCH and c % 2 == 0:
                            mod_chunk(11, c // 2)
                if i < 4:
                    ve.wait_ge(xr_loaded, 16 * (fb + 1))
                if i == 3:
                    ve.wait_ge(b_dc, B_HEADS)
                    ve.memset(prob[:, 1, :], 0.0).then_inc(zeroed, 1)
                    ve.wait_ge(zeroed, 3)
                    mod_out(11)
                    ve.wait_ge(m_out, 12)
                    finish_scale(1)
                if i < 7:
                    residual(0, i, fb, T)
            last_residual(0)
            last_sums(0)
            ve.wait_ge(ss_root, 2)
            ve.reciprocal(st(R_RMS, 2), st(R_RMS, 2)).then_inc(ss_rec, 1)
            last_residual(1)
            for k in range(4):
                h_step(1, k, 0, KT - 1)
            last_sums(1)

            def body_c(j, first=False):
                n0 = N_C + 3 * NCH * j
                for s in range(3 * KT):
                    if first and s + 4 < KT:
                        h_step(1, s + 4, 0, KT - 1)
                    if first and s == CTX_SUMS:
                        ve.wait_ge(ss_root, 3)
                        ve.reciprocal(st(R_RMS + CONTEXT[0], 2), st(R_RMS + CONTEXT[0], 2)).then_inc(ss_rec, 1)
                    if s == KT - 1:
                        if first:
                            ve.wait_ge(h_norm, normed_context(1, 3))
                        for t in (0, 2):
                            ve.wait_ge(proj_done[t], done_c(j, 0, t) + 1)
                            ve.tensor_copy(stream[:, bass.ds(4 * j + t, 1), SEQ:T], pj[:, t:t + 1, 0:SEQ]) \
                                .then_inc(bank_free[t], 1)
                    if first and s in CTX_TILE:
                        k = CTX_TILE[s]
                        h_lo(k, slice(SEQ, T), modulated_ctx[1][k % depth], 3 * KT + k)
                    if s == 2 * KT - 1:
                        for t in (0, 2):
                            ve.wait_ge(proj_done[t], done_c(j, 1, t) + 1)
                            past(ve, c_o, 4 * j)
                            ve.tensor_copy(qk[:, t // 2, 0:SEQ], pj[:, t, 0:SEQ]).then_inc(bank_free[t], 1)
                    if s == 3 * KT - 1:
                        ve.wait_ge(proj_done[0], done_c(j, 2, 0) + 1)
                        ve.tensor_copy(kv[:, 0, :], pj[:, 0, :]).then_inc(bank_free[0], 1)
                    if not first:
                        attend_c(j - 1, s)
                    norm_q_c(j, s)
                    if s % 2 == 0:
                        c = s // 2 + AHEAD
                        split_lo(n0 + c, c, CH // 2 if 2 * NCH <= c < 3 * NCH else CH)
                    if s in MOD_SLOTS[first]:
                        mod_chunk(12 + j, MOD_SLOTS[first].index(s), 1)

            ve.tensor_scalar(sm(S_QK), sm(S_QK), C_DIM ** -0.5, None, ALU.mult).then_inc(setup_v, 1)
            ve.wait_ge(setup_v, 4)
            ve.wait_ge(trig_loaded, 32)
            body_c(0, True)
            body_c(1)
            with ve.Fori(2, C_KV) as j:
                body_c(j)

            for k in range(4):
                o_lo(4, k)
            for i, fb, kts, n0 in out_blocks():
                for kt in kts:
                    c = n0 + (kt - kts[0]) // 2 + AHEAD
                    if i == 0 and kt + 4 < EARLY:
                        o_lo(4, kt + 4)
                    if i == 3 and kt >= EARLY - 4:
                        o_lo(4, kt + 4)
                    if i < 4:
                        attend_c(C_KV - 1, EARLY * i + kt)
                    if kt % 2 == 0 and c < 4 * NCH:
                        split_lo(N_O1 + c, c)
                if i == 3:
                    ve.wait_ge(c_t, 8 * C_KV)
                    ve.memset(prob[:, 1, :], 0.0).then_inc(zeroed, 1)
                    ve.wait_ge(zeroed, 4)
                residual(1, i, fb, SEQ)
            ve.wait_ge(ss_root, 4)
            ve.reciprocal(st(R_RMS, 2), st(R_RMS, 2)).then_inc(ss_rec, 1)
            ve.wait_ge(ss_spread, 4)
            for k in range(KT):
                tile = stream[:, k, 0:SEQ]
                ve.scalar_tensor_tensor(tile, tile, sm(S_FN + k), sc[:, 0:SEQ], ALU.mult, ALU.mult) \
                    .then_inc(out_ready, 1)


def _rotation(dim):
    axis, half = dim // 2, dim // 4
    m = np.zeros((P, P), np.float32)
    for f in range(P):
        if f % axis < half:
            m[f + half, f] = -1.0
        else:
            m[f - half, f] = 1.0
    return m


def _angles(dim):
    axis, half = dim // 2, dim // 4
    tok = np.arange(SEQ)
    pos = np.stack([tok // GRID_W, tok % GRID_W]).astype(np.float32)
    inv = (ROPE_THETA ** (-np.arange(0, axis, 2, dtype=np.float32) / np.float32(axis))).astype(np.float32)
    ang = np.zeros((P, SEQ), np.float32)
    for f in range(P):
        ang[f] = pos[(f % dim) // axis] * inv[f % axis % half]
    return np.stack([np.cos(ang), np.sin(ang)], 1).astype(np.float32)


def _distances():
    k = np.arange(256).reshape(2, P).transpose(1, 0)[:, :, None]
    q = np.arange(256)[None, None, :]
    d = [np.maximum(q - k, 0), np.maximum(k - q, 0), (q == k) * 1, 256 + q - k, 256 - q + k]
    return np.stack([v.reshape(P, 512) for v in d], 1).astype(np.float32)


def kernel(**inputs):
    import concourse.bacc as _bacc
    from concourse.bass_utils import run_bass_kernel_spmd as _run

    a = {k: np.asarray(v) for k, v in inputs.items()}

    def chunks(w, blocks):
        cols = [np.concatenate([w[:, s:s + n] for s, n in b], 1) for b in blocks]
        return np.ascontiguousarray(np.concatenate(
            [b.reshape(NCH, 2, P, -1).transpose(0, 2, 1, 3).reshape(NCH, P, -1) for b in cols], 0))

    ev, od = a["ev_w_in"][0], a["od_w_in"][0]
    mod_order = [(0, 1), (0, 0), (0, 2), (1, 1), (1, 0), (1, 2)]
    four = [[(512 * i, 512)] for i in range(4)]
    w_mod = np.concatenate([chunks(a["w_mod"][l][:, 2048 * t:2048 * t + 2048], four) for l, t in mod_order[2:]], 0)
    b_mod = np.concatenate([a["b_mod"][l, 2048 * t:2048 * t + 2048].reshape(16, P) for l, t in mod_order], 0).T
    w_b = []
    for b in range(B_HEADS):
        q, k, v, g = 4096 + 128 * b, 4608 + 128 * b, 5120 + 256 * b, 6144 + 256 * b
        w_b += [[(q, 128), (k, 128), (v, 128)], [(v + 128, 128), (g, 256)]]
    w_c = []
    for j in range(C_KV):
        w_c += [[(3072 + 512 * j, 512)], [(512 * j, 512)], [(2048 + 128 * j, 128), (2560 + 128 * j, 128)]]
    w_all = np.zeros((N_END, P, CH), np.float32)

    def place(n, part):
        w_all[n:n + len(part), :, 0:part.shape[-1]] = part

    heads_a = [[(1024 * i + 128 * h, 128) for i in range(4)] for h in range(A_HEADS)]
    first_head = chunks(ev, heads_a[0:1])
    for n, (kind, what, c) in enumerate(prologue()):
        if kind == "mod":
            third = 1 - what % 2
            cols = 2048 * third + 512 * (what // 2)
            if c == 0:
                place(n, chunks(a["w_mod"][0], [[(cols, 512)]]))
        else:
            place(n, first_head[c:c + 1])
    place(N_A + NCH, chunks(ev, heads_a[1:]))
    for i, block in enumerate(w_b):
        place(N_B + NCH * i, chunks(ev, [block]))
    for i, block in enumerate(w_c):
        place(N_C + NCH * i, chunks(od, [block]))
    for start, w in ((N_O0, a["ev_w_out"][0]), (N_O1, a["od_w_out"][0])):
        for i, fb, kts, n0 in out_blocks():
            place(start + n0, chunks(w, four[fb:fb + 1])[kts[0] // 2:kts[-1] // 2 + 1])
    small = np.zeros((P, S_END), np.float32)
    small[:, S_C:S_C + 32] = np.stack([a["c"][0].reshape(16, P).T, a["c_ctx"].reshape(16, P).T], -1).reshape(P, 32)
    small[:, S_G:S_G + 32] = a["norm_g"].reshape(32, P).T
    small[:, S_B:S_B + 96] = b_mod
    small[:, S_SUBLN] = a["diff_subln"][0]
    small[:, S_DECAY:S_DECAY + 8] = a["ret_decay"][0].reshape(1, 8)
    small[:, S_GN:S_GN + 8] = a["ret_gn"][0].reshape(8, P).T
    small[:, S_QK:S_QK + 2] = a["qk_norm"][0].T
    small[:, S_FN:S_FN + 16] = a["final_norm"].reshape(16, P).T
    small[0:A_DIM, S_DL:S_DL + 4] = a["diff_lambda"][0].T
    small[0:4, S_SEL:S_SEL + 2] = [[1, 0], [0, 1], [1, 0], [0, 1]]
    arrays = {
        "x_t": np.ascontiguousarray(np.concatenate([a["x"][0], a["ctx"][0]], 0).T).reshape(KT, P, T),
        "w_mod": w_mod,
        "w_all": w_all,
        "small_in": small,
        "mats_in": np.stack([_rotation(A_DIM), _rotation(C_DIM), np.ones((P, P), np.float32),
                             np.eye(P, dtype=np.float32)], 1),
        "trig_in": np.stack([_angles(A_DIM), _angles(C_DIM)], 0),
        "dist_in": _distances(),
    }
    arrays = {k: np.ascontiguousarray(v) for k, v in arrays.items()}
    nc = _bacc.Bacc("TRN2", target_bir_lowering=False, num_devices=1)
    args = [nc.dram_tensor(k, v.shape, F32, kind="ExternalInput").ap() for k, v in arrays.items()]
    args.append(nc.dram_tensor("out_t", (KT, P, SEQ), F32, kind="ExternalOutput").ap())
    bass_hybrid_backbone(nc, *args)
    r = _run(nc, [arrays], core_ids=[0])
    got = np.asarray(r.results[0]["out_t"])
    return np.ascontiguousarray(got.reshape(D_MODEL, SEQ).T).reshape(1, SEQ, D_MODEL)
```
